# Optimizing a Trainium2 kernel written in Bass

```python
import math
import jax, jax.numpy as jnp
from jax import lax
import numpy as np

D_MODEL = 2048
BATCH = 1
SEQ = 256
DEPTH = 2

GRID_W = 64

MLA_HEADS = 8
MLA_Q_LORA = D_MODEL // 4
MLA_KV_LORA = D_MODEL // 8
MLA_NOPE = 128
MLA_ROPE = 64
MLA_V = (D_MODEL // 2) // MLA_HEADS
MLA_WIDTH = MLA_HEADS * MLA_V
ROPE_BASE = 10000.0
Q_BLOCK = 128

NAT_HEAD_DIM = 64
NAT_HEADS = (D_MODEL // 2) // NAT_HEAD_DIM
NAT_WIDTH = NAT_HEADS * NAT_HEAD_DIM
NAT_WIN_R = 8
NAT_WIN_C = 16

D_MIX = MLA_WIDTH + NAT_WIDTH

IN_WIDTHS = (MLA_Q_LORA, MLA_KV_LORA, MLA_ROPE, NAT_WIDTH, NAT_WIDTH, NAT_WIDTH)
D_IN = sum(IN_WIDTHS)
IN_OFFSETS = [int(o) for o in np.cumsum(IN_WIDTHS)[:-1]]

PEER_HEADS = 8
PEER_N_KEYS = 128
PEER_N_EXPERTS = PEER_N_KEYS * PEER_N_KEYS
PEER_TOPK = 16
PEER_D_QUERY = 256
PEER_TOKEN_BLOCK = 128

RMS_EPS = 1e-6

kernel_name = "hymba_mla_natten_peer_encoder"

def rms_norm(x, g):
    xf = x.astype(jnp.float32)
    y = xf * lax.rsqrt(jnp.mean(xf * xf, axis=-1, keepdims=True) + RMS_EPS)
    return (y * g.astype(jnp.float32)).astype(x.dtype)

def rope_tables(seq_len):
    inv = ROPE_BASE ** (-jnp.arange(0, MLA_ROPE, 2, dtype=jnp.float32) / MLA_ROPE)
    ang = jnp.arange(seq_len, dtype=jnp.float32)[:, None] * inv[None, :]
    return jnp.cos(ang), jnp.sin(ang)

def apply_rope(t, cos, sin):
    tf = t.astype(jnp.float32)
    half = tf.shape[-1] // 2
    t1, t2 = tf[..., :half], tf[..., half:]
    return jnp.concatenate([t1 * cos - t2 * sin, t2 * cos + t1 * sin], axis=-1).astype(t.dtype)

def mla_group(c_q, c_kv, k_pe, q_norm, w_uq, kv_norm, w_ukv):
    B, S, _ = c_q.shape
    cos, sin = rope_tables(S)
    q = (rms_norm(c_q, q_norm) @ w_uq).reshape(B, S, MLA_HEADS, MLA_NOPE + MLA_ROPE)
    q_nope = q[..., :MLA_NOPE]
    q_pe = apply_rope(q[..., MLA_NOPE:], cos[:, None, :], sin[:, None, :])
    k_pe = apply_rope(k_pe, cos, sin)
    kv = (rms_norm(c_kv, kv_norm) @ w_ukv).reshape(B, S, MLA_HEADS, MLA_NOPE + MLA_V)
    k_nope, v = kv[..., :MLA_NOPE], kv[..., MLA_NOPE:]
    scale = (MLA_NOPE + MLA_ROPE) ** -0.5
    n_blk = S // Q_BLOCK

    def to_blocks(t):
        return jnp.moveaxis(t.reshape(B, n_blk, Q_BLOCK, *t.shape[2:]), 1, 0)

    def attend(blk):
        qn, qp = blk
        s = (jnp.einsum('bqhd,bkhd->bhqk', qn, k_nope, preferred_element_type=jnp.float32)
             + jnp.einsum('bqhd,bkd->bhqk', qp, k_pe, preferred_element_type=jnp.float32))
        p = jax.nn.softmax(s * scale, axis=-1).astype(v.dtype)
        return jnp.einsum('bhqk,bkhd->bqhd', p, v)

    o = lax.map(attend, (to_blocks(q_nope), to_blocks(q_pe)))
    return jnp.moveaxis(o, 0, 1).reshape(B, S, MLA_WIDTH)

def nat_group(q, k, v, rpb):
    B, S, _ = q.shape
    rows = S // GRID_W
    kr = min(NAT_WIN_R, rows)
    n_cb = GRID_W // NAT_WIN_C
    band_w = 2 * NAT_WIN_C

    def grid(t):
        return t.reshape(B, rows, GRID_W, NAT_HEADS, NAT_HEAD_DIM)

    q = grid(q * (NAT_HEAD_DIM ** -0.5))
    k = grid(k)
    v = grid(v)
    cb = np.clip(np.arange(n_cb) * NAT_WIN_C - NAT_WIN_C // 2, 0, GRID_W - band_w)
    key_cols = cb[:, None] + np.arange(band_w)
    q_cols = np.arange(n_cb)[:, None] * NAT_WIN_C + np.arange(NAT_WIN_C)
    c_start = np.clip(q_cols - NAT_WIN_C // 2, 0, GRID_W - NAT_WIN_C)
    kc = key_cols[:, None, :]
    col_mask = (kc >= c_start[..., None]) & (kc < c_start[..., None] + NAT_WIN_C)
    dc_idx = np.clip(kc - q_cols[..., None], -(NAT_WIN_C - 1), NAT_WIN_C - 1) + (NAT_WIN_C - 1)
    mask = jnp.asarray(col_mask)[:, :, None, :]

    def attend_row(r):
        rs = jnp.clip(r - kr // 2, 0, rows - kr)
        q_row = lax.dynamic_index_in_dim(q, r, axis=1, keepdims=False)
        q_row = q_row.reshape(B, n_cb, NAT_WIN_C, NAT_HEADS, NAT_HEAD_DIM)
        k_band = lax.dynamic_slice_in_dim(k, rs, kr, axis=1)[:, :, key_cols]
        v_band = lax.dynamic_slice_in_dim(v, rs, kr, axis=1)[:, :, key_cols]
        dr_idx = rs + jnp.arange(kr) - r + (NAT_WIN_R - 1)
        bias = rpb[:, dr_idx][:, :, dc_idx]
        bias = jnp.transpose(bias, (0, 2, 3, 1, 4)).astype(jnp.float32)
        s = jnp.einsum('bnqhd,binkhd->bhnqik', q_row, k_band,
                       preferred_element_type=jnp.float32) + bias
        s = jnp.where(mask, s, -jnp.inf)
        p = jax.nn.softmax(s.reshape(*s.shape[:4], kr * band_w), axis=-1)
        p = p.reshape(s.shape).astype(v.dtype)
        o = jnp.einsum('bhnqik,binkhd->bnqhd', p, v_band)
        return o.reshape(B, GRID_W, NAT_WIDTH)

    o = lax.map(attend_row, jnp.arange(rows))
    return jnp.moveaxis(o, 0, 1).reshape(B, S, NAT_WIDTH)

def peer_ffn(h, w_q, sub_keys, u, v):
    B, S, D = h.shape
    half = PEER_D_QUERY // 2
    q = (h @ w_q).reshape(B, S, PEER_HEADS, PEER_D_QUERY)
    s1 = jnp.einsum('bshd,nd->bshn', q[..., :half], sub_keys[0], preferred_element_type=jnp.float32)
    s2 = jnp.einsum('bshd,nd->bshn', q[..., half:], sub_keys[1], preferred_element_type=jnp.float32)
    v1, i1 = lax.top_k(s1, PEER_TOPK)
    v2, i2 = lax.top_k(s2, PEER_TOPK)
    cand_s = (v1[..., :, None] + v2[..., None, :]).reshape(B, S, PEER_HEADS, PEER_TOPK * PEER_TOPK)
    cand_i = (i1[..., :, None] * PEER_N_KEYS + i2[..., None, :]).reshape(B, S, PEER_HEADS, PEER_TOPK * PEER_TOPK)
    top_s, pos = lax.top_k(cand_s, PEER_TOPK)
    idx = jnp.take_along_axis(cand_i, pos, axis=-1)
    g = jax.nn.softmax(top_s, axis=-1)
    T = B * S
    K = PEER_HEADS * PEER_TOPK
    n_blk = T // PEER_TOKEN_BLOCK
    hb = h.reshape(n_blk, PEER_TOKEN_BLOCK, D)
    ib = idx.reshape(n_blk, PEER_TOKEN_BLOCK, K)
    gb = g.reshape(n_blk, PEER_TOKEN_BLOCK, K)

    def experts(blk):
        h_t, i_t, g_t = blk
        act = jnp.einsum('td,tkd->tk', h_t, u[i_t], preferred_element_type=jnp.float32)
        a = (jax.nn.gelu(act, approximate=False) * g_t).astype(h_t.dtype)
        return jnp.einsum('tk,tkd->td', a, v[i_t])

    y = lax.map(experts, (hb, ib, gb))
    return y.reshape(B, S, D)

def setup_inputs(seed: int = 0) -> dict:
    key = jax.random.key(seed)
    ks = jax.random.split(key, 17)
    L, D = DEPTH, D_MODEL
    f32 = jnp.float32

    def nrm(k, shape, scale):
        return jax.random.normal(k, shape, f32) * scale

    def gain(k, shape):
        return 1.0 + 0.02 * jax.random.normal(k, shape, f32)

    return {
        "x": jax.random.normal(ks[0], (BATCH, SEQ, D), f32),
        "attn_norm": gain(ks[1], (L, D)),
        "w_in": nrm(ks[2], (L, D, D_IN), D ** -0.5),
        "mla_q_norm": gain(ks[3], (L, MLA_Q_LORA)),
        "mla_w_uq": nrm(ks[4], (L, MLA_Q_LORA, MLA_HEADS * (MLA_NOPE + MLA_ROPE)), MLA_Q_LORA ** -0.5),
        "mla_kv_norm": gain(ks[5], (L, MLA_KV_LORA)),
        "mla_w_ukv": nrm(ks[6], (L, MLA_KV_LORA, MLA_HEADS * (MLA_NOPE + MLA_V)), MLA_KV_LORA ** -0.5),
        "nat_rpb": nrm(ks[7], (L, NAT_HEADS, 2 * NAT_WIN_R - 1, 2 * NAT_WIN_C - 1), 0.1),
        "mla_out_norm": gain(ks[8], (L, MLA_WIDTH)),
        "nat_out_norm": gain(ks[9], (L, NAT_WIDTH)),
        "w_out": nrm(ks[10], (L, D_MIX, D), D_MIX ** -0.5),
        "ffn_norm": gain(ks[11], (L, D)),
        "peer_w_q": nrm(ks[12], (L, D, PEER_HEADS * PEER_D_QUERY), D ** -0.5),
        "peer_sub_keys": nrm(ks[13], (L, 2, PEER_N_KEYS, PEER_D_QUERY // 2), (PEER_D_QUERY // 2) ** -0.5),
        "peer_u": nrm(ks[14], (L, PEER_N_EXPERTS, D), D ** -0.5),
        "peer_v": nrm(ks[15], (L, PEER_N_EXPERTS, D), PEER_HEADS ** -0.5),
        "final_norm": gain(ks[16], (D,)),
    }

def reference(x, attn_norm, w_in, mla_q_norm, mla_w_uq, mla_kv_norm, mla_w_ukv, nat_rpb,
              mla_out_norm, nat_out_norm, w_out, ffn_norm, peer_w_q, peer_sub_keys,
              peer_u, peer_v, final_norm):
    for l in range(DEPTH):
        h = rms_norm(x, attn_norm[l])
        proj = h @ w_in[l]
        c_q, c_kv, k_pe, nq, nk, nv = jnp.split(proj, IN_OFFSETS, axis=-1)
        mla_o = mla_group(c_q, c_kv, k_pe, mla_q_norm[l], mla_w_uq[l], mla_kv_norm[l], mla_w_ukv[l])
        nat_o = nat_group(nq, nk, nv, nat_rpb[l])
        mixed = jnp.concatenate([rms_norm(mla_o, mla_out_norm[l]),
                                 rms_norm(nat_o, nat_out_norm[l])], axis=-1)
        x = x + mixed @ w_out[l]
        x = x + peer_ffn(rms_norm(x, ffn_norm[l]), peer_w_q[l], peer_sub_keys[l], peer_u[l], peer_v[l])
    return rms_norm(x, final_norm)


_drawn_inputs = setup_inputs


def setup_inputs(seed=0):
    import zlib

    import numpy as np

    out = dict(_drawn_inputs(seed))
    spreads = {}
    factors = {'mla_q_norm': 3.036, 'final_norm': 2.887}
    for name, (base, spread) in spreads.items():
        noise = np.random.default_rng([zlib.crc32(name.encode()), seed]).standard_normal(out[name].shape)
        drawn = base * np.exp(spread * noise) if base else spread * noise
        out[name] = __import__('jax').numpy.asarray(drawn.astype(out[name].dtype))
    for name, factor in factors.items():
        out[name] = (out[name] * factor).astype(out[name].dtype)
    return out
```

```python
from contextlib import ExitStack, contextmanager

import concourse.bass as bass
from concourse import mybir

F32 = mybir.dt.float32
F32R = mybir.dt.float32r
BF16 = mybir.dt.bfloat16
U32 = mybir.dt.uint32
ACT = mybir.ActivationFunctionType
ALU = mybir.AluOpType
AX = mybir.AxisListType

P = 128
L, D, T = 2, 2048, 256
TT = T // P
DC = D // P
SL = 512
Q_LORA, KV_LORA, ROPE = 512, 256, 64
MH, NOPE, MV = 8, 128, 128
NH, ND = 16, 64
W_MIX = 1024
D_IN = 3904
NAT0 = Q_LORA + KV_LORA + ROPE
GRID_W, WIN_R, WIN_C, ROWS = 64, 8, 16, 4
NDR = 6
DR_ALL = 2 * WIN_R - 1
DC_ALL = 2 * WIN_C - 1
PH, NK, TOPK = 8, 128, 16
HK = PH * TOPK
HALF_J = NK // 2
EPS = 1e-6
NEG = -3.0e38
NP = 4
PU = 4
R = 4
GC = dict(attn=0, ffn=16, q=32, kv=36, mla=38, nat=46)
NG = 54

ARENA = HALF_J * T
GJ, BT, SHIFT = 4, 16, 8
GROUPS, PAIRS, BATCHES = HALF_J // GJ, HALF_J // GJ // 2, T // BT
N_A, N_HALF = 16, 2 * HALF_J
U_A, U_HALF, U_AHALF = 4 * DC, 2 * GROUPS * DC, GROUPS * DC
GATE0 = 2
YN = 8192
REST = 12288
STAGE = 7168


def build(nc, x_in, gains, w_in, w_uq, w_ukv, rpb, w_out, w_q, keys, u_tab, v_tab, final_norm, consts, out):
    ctx = ExitStack()
    with ctx:
        def sb(name, shape, dt=F32):
            return ctx.enter_context(nc.sbuf_tensor(name, shape, dt))

        x = sb("x", [P, TT, D])
        arena = sb("arena", [P, ARENA])
        stage = sb("stage", [P, STAGE])
        ht_hi = sb("ht_hi", [P, DC, T], F32R)
        ht_lo = sb("ht_lo", [P, DC, T], F32R)
        unit_hi = sb("unit_hi", [P, R, SL], F32R)
        unit_lo = sb("unit_lo", [P, R, SL], F32R)
        piece = sb("piece", [P, NP, PU * SL])
        wj_hi = sb("wj_hi", [P, 2, T], F32R)
        wj_lo = sb("wj_lo", [P, 2, T], F32R)
        ga = sb("ga", [P, 2, TT, SL])
        con = sb("con", [P, 128 + 128 + 64 + 16])
        iota = sb("iota", [P, NK], BF16)
        grow = stage[:, 0:P]
        gall = sb("gall", [P, L * NG])
        gcol = sb("gcol", [P, NG])
        i1t = sb("i1t", [P, T], BF16)
        i2t = sb("i2t", [P, T], BF16)
        gt = sb("gt", [P, 3, T], BF16)
        ssq = sb("ssq", [P, 4])
        rms = sb("rms", [P, 4])
        rstd = sb("rstd", [P, 4])
        mx = sb("mx", [P, 2, 4])
        den = sb("den", [P, 2, 4])
        rden = sb("rden", [P, 2, 4])
        smax = sb("smax", [P, 2, 4])
        per_round = sb("per_round", [P, 2 * TT * PH])
        ident = con[:, 0:128]
        cos = con[:, 128:192].rearrange("p (a f) -> p a f", a=TT)
        sin = con[:, 192:256].rearrange("p (a f) -> p a f", a=TT)
        mask = con[:, 256:320]
        iota16 = con[:, 320:336]
        ps = ctx.enter_context(nc.psum_tensor("ps", [P, 8 * SL], F32))

        rpb_pad = nc.dram_tensor("rpb_pad", (L * NH * DR_ALL, P), F32).ap()
        skewed = nc.dram_tensor("skewed", (NH, NDR + 1, GRID_W, P - 1), F32).ap()

        names = [f"arrived{s}" for s in range(NP)] + """hi_ready lo_ready unit_used squared mean_ready root_ready
            rows_ready chunk_turned chunk_hi chunk_lo chain_v chain_a bank_full bank_read scored maxed expd probs_turned
            probs_read mixed attended layer_in bias_in keys_in ranked gates_exp slice_out nat_turned rope_ready heads_turned
            u_turned gelu_done gelu_turned w_stored onehot_rows gates_made w_gated wj_hi_ready wj_lo_ready
            hot_chain rank_chain psum_clear bias_skewed stored q_out qt_full qt_read score_full score_read small_full small_read x_added""".split()
        S = {n: ctx.enter_context(nc.semaphore(n)) for n in names}
        setup_in = ctx.enter_context(nc.semaphore("setup_in"))
        setup_c = ctx.enter_context(nc.semaphore("setup_c"))
        pad_ready = ctx.enter_context(nc.semaphore("pad_ready"))
        bias_made = ctx.enter_context(nc.semaphore("bias_made"))
        nums = sorted(s.num for s in S.values())
        assert nums[-1] - nums[0] == len(nums) - 1
        cleared = range(nums[0], nums[-1] + 1)

        def bank(b, n=1):
            return ps[:, b * SL:(b + n) * SL]

        def rounds(slot, n):
            return (n - slot) * (16 // NP) + 16

        def piece_here(eng, slot, n):
            eng.wait_ge(S[f"arrived{slot}"], rounds(slot, n))

        def unit_high(act, u, k, src, w, wait=True):
            if wait:
                act.wait_ge(S["unit_used"], u - R + 1)
            nc.scalar.activation(unit_hi[:, k % R, 0:w], src, ACT.Copy).then_inc(S["hi_ready"], 1)

        def unit_low(dve, u, k, src, w):
            dve.wait_ge(S["hi_ready"], u + 1)
            nc.vector.tensor_tensor(unit_lo[:, k % R, 0:w], src, unit_hi[:, k % R, 0:w].bitcast(F32),
                                    ALU.subtract).then_inc(S["lo_ready"], 1)

        def unit_product(pe, u, k, hi, lo, outs, w, start, stop):
            pe.wait_ge(S["lo_ready"], u + 1)
            last = None
            for tt in range(TT):
                a, b = hi[:, tt * P:(tt + 1) * P], lo[:, tt * P:(tt + 1) * P]
                nc.tensor.matmul(outs[tt], a, unit_hi[:, k % R, 0:w], start=start, stop=False)
                nc.tensor.matmul(outs[tt], a, unit_lo[:, k % R, 0:w], start=False, stop=False)
                last = nc.tensor.matmul(outs[tt], b, unit_hi[:, k % R, 0:w], start=False, stop=stop)
            last.then_inc(S["unit_used"], 1)

        def unit_src(n, k, w=SL):
            return piece[:, n % NP, k * w:(k + 1) * w]

        def slice_high(act, u0, n0, k0, m0, w, wait=True):
            for k in range(DC):
                if k % PU == 0:
                    piece_here(act, (m0 + k // PU) % NP, n0 + k // PU)
                unit_high(act, u0 + k, k0 + k, unit_src(m0 + k // PU, k % PU, w), w, wait or k >= R)

        def slice_low(dve, u0, k0, m0, w):
            for k in range(DC):
                unit_low(dve, u0 + k, k0 + k, unit_src(m0 + k // PU, k % PU, w), w)

        def slice_product(pe, u0, k0, outs, w):
            for k in range(DC):
                unit_product(pe, u0 + k, k0 + k, ht_hi[:, k], ht_lo[:, k], outs, w, k == 0, k == DC - 1)

        def squares(act, parts, wait=None):
            if wait:
                act.wait_ge(*wait)
            for i, (c, rows, junk) in enumerate(parts):
                ins = nc.scalar.activation(junk, rows, ACT.Square, accum_out=ssq[:, c:c + 1])
            ins.then_inc(S["squared"], 1)

        def means(dve, n, parts):
            dve.wait_ge(S["squared"], n)
            for c0, c1, width in parts:
                ins = nc.vector.tensor_scalar(rms[:, c0:c1], ssq[:, c0:c1], 1.0 / width, EPS, ALU.mult, ALU.add)
            ins.then_inc(S["mean_ready"], 1)

        def roots(act, n, cols):
            act.wait_ge(S["mean_ready"], n)
            nc.scalar.activation(ssq[:, 0:cols], rms[:, 0:cols], ACT.Sqrt).then_inc(S["root_ready"], 1)

        def scale_rows(dve, n, cols, parts, chain):
            dve.wait_ge(S["root_ready"], n)
            chain(nc.vector.reciprocal(rstd[:, 0:cols], ssq[:, 0:cols]))
            for c, dst, src in parts:
                ins = nc.vector.tensor_scalar(dst, src, rstd[:, c:c + 1], None, ALU.mult)
            ins.then_inc(S["rows_ready"], 1)

        def turn_chunks(pe, n_rows, c0, chunks):
            pe.wait_ge(S["rows_ready"], n_rows)
            for i, src in enumerate(chunks):
                c = c0 + i
                if c >= 4:
                    pe.wait_ge(S["chunk_lo"], c - 3)
                for tt in range(TT):
                    ins = nc.tensor.transpose(bank(4 + c % 4)[:, tt * P:(tt + 1) * P], src(tt), ident)
                ins.then_inc(S["chunk_turned"], 1)

        def chunks_high(act, c0, count, gain0):
            for i in range(count):
                c = c0 + i
                act.wait_ge(S["chunk_turned"], c + 1)
                nc.scalar.activation(ht_hi[:, i], bank(4 + c % 4)[:, 0:T], ACT.Copy,
                                     scale=gcol[:, gain0(i):gain0(i) + 1]).then_inc(S["chunk_hi"], 1)

        def chunks_low(dve, c0, count, gain0):
            for i in range(count):
                c = c0 + i
                dve.wait_ge(S["chunk_hi"], c + 1)
                nc.vector.scalar_tensor_tensor(ht_lo[:, i], bank(4 + c % 4)[:, 0:T], gcol[:, gain0(i):gain0(i) + 1],
                                               ht_hi[:, i].bitcast(F32), ALU.mult, ALU.subtract
                                               ).then_inc(S["chunk_lo"], 1)

        def chainer(eng, sem):
            count = [0]

            def chain(ins):
                count[0] += 1
                ins.then_inc(sem, 1)
                eng.wait_ge(sem, count[0])
            return chain

        with nc.Block() as block:
            @block.sync
            def _(sp):
                sp.dma_start(x[:, :, :], x_in.rearrange("(a p) d -> p a d", p=P)).then_inc(setup_in, 16)
                sp.dma_start(con[:, :], consts).then_inc(setup_in, 16)
                for l in range(L):
                    for name in GC:
                        r0 = l * NG + GC[name]
                        src = gains[name][l].rearrange("(c p) -> c p", p=P)
                        sp.dma_start(grow[r0:r0 + src.shape[0], :], src).then_inc(setup_in, 16)

            @block.gpsimd
            def _(pool):
                nc.gpsimd.iota(iota[:, :], [[1, NK]], base=0, channel_multiplier=0,
                               allow_small_or_imprecise_dtypes=True)
                zeros = arena[0:120, 0:512]
                nc.gpsimd.memset(zeros, 0.0).then_inc(pad_ready, 1)

            @block.scalar
            def _(act):
                act.wait_ge(pad_ready, 1)
                pad = rpb_pad.rearrange("(p a) m -> p a m", p=120)
                act.dma_start(pad, arena[0:120, 0:512].rearrange("p (a m) -> p a m", m=P)).then_inc(bias_made, 16)
                act.wait_ge(bias_made, 16)
                m0 = GRID_W - WIN_C
                act.dma_start(rpb_pad[:, m0:m0 + DC_ALL], rpb.rearrange("l h r c -> (l h r) c")).then_inc(bias_made, 16)

            @block.tensor
            def _(pe):
                pe.wait_ge(setup_in, 16 * (2 + L * len(GC)))
                nc.tensor.transpose(bank(0)[:, 0:L * NG], grow[0:L * NG, :], ident[0:L * NG, 0:L * NG]
                                    ).then_inc(setup_c, 1)

            @block.vector
            def _(dve):
                dve.wait_ge(setup_c, 1)
                nc.vector.tensor_copy(gall[:, :], bank(0)[:, 0:L * NG])

        proj = arena[:, 0:YN].rearrange("p (s a n) -> p s a n", s=8, a=TT)
        ckv = proj[:, 0, :, 0:KV_LORA]
        kpe = proj[:, 0, :, KV_LORA:KV_LORA + ROPE]
        cq = proj[:, 1]
        yn = arena[:, YN:YN + TT * D].rearrange("p (a d) -> p a d", a=TT)
        nqt = arena[:, YN:YN + 2048].rearrange("p (h t) -> p h t", h=8)
        nkt = arena[:, YN + 2048:YN + 4096].rearrange("p (h t) -> p h t", h=8)
        sbuf_s = arena[:, REST:REST + 2048].rearrange("p (b h k) -> p b h k", b=2, h=4)
        sbuf_p = arena[:, REST + 2048:REST + 4096].rearrange("p (b h c q) -> p b h c q", b=2, h=4, c=2)
        nat_o = arena[:, 2048:4096].rearrange("p (a n) -> p a n", a=TT)
        bias = stage[:, 0:NH * NDR * GRID_W].rearrange("p (h m) -> p h m", h=NH)
        bias_rows = stage[:, 0:NH * NDR * GRID_W].rearrange("p (h r k) -> p h r k", h=NH, r=NDR)
        cqn = arena[:, 4096:5120].rearrange("p (a n) -> p a n", a=TT)
        ckvn = arena[:, 5120:5632].rearrange("p (a n) -> p a n", a=TT)
        q_mla = arena[:, YN:YN + 3072].rearrange("p (a n) -> p a n", a=TT)
        kv_mla = arena[:, 4096:8192].rearrange("p (a n) -> p a n", a=TT)
        qpe = arena[:, YN + 3072:YN + 4096].rearrange("p (a h f) -> p a h f", a=TT, h=MH)
        mla_o = arena[:, YN:YN + 2048].rearrange("p (a n) -> p a n", a=TT)
        qnt = stage[:, 0:2048].rearrange("p (h t) -> p h t", h=MH)
        qpt = stage[:, 2048:3072].rearrange("p (h t) -> p h t", h=4)
        knt = stage[:, 3072:5120].rearrange("p (h t) -> p h t", h=MH)
        kpt = stage[:, 5120:5376]
        kpr = stage[:, 5376:5632].rearrange("p (a b f) -> p a b f", a=TT, b=2)
        rt1 = stage[:, 5632:6144].rearrange("p (a h f) -> p a h f", a=TT, h=MH)
        rt2 = stage[:, 6144:6656].rearrange("p (a h f) -> p a h f", a=TT, h=MH)

        SCALE = float(NOPE + ROPE) ** -0.5
        NB = 8
        MB = 4
        U_UQ, U_UKV, U_OUT = 8 * DC, 8 * DC + 12, 8 * DC + 20
        N_UQ, N_UKV, N_OUT = 32, 35, 37

        QH, KVH = NOPE + ROPE, NOPE + MV

        def k_head(h, tt):
            return kv_mla[:, tt, h * KVH:h * KVH + NOPE]

        def v_head(h, tt):
            return kv_mla[:, tt, h * KVH + NOPE:(h + 1) * KVH]

        q_peer = arena[:, 0:TT * D].rearrange("p (a n) -> p a n", a=TT)
        q_peer_t = arena[:, 4096:8192].rearrange("p (b t) -> p b t", t=T)
        w_view = arena[:, :].rearrange("p (j t) -> p j t", t=T)
        score_rows = stage[:, 0:4096]
        scores = score_rows.rearrange("p (a b n) -> p a b n", a=TT, b=2 * PH)
        keys_rows = stage[:, 5888:6144].rearrange("p (l s d) -> p l s d", l=1, s=2)
        keys_t = stage[:, 4096:4352]
        work, cand, pick = (stage[:, c:c + 512].rearrange("p (a n) -> p a n", a=2) for c in (4096, 4608, 5120))
        pick = pick.rearrange("p a (k j) -> p a k j", k=TOPK)
        small = stage[:, 5632:5888]
        key_rows = [stage[:, 6144:6400], stage[:, 6400:6656]]
        gate_rows, gates = stage[:, 6656:6912], stage[:, 6912:7168]
        top_v = small[:, 0:32].rearrange("p (a k) -> p a k", a=2)
        top_i = small[:, 32:64].bitcast(U32).rearrange("p (a k) -> p a k", a=2)
        top_if = small[:, 64:96].rearrange("p (a k) -> p a k", a=2)
        best_v = small[:, 96:112]
        best_p = small[:, 112:128].bitcast(U32)
        pos_i = small[:, 128:160].bitcast(U32).rearrange("p (a k) -> p a k", a=2)
        pos_f = small[:, 160:192].rearrange("p (a k) -> p a k", a=2)
        gmax, gsum = per_round[:, 0:TT * PH], per_round[:, TT * PH:2 * TT * PH]
        hot2 = stage[:, 0:2048].bitcast(BF16).rearrange("p (b k t) -> p b k t", b=2, t=BT)
        hotg = stage[:, 2048:5120].bitcast(BF16).rearrange("p (b c k t) -> p b c k t", b=2, c=3, t=BT)
        iota_t = stage[:, 5120:6144].bitcast(BF16).rearrange("p (k t) -> p k t", t=BT)
        rest = ga[:, 1, 0].rearrange("p (a t) -> p a t", a=2)
        hot1 = ga[:, 0].rearrange("p a n -> p (a n)").bitcast(BF16).rearrange("p (b k t) -> p b k t", b=2, t=BT)

        def g_count(g):
            return g[0] * GROUPS + g[1]

        def g_units(g):
            return g[0] * U_HALF + g[1] * DC

        def latent_src(s, k):
            if s < 3:
                return unit_src(N_UQ + s, k)
            c = k * 2 * SL + ((s - 3) % 2) * SL
            return piece[:, (N_UKV + (s - 3) // 2) % NP, c:c + SL]

        def heads_dst(i):
            if i < 4:
                return qnt[:, 2 * i:2 * i + 2].rearrange("p h t -> p (h t)"), SL
            if i < 8:
                return knt[:, 2 * (i - 4):2 * (i - 4) + 2].rearrange("p h t -> p (h t)"), SL
            if i < 10:
                return qpt[:, 2 * (i - 8):2 * (i - 8) + 2].rearrange("p h t -> p (h t)"), SL
            return kpt, T

        def score_at(b, h):
            c = 2 * (h % 2) + h // 2
            return bank(2 * (b % 2), 2)[:, c * T:(c + 1) * T]

        def attention_act(act, b0, count, mla):
            def probs(b):
                if b >= b0 + 2:
                    act.wait_ge(S["probs_turned"], b - 1)
                act.wait_ge(S["maxed"], b + 1)
                for h in range(4):
                    src = score_at(b, h) if mla else sbuf_s[:, b % 2, h]
                    ins = nc.scalar.activation(sbuf_s[:, b % 2, h], src, ACT.Exp,
                                               bias=mx[:, b % 2, h:h + 1], scale=SCALE if mla else 1.0,
                                               accum_out=den[:, b % 2, h:h + 1])
                ins.then_inc(S["expd"], 1)

            def turned(b):
                act.wait_ge(S["probs_turned"], b + 1)
                if b >= b0 + 2:
                    act.wait_ge(S["mixed"], b - 1)
                nc.scalar.activation(sbuf_p[:, b % 2].rearrange("p h c q -> p (h c q)"), bank(4, 2),
                                     ACT.Copy).then_inc(S["probs_read"], 1)

            for b in range(b0, b0 + count + 1):
                if b < b0 + count:
                    probs(b)
                if b > b0:
                    turned(b - 1)

        def attention_dve(dve, b0, count, mla, chain):
            def maxima(b):
                dve.wait_ge(S["scored"], b + 1)
                i = b - b0
                sc = bank(2 * (b % 2), 2).rearrange("p (o e k) -> p e o k", o=2, e=2)
                if not mla:
                    if b >= b0 + 2:
                        dve.wait_ge(S["probs_turned"], b - 1)
                    tt, h0 = i // 4, 4 * (i % 4)
                    r0 = (2 - 2 * tt) * GRID_W
                    for o in range(2):
                        ins = nc.vector.scalar_tensor_tensor(
                            sbuf_s[:, b % 2, o::2], bank(2 * (b % 2) + o).rearrange("p (e k) -> p e k", e=2),
                            float(ND) ** -0.5, bias[:, h0 + o:h0 + 4:2, r0:r0 + T], ALU.mult, ALU.add)
                    chain(ins)
                    chain(nc.vector.tensor_reduce(smax[:, b % 2, :], sbuf_s[:, b % 2], AX.X, ALU.max))
                else:
                    chain(nc.vector.tensor_reduce(smax[:, b % 2, :].rearrange("p (e o) -> p e o", o=2), sc, AX.X,
                                                  ALU.max))
                nc.vector.tensor_scalar(mx[:, b % 2, :], smax[:, b % 2, :], -(SCALE if mla else 1.0), None,
                                        ALU.mult).then_inc(S["maxed"], 1)

            def normalise(b):
                dve.wait_ge(S["mixed"], b + 1)
                i = b - b0
                w = MV if mla else ND
                tt, h0 = (i // 2, 4 * (i % 2)) if mla else (i // 4, 4 * (i % 4))
                dst = (mla_o if mla else nat_o)[:, tt, h0 * w:(h0 + 4) * w].rearrange("p (h d) -> p h d", h=4)
                nc.vector.tensor_tensor(dst, bank(6 + b % 2)[:, 0:4 * w].rearrange("p (h d) -> p h d", h=4),
                                        rden[:, b % 2, :].unsqueeze(2).to_broadcast([P, 4, w]),
                                        ALU.mult).then_inc(S["attended"], 1)

            for b in range(b0, b0 + count + 2):
                if b >= b0 + 2:
                    dve.wait_ge(S["expd"], b - 1)
                    chain(nc.vector.reciprocal(rden[:, b % 2, :], den[:, b % 2, :]))
                if b < b0 + count:
                    maxima(b)
                if b >= b0 + 2:
                    normalise(b - 2)

        def attention_pe(pe, b0, count, scores, v_of, w, mla):
            for b in range(b0, b0 + count + 2):
                if b < b0 + count:
                    if b >= b0 + 2:
                        pe.wait_ge(S["expd" if mla else "maxed"], b - 1)
                    outs = [score_at(b, h) for h in range(4)]
                    scores(b - b0, outs).then_inc(S["scored"], 1)
                if b0 + 1 <= b <= b0 + count:
                    a = b - 1
                    pe.wait_ge(S["expd"], a + 1)
                    if a > b0:
                        pe.wait_ge(S["probs_read"], a)
                    for h in range(4):
                        for c in range(2):
                            ins = nc.tensor.transpose(bank(4, 2)[:, (2 * h + c) * P:(2 * h + c + 1) * P],
                                                      sbuf_s[:, a % 2, h, c * P:(c + 1) * P], ident)
                    ins.then_inc(S["probs_turned"], 1)
                if b >= b0 + 2:
                    a = b - 2
                    pe.wait_ge(S["probs_read"], a + 1)
                    if a >= b0 + 2:
                        pe.wait_ge(S["attended"], a - 1)
                    for h in range(4):
                        for c in range(2):
                            ins = nc.tensor.matmul(bank(6 + a % 2)[:, h * w:(h + 1) * w],
                                                   sbuf_p[:, a % 2, h, c], v_of(a - b0, h, c),
                                                   start=(c == 0), stop=(c == 1))
                    ins.then_inc(S["mixed"], 1)

        with nc.Fori(0, L) as layer:
            with nc.Block() as block:
                @block.sync
                def _(sp):
                    wl = w_in.rearrange("l (c p) n -> p l c n", p=P)

                    def w_piece(n, slot, q, col, w, wait=True):
                        dst = piece[:, slot, 0:PU * w].rearrange("p (l c n) -> p l c n", l=1, c=PU)
                        if wait:
                            sp.wait_ge(S["lo_ready"], PU * (n - NP + 1))
                        sp.dma_start(dst, wl[:, bass.ds(layer, 1), q * PU:(q + 1) * PU, col]).then_inc(S[f"arrived{slot}"], 16)

                    for q in range(4):
                        w_piece(q, q, q, slice(Q_LORA, NAT0), NAT0 - Q_LORA, wait=False)
                    for q in range(4):
                        w_piece(4 + q, q, q, slice(0, Q_LORA), SL)
                    pad_rows = rpb_pad.rearrange("(l h r) m -> l h r m", h=NH, r=DR_ALL)
                    sp.wait_ge(bias_made, 16 * 2)

                    def skew(r):
                        src = pad_rows[bass.ds(layer, 1), :, bass.ds(r + WIN_R - ROWS, 1), 0:P - 1].rearrange(
                            "l h r m -> (l h) r m").to_broadcast([NH, GRID_W, P - 1])
                        dst = skewed[:, bass.ds(r, 1)].rearrange("h r c m -> h (r c) m")
                        sp.dma_start(dst, src).then_inc(S["bias_skewed"], 16)

                    with sp.Fori(0, 6) as s:
                        for q in range(4):
                            w_piece(8 + s * 4 + q, q, q, bass.ds(NAT0 + s * SL, SL), SL)
                        skew(s)
                    skew(NDR)
                    sp.wait_ge(S["bias_skewed"], 16 * (NDR + 1))
                    row = GRID_W * (P - 1)
                    for par in range(2):
                        for r in range(NDR):
                            src = bass.AP(skewed.tensor, (r + 1 - par) * row + GRID_W - 1, [[P - 2, GRID_W], [(NDR + 1) * row, NH], [1, GRID_W]])
                            sp.dma_start(bias_rows[par * GRID_W:(par + 1) * GRID_W, :, r], src
                                         ).then_inc(S["bias_in"], 16)
                    uq = w_uq.rearrange("l (c p) n -> p l c n", p=P)
                    for s in range(3):
                        n = N_UQ + s
                        sp.wait_ge(S["lo_ready"], PU * (n - NP + 1))
                        sp.dma_start(piece[:, n % NP, :].rearrange("p (l c n) -> p l c n", l=1, c=4),
                                     uq[:, bass.ds(layer, 1), :, s * SL:(s + 1) * SL]).then_inc(S[f"arrived{n % NP}"], 16)
                    ukv = w_ukv.rearrange("l (c p) n -> p l c n", p=P)
                    for s in range(2):
                        n = N_UKV + s
                        sp.wait_ge(S["lo_ready"], PU * (n - NP + 1))
                        sp.dma_start(piece[:, n % NP, :].rearrange("p (l c n) -> p l c n", l=1, c=2),
                                     ukv[:, bass.ds(layer, 1), :, s * 1024:(s + 1) * 1024]).then_inc(S[f"arrived{n % NP}"], 16)
                    wo = w_out.rearrange("l (c p) n -> p l c n", p=P)
                    with sp.Fori(0, 4) as s:
                        for q in range(4):
                            slot = (N_OUT + q) % NP
                            sp.wait_ge(S["lo_ready"], PU * (N_OUT + s * 4 + q - NP + 1))
                            sp.dma_start(piece[:, slot, :].rearrange("p (l c n) -> p l c n", l=1, c=PU),
                                         wo[:, bass.ds(layer, 1), q * PU:(q + 1) * PU, bass.ds(s * SL, SL)]
                                         ).then_inc(S[f"arrived{slot}"], 16)

                @block.scalar
                def _(act):
                    chain = chainer(act, S["chain_a"])
                    squares(act, [(tt, x[:, tt], yn[:, tt]) for tt in range(TT)])
                    roots(act, 1, 2)
                    chunks_high(act, 0, DC, lambda i: GC["attn"] + i)
                    slice_high(act, 0, 0, 0, 0, NAT0 - Q_LORA, wait=False)
                    slice_high(act, DC, 4, 0, 0, SL)

                    def evacuate(s, first, w=SL):
                        act.wait_ge(S["unit_used"], (s + 1) * DC)
                        dst = proj[:, s] if isinstance(s, int) else arena[:, bass.ds(s * 1024, 1024)].rearrange(
                            "p (a n) -> p a n", a=TT)
                        nc.scalar.activation(dst[:, :, 0:w], bank(2 * first, 2).rearrange(
                            "p (a n) -> p a n", a=TT)[:, :, 0:w], ACT.Copy).then_inc(S["slice_out"], 1)

                    evacuate(0, 0, NAT0 - Q_LORA)
                    with act.Fori(0, 3) as i:
                        for b in range(2):
                            s = 2 + i * 2 + b
                            for k in range(DC):
                                if k % PU == 0:
                                    piece_here(act, k // PU, 4 * s + k // PU)
                                unit_high(act, s * DC + k, k, unit_src(k // PU, k % PU), SL)
                                if k == 2:
                                    evacuate(s - 1, 1 - b)
                    evacuate(7, 1)
                    for i in range(8):
                        act.wait_ge(S["bank_full"], i + 1)
                        dst = (nqt if i < 4 else nkt)[:, 2 * (i % 4):2 * (i % 4) + 2].rearrange("p h t -> p (h t)")
                        nc.scalar.activation(dst, bank(4 + i % 4), ACT.Copy).then_inc(S["bank_read"], 1)
                    attention_act(act, 0, NB, False)
                    squares(act, [(tt, cq[:, tt], cqn[:, tt]) for tt in range(TT)]
                            + [(2 + tt, ckv[:, tt], ckvn[:, tt]) for tt in range(TT)])
                    roots(act, 2, 4)
                    chunks_high(act, DC, 6, lambda i: GC["q"] + i)
                    def latent_out(s):
                        act.wait_ge(S["unit_used"], U_UQ + 4 * (s + 1) if s < 3 else U_UKV + 2 * (s - 2))
                        dst = q_mla[:, :, s * SL:(s + 1) * SL] if s < 3 else kv_mla[:, :, (s - 3) * SL:(s - 2) * SL]
                        nc.scalar.activation(dst, bank(2 * (s % 4), 2).rearrange("p (a n) -> p a n", a=TT),
                                             ACT.Copy).then_inc(S["slice_out"], 1)

                    for s in range(7):
                        n = N_UQ + s if s < 3 else N_UKV + (s - 3) // 2
                        if s < 3 or s % 2 == 1:
                            piece_here(act, n % NP, n)
                        for k in range(4 if s < 3 else 2):
                            u = U_UQ + 4 * s + k if s < 3 else U_UKV + 2 * (s - 3) + k
                            unit_high(act, u, u, latent_src(s, k), SL)
                        if s >= 1:
                            latent_out(s - 1)
                    latent_out(6)
                    for i in range(11):
                        act.wait_ge(S["bank_full"], 8 + i + 1)
                        dst, w = heads_dst(i)
                        nc.scalar.activation(dst, bank(4 + i % 4)[:, 0:w], ACT.Copy).then_inc(S["bank_read"], 1)
                    attention_act(act, NB, MB, True)
                    act.wait_ge(S["attended"], NB + MB)
                    squares(act, [(tt, mla_o[:, tt], kv_mla[:, 0, tt * W_MIX:(tt + 1) * W_MIX]) for tt in range(TT)]
                            + [(2 + tt, nat_o[:, tt], kv_mla[:, 1, tt * W_MIX:(tt + 1) * W_MIX])
                               for tt in range(TT)])
                    roots(act, 3, 4)
                    chunks_high(act, DC + 6, DC, lambda i: GC["mla"] + i)
                    with act.Fori(0, 4) as s:
                        for k in range(DC):
                            if k % PU == 0:
                                piece_here(act, (N_OUT + k // PU) % NP, N_OUT + 4 * s + k // PU)
                            unit_high(act, U_OUT + s * DC + k, U_OUT + k, unit_src(N_OUT + k // PU, k % PU), SL)

                @block.vector
                def _(dve):
                    chain = chainer(dve, S["chain_v"])
                    chain(nc.vector.tensor_copy(gcol[:, :], gall[:, bass.ds(layer * NG, NG)]))
                    means(dve, 1, [(0, 2, D)])
                    scale_rows(dve, 1, 2, [(tt, yn[:, tt], x[:, tt]) for tt in range(TT)], chain)
                    chunks_low(dve, 0, DC, lambda i: GC["attn"] + i)
                    slice_low(dve, 0, 0, 0, NAT0 - Q_LORA)
                    slice_low(dve, DC, 0, 0, SL)
                    with dve.Fori(0, 6) as s:
                        slice_low(dve, 2 * DC + s * DC, 0, 0, SL)
                    dve.wait_ge(S["bias_in"], 16 * 2 * NDR)
                    b3 = stage[:, 0:NH * NDR * GRID_W].rearrange("p (m k) -> p m k", k=GRID_W)
                    chain(nc.vector.tensor_tensor(b3, b3, mask.unsqueeze(1).to_broadcast([P, NH * NDR, GRID_W]),
                                                  ALU.add))
                    attention_dve(dve, 0, NB, False, chain)
                    means(dve, 2, [(0, 2, Q_LORA), (2, 4, KV_LORA)])
                    scale_rows(dve, 2, 4, [(tt, cqn[:, tt], cq[:, tt]) for tt in range(TT)]
                               + [(2 + tt, ckvn[:, tt], ckv[:, tt]) for tt in range(TT)], chain)
                    chunks_low(dve, DC, 6, lambda i: GC["q"] + i)
                    for s in range(7):
                        for k in range(4 if s < 3 else 2):
                            u = U_UQ + 4 * s + k if s < 3 else U_UKV + 2 * (s - 3) + k
                            unit_low(dve, u, u, latent_src(s, k), SL)
                    def rotate(parts):
                        for f, s, c, n, of, os_, a, b in parts:
                            nc.vector.tensor_tensor(a, f, c, ALU.mult)
                            ins = nc.vector.tensor_tensor(b, s, n, ALU.mult)
                        chain(ins)
                        for f, s, c, n, of, os_, a, b in parts:
                            ins = nc.vector.tensor_tensor(of, a, b, ALU.subtract)
                        chain(ins)
                        for f, s, c, n, of, os_, a, b in parts:
                            nc.vector.tensor_tensor(a, s, c, ALU.mult)
                            ins = nc.vector.tensor_tensor(b, f, n, ALU.mult)
                        chain(ins)
                        for f, s, c, n, of, os_, a, b in parts:
                            ins = nc.vector.tensor_tensor(os_, a, b, ALU.add)
                        chain(ins)

                    HR = ROPE // 2
                    rotate([(kpe[:, :, 0:HR], kpe[:, :, HR:ROPE], cos, sin, kpr[:, :, 0, 0:HR], kpr[:, :, 0, HR:ROPE],
                             rt1[:, :, 0], rt2[:, :, 0])])
                    chain(nc.vector.tensor_copy(kpr[:, :, 1], kpr[:, :, 0]))
                    dve.wait_ge(S["slice_out"], 8 + 3)
                    parts = []
                    for h in range(MH):
                        c = h * QH + NOPE
                        parts.append((q_mla[:, :, c:c + HR], q_mla[:, :, c + HR:c + ROPE], cos, sin,
                                      qpe[:, :, h, 0:HR], qpe[:, :, h, HR:ROPE], rt1[:, :, h], rt2[:, :, h]))
                    rotate(parts)
                    dve.sem_inc(S["rope_ready"], 1)
                    attention_dve(dve, NB, MB, True, chain)
                    means(dve, 3, [(0, 4, W_MIX)])
                    scale_rows(dve, 3, 4, [(tt, mla_o[:, tt], mla_o[:, tt]) for tt in range(TT)]
                               + [(2 + tt, nat_o[:, tt], nat_o[:, tt]) for tt in range(TT)], chain)
                    chunks_low(dve, DC + 6, DC, lambda i: GC["mla"] + i)
                    with dve.Fori(0, 4) as s:
                        for k in range(DC):
                            unit_low(dve, U_OUT + s * DC + k, U_OUT + k, unit_src(N_OUT + k // PU, k % PU), SL)
                    for s in range(4):
                        dve.wait_ge(S["unit_used"], U_OUT + (s + 1) * DC)
                        xs = x[:, :, s * SL:(s + 1) * SL]
                        nc.vector.tensor_tensor(xs, bank(2 * s, 2).rearrange("p (a n) -> p a n", a=TT), xs, ALU.add)

                @block.tensor
                def _(pe):
                    turn_chunks(pe, 1, 0, [lambda tt, c=c: yn[:, tt, c * P:(c + 1) * P] for c in range(DC)])
                    pe.wait_ge(S["chunk_lo"], DC)
                    slice_product(pe, 0, 0, [bank(tt)[:, 0:NAT0 - Q_LORA] for tt in range(TT)], NAT0 - Q_LORA)
                    slice_product(pe, DC, 0, [bank(2 + tt) for tt in range(TT)], SL)
                    with pe.Fori(0, 3) as i:
                        for b in range(2):
                            s = 2 + i * 2 + b
                            pe.wait_ge(S["slice_out"], s - 1)
                            slice_product(pe, s * DC, 0, [bank(2 * b + tt) for tt in range(TT)], SL)
                    pe.wait_ge(S["slice_out"], 8)
                    for i in range(8):
                        if i >= 4:
                            pe.wait_ge(S["bank_read"], i - 3)
                        for k in range(4):
                            pair, tt = 2 * (i % 4) + k // 2, k % 2
                            src = proj[:, (2 if i < 4 else 4) + pair // 4, tt, (pair % 4) * P:(pair % 4 + 1) * P]
                            ins = nc.tensor.transpose(bank(4 + i % 4)[:, k * P:(k + 1) * P], src, ident)
                        ins.then_inc(S["bank_full"], 1)
                    pe.wait_ge(S["bank_read"], 8)

                    def nat_scores(i, outs):
                        tt, h0 = i // 4, 4 * (i % 4)
                        for h in range(4):
                            pair, r0 = (h0 + h) // 2, ((h0 + h) % 2) * ND
                            ins = nc.tensor.matmul(outs[h], nqt[r0:r0 + ND, pair, tt * P:(tt + 1) * P],
                                                   nkt[r0:r0 + ND, pair, :], start=True, stop=True)
                        return ins

                    def nat_v(i, h, c):
                        hh = 4 * (i % 4) + h
                        return proj[:, 6 + hh // 8, c, (hh % 8) * ND:(hh % 8 + 1) * ND]

                    attention_pe(pe, 0, NB, nat_scores, nat_v, ND, False)
                    turn_chunks(pe, 2, DC, [lambda tt, c=c: cqn[:, tt, c * P:(c + 1) * P] for c in range(4)]
                                + [lambda tt, c=c: ckvn[:, tt, c * P:(c + 1) * P] for c in range(2)])
                    pe.wait_ge(S["chunk_lo"], DC + 6)
                    pe.wait_ge(S["attended"], NB)
                    for s in range(3):
                        for k in range(4):
                            u = U_UQ + 4 * s + k
                            unit_product(pe, u, u, ht_hi[:, k], ht_lo[:, k], [bank(2 * s + tt) for tt in range(TT)],
                                         SL, k == 0, k == 3)
                    for s in range(4):
                        if s >= 1:
                            pe.wait_ge(S["slice_out"], 8 + s)
                        for c in range(2):
                            u = U_UKV + 2 * s + c
                            unit_product(pe, u, u, ht_hi[:, 4 + c], ht_lo[:, 4 + c],
                                         [bank(2 * ((3 + s) % 4) + tt) for tt in range(TT)], SL, c == 0, c == 1)
                    pe.wait_ge(S["slice_out"], 8 + 7)
                    for i in range(11):
                        if i == 8:
                            pe.wait_ge(S["rope_ready"], 1)
                        if i >= 4:
                            pe.wait_ge(S["bank_read"], 8 + i - 3)
                        for k in range(4 if i < 10 else 2):
                            tt = k % 2
                            o = bank(4 + i % 4)[:, k * P:(k + 1) * P]
                            if i < 4:
                                h = 2 * i + k // 2
                                ins = nc.tensor.transpose(o, q_mla[:, tt, h * QH:h * QH + NOPE], ident)
                            elif i < 8:
                                ins = nc.tensor.transpose(o, k_head(2 * (i - 4) + k // 2, tt), ident)
                            elif i < 10:
                                hp = 2 * (i - 8) + k // 2
                                ins = nc.tensor.transpose(
                                    o, qpe[:, tt, 2 * hp:2 * hp + 2].rearrange("p h f -> p (h f)"), ident)
                            else:
                                ins = nc.tensor.transpose(o, kpr[:, tt].rearrange("p b f -> p (b f)"), ident)
                        ins.then_inc(S["bank_full"], 1)
                    pe.wait_ge(S["bank_read"], 8 + 11)

                    def mla_scores(i, outs):
                        tt, h0 = i // 2, 4 * (i % 2)
                        for h in range(4):
                            hh = h0 + h
                            r0 = (hh % 2) * ROPE
                            nc.tensor.matmul(outs[h], qnt[:, hh, tt * P:(tt + 1) * P], knt[:, hh, :],
                                             start=True, stop=False)
                            ins = nc.tensor.matmul(outs[h], qpt[r0:r0 + ROPE, hh // 2, tt * P:(tt + 1) * P],
                                                   kpt[r0:r0 + ROPE, :], start=False, stop=True)
                        return ins

                    attention_pe(pe, NB, MB, mla_scores, lambda i, h, c: v_head(4 * (i % 2) + h, c), MV, True)
                    turn_chunks(pe, 3, DC + 6, [lambda tt, c=c: mla_o[:, tt, c * P:(c + 1) * P] for c in range(8)]
                                + [lambda tt, c=c: nat_o[:, tt, c * P:(c + 1) * P] for c in range(8)])
                    pe.wait_ge(S["chunk_lo"], DC + 6 + DC)
                    with pe.Fori(0, 4) as s:
                        outs = [ps[:, bass.ds(s * (2 * SL) + tt * SL, SL)] for tt in range(TT)]
                        for k in range(DC):
                            unit_product(pe, U_OUT + s * DC + k, U_OUT + k, ht_hi[:, k], ht_lo[:, k], outs, SL,
                                         k == 0, k == DC - 1)

            nc.all_engine_barrier(sems_to_clear=cleared)
            with nc.Block() as block:
                @block.sync
                def _(sp):
                    sp.dma_start(keys_rows, keys.rearrange("l s n d -> n l s d")[:, bass.ds(layer, 1)]
                                 ).then_inc(S["keys_in"], 16)
                    wq = w_q.rearrange("l (c p) n -> p l c n", p=P)
                    ut = u_tab.rearrange("l (j p) d -> p l j d", p=P)
                    vt = v_tab.rearrange("l (j p) d -> p l j d", p=P)

                    def put(n, slot, src, c, wait=True):
                        if wait:
                            sp.wait_ge(S["lo_ready"], PU * (n - NP + 1))
                        sp.dma_start(piece[:, slot, :].rearrange("p (l c n) -> p l c n", l=1, c=c), src
                                     ).then_inc(S[f"arrived{slot}"], 16)

                    ly = bass.ds(layer, 1)
                    for q in range(4):
                        put(q, q, wq[:, ly, q * PU:(q + 1) * PU, 0:SL], PU, wait=False)
                    with sp.Fori(1, 4) as s:
                        for q in range(4):
                            put(s * 4 + q, q, wq[:, ly, q * PU:(q + 1) * PU, bass.ds(s * SL, SL)], PU)
                    with sp.Fori(0, 2) as half:
                        with sp.Fori(0, GROUPS) as g:
                            for q in range(4):
                                put(N_A + half * N_HALF + g * 4 + q, q,
                                    ut[:, ly, bass.ds(half * HALF_J + g * GJ, GJ), q * SL:(q + 1) * SL], GJ)
                        with sp.Fori(0, GROUPS) as g:
                            for q in range(4):
                                put(N_A + half * N_HALF + HALF_J + g * 4 + q, q,
                                    vt[:, ly, bass.ds(half * HALF_J + g * 4 + q, 1), :], 1)

                @block.scalar
                def _(act):
                    chain = chainer(act, S["chain_a"])
                    act.sem_inc(S["gelu_done"], 2)
                    act.sem_inc(S["w_stored"], 1)
                    squares(act, [(tt, x[:, tt], yn[:, tt]) for tt in range(TT)])
                    roots(act, 1, 2)
                    chunks_high(act, 0, DC, lambda i: GC["ffn"] + i)
                    slice_high(act, 0, 0, 0, 0, SL, wait=False)
                    with act.Fori(1, 4) as s:
                        slice_high(act, s * DC, s * 4, 0, 0, SL)
                    for s in range(4):
                        act.wait_ge(S["unit_used"], (s + 1) * DC)
                        nc.scalar.activation(q_peer[:, :, s * SL:(s + 1) * SL],
                                             bank(2 * s, 2).rearrange("p (a n) -> p a n", a=TT), ACT.Copy
                                             ).then_inc(S["q_out"], 1)
                    for i in range(9):
                        act.wait_ge(S["qt_full"], i + 1)
                        if i < 8:
                            dst = q_peer_t[:, 2 * i:2 * i + 2].rearrange("p b t -> p (b t)")
                            nc.scalar.activation(dst, bank(i), ACT.Copy).then_inc(S["qt_read"], 1)
                        else:
                            nc.scalar.activation(keys_t, bank(0)[:, 0:2 * NK], ACT.Copy).then_inc(S["qt_read"], 1)
                    for i in range(8):
                        act.wait_ge(S["score_full"], i + 1)
                        nc.scalar.activation(scores[:, i // 4, 4 * (i % 4):4 * (i % 4) + 4].rearrange(
                            "p b n -> p (b n)"), bank(i), ACT.Copy).then_inc(S["score_read"], 1)
                    def gelu(g, par):
                        act.wait_ge(S["unit_used"], U_A + g_units(g) + DC)
                        act.wait_ge(S["gelu_turned"], g_count(g) + 1)
                        for tt in range(TT):
                            ins = nc.scalar.activation(ga[:, par, tt], bank(2 * par + tt), ACT.Gelu)
                        ins.then_inc(S["gelu_done"], 1)

                    def store(g):
                        act.wait_ge(S["gelu_turned"], g_count(g) + 2 + 1)
                        nc.scalar.activation(arena[:, bass.ds(g[1] * (GJ * T), GJ * T)], bank(6, 2), ACT.Copy
                                             ).then_inc(S["w_stored"], 1)

                    def step(half, i, k, tails):
                        g = (half, i * 2 + k // DC)
                        a = i * (2 * DC) + k
                        act.wait_ge(S["unit_used"], U_A + half * U_HALF + a - R + 1)
                        act.wait_ge(S["u_turned"], half * U_AHALF + a + 1)
                        nc.scalar.activation(unit_hi[:, k % R], bank(4 + k % 2), ACT.Copy).then_inc(S["hi_ready"], 1)
                        before = (half, g[1] - 1)
                        if tails and k % DC == 2:
                            gelu(before, (k // DC + 1) % 2)
                        if tails and k % DC == 7:
                            store(before)

                    with act.Fori(0, 2) as half:
                        for k in range(SHIFT):
                            step(half, 0, k, False)
                        with act.Fori(0, PAIRS - 1) as i:
                            for k in range(SHIFT, 2 * DC + SHIFT):
                                step(half, i + k // (2 * DC), k % (2 * DC), True)
                        for k in range(SHIFT, 2 * DC):
                            step(half, PAIRS - 1, k, True)
                        gelu((half, GROUPS - 1), 1)
                        store((half, GROUPS - 1))
                        act.wait_ge(S["ranked"], half + 1)
                        nc.scalar.activation(gates, gate_rows, ACT.Exp).then_inc(S["gates_exp"], 1)
                        act.wait_ge(S["small_full"], half + 1)
                        nc.scalar.activation(i1t[:, :], bank(0)[:, 0:T], ACT.Copy)
                        nc.scalar.activation(i2t[:, :], bank(1)[:, 0:T], ACT.Copy).then_inc(S["small_read"], 1)
                        act.wait_ge(S["w_gated"], (half + 1) * BATCHES + GATE0)
                        with act.Fori(0, GROUPS) as g:
                            for b in range(4):
                                j = g * 4 + b
                                act.wait_ge(S["unit_used"], U_A + half * U_HALF + U_AHALF + (j - 1) * 4)
                                nc.scalar.activation(wj_hi[:, b % 2], arena[:, bass.ds(j * T, T)], ACT.Copy
                                                     ).then_inc(S["wj_hi_ready"], 1)
                                n = N_A + half * N_HALF + HALF_J + j
                                piece_here(act, b, n)
                                for k in range(4):
                                    unit_high(act, U_A + half * U_HALF + U_AHALF + j * 4 + k, k, unit_src(b, k), SL)

                @block.vector
                def _(dve):
                    chain = chainer(dve, S["chain_v"])
                    means(dve, 1, [(0, 2, D)])
                    scale_rows(dve, 1, 2, [(tt, yn[:, tt], x[:, tt]) for tt in range(TT)], chain)
                    chunks_low(dve, 0, DC, lambda i: GC["ffn"] + i)
                    with dve.Fori(0, 4) as s:
                        slice_low(dve, s * DC, 0, 0, SL)
                    dve.wait_ge(S["score_read"], 8)
                    dve.sem_inc(S["psum_clear"], 1)
                    dve.sem_inc(S["w_gated"], GATE0)

                    def link(n, ins):
                        ins.then_inc(S["rank_chain"], 1)
                        dve.wait_ge(S["rank_chain"], n)

                    def rank(part, r):
                        if part == 0:
                            dve.sem_clear(S["rank_chain"])
                            link(1, nc.vector.tensor_copy(work[:, 0], score_rows[:, bass.ds(r * 2 * NK, 2 * NK)]))
                        elif part == 1:
                            for s in range(2):
                                ins = nc.vector.max(top_v[:, s, 0:8], work[:, 0, s * NK:(s + 1) * NK])
                            link(2, ins)
                        elif part == 2:
                            for s in range(2):
                                nc.vector.max_index(top_i[:, s, 0:8], top_v[:, s, 0:8],
                                                    work[:, 0, s * NK:(s + 1) * NK])
                        elif part == 3:
                            for s in range(2):
                                ins = nc.vector.match_replace(work[:, 1, s * NK:(s + 1) * NK], top_v[:, s, 0:8],
                                                              work[:, 0, s * NK:(s + 1) * NK], NEG)
                            link(3, ins)
                        elif part == 4:
                            for s in range(2):
                                ins = nc.vector.max(top_v[:, s, 8:16], work[:, 1, s * NK:(s + 1) * NK])
                            link(4, ins)
                        elif part == 5:
                            for s in range(2):
                                nc.vector.max_index(top_i[:, s, 8:16], top_v[:, s, 8:16],
                                                    work[:, 1, s * NK:(s + 1) * NK])
                        elif part == 6:
                            link(5, nc.vector.tensor_tensor(
                                cand[:, 0].rearrange("p (a b) -> p a b", a=TOPK),
                                top_v[:, 0].unsqueeze(2).to_broadcast([P, TOPK, TOPK]),
                                top_v[:, 1].unsqueeze(1).to_broadcast([P, TOPK, TOPK]), ALU.add))
                            nc.vector.tensor_copy(top_if, top_i)
                        elif part == 7:
                            link(6, nc.vector.max(best_v[:, 0:8], cand[:, 0]))
                            nc.vector.max_index(best_p[:, 0:8], best_v[:, 0:8], cand[:, 0])
                        elif part == 8:
                            link(7, nc.vector.match_replace(cand[:, 1], best_v[:, 0:8], cand[:, 0], NEG))
                        elif part == 9:
                            link(8, nc.vector.max(best_v[:, 8:16], cand[:, 1]))
                            link(9, nc.vector.max_index(best_p[:, 8:16], best_v[:, 8:16], cand[:, 1]))
                        elif part == 10:
                            nc.vector.tensor_copy(gate_rows[:, bass.ds(r * TOPK, TOPK)], best_v)
                            nc.vector.tensor_scalar(pos_i[:, 0], best_p, 4, None, ALU.logical_shift_right)
                            link(10, nc.vector.tensor_scalar(pos_i[:, 1], best_p, TOPK - 1, None, ALU.bitwise_and))
                        elif part == 11:
                            link(11, nc.vector.tensor_copy(pos_f, pos_i))
                        elif part == 12:
                            for s in range(2):
                                ins = nc.vector.tensor_tensor(
                                    pick[:, s], iota16.unsqueeze(1).to_broadcast([P, TOPK, TOPK]),
                                    pos_f[:, s].unsqueeze(2).to_broadcast([P, TOPK, TOPK]), ALU.is_equal)
                            link(12, ins)
                        elif part == 13:
                            for s in range(2):
                                ins = nc.vector.tensor_tensor(
                                    pick[:, s], pick[:, s],
                                    top_if[:, s].unsqueeze(1).to_broadcast([P, TOPK, TOPK]), ALU.mult)
                            link(13, ins)
                        elif part == 14:
                            for s in range(2):
                                ins = nc.vector.tensor_reduce(key_rows[s][:, bass.ds(r * TOPK, TOPK)], pick[:, s],
                                                              AX.X, ALU.add)
                            link(14, ins)

                    assert TT * PH == GROUPS, "a round for each group of experts"
                    for half in range(2):
                        with dve.Fori(0, GROUPS) as g:
                            for k in range(DC):
                                unit_low(dve, U_A + half * U_HALF + g * DC + k, k, bank(4 + k % 2), SL)
                                if half == 0:
                                    rank(k, g)
                        g3 = gates.rearrange("p (r k) -> p r k", k=TOPK)
                        if half == 0:
                            r3 = gate_rows.rearrange("p (r k) -> p r k", k=TOPK)
                            chain(nc.vector.tensor_copy(gmax, r3[:, :, 0]))
                            chain(nc.vector.tensor_tensor(
                                r3, r3, gmax.unsqueeze(2).to_broadcast([P, TT * PH, TOPK]), ALU.subtract))
                            chain(nc.vector.tensor_copy(iota_t, iota[:, :].unsqueeze(2).to_broadcast([P, NK, BT])))
                        dve.sem_inc(S["ranked"], 1)
                        dve.wait_ge(S["gates_exp"], half + 1)
                        chain(nc.vector.tensor_reduce(gsum, g3, AX.X, ALU.add))
                        chain(nc.vector.reciprocal(gmax, gsum))
                        nc.vector.tensor_tensor(g3, g3, gmax.unsqueeze(2).to_broadcast([P, TT * PH, TOPK]), ALU.mult
                                                ).then_inc(S["rows_ready"], 1)
                        dve.wait_ge(S["small_read"], half + 1)
                        gps = bank(2)[:, 0:T]
                        chain(nc.vector.tensor_copy(gt[:, 0], gps))
                        chain(nc.vector.tensor_tensor(rest[:, 0], gps, gt[:, 0], ALU.subtract))
                        chain(nc.vector.tensor_copy(gt[:, 1], rest[:, 0]))
                        chain(nc.vector.tensor_tensor(rest[:, 1], rest[:, 0], gt[:, 1], ALU.subtract))
                        chain(nc.vector.tensor_copy(gt[:, 2], rest[:, 1]))

                        def hot_rows(i, b):
                            ts = bass.ds((i * 2 + b) * BT, BT)
                            n = half * BATCHES + i * 2 + b
                            nc.vector.tensor_tensor(
                                hot1[:, b], iota_t[:, half * HALF_J:(half + 1) * HALF_J],
                                i1t[:, ts].unsqueeze(1).to_broadcast([P, HALF_J, BT]), ALU.is_equal
                            ).then_inc(S["hot_chain"], 1)
                            dve.wait_ge(S["gates_made"], n + 1)
                            nc.vector.tensor_tensor(
                                hot2[:, b], iota_t, i2t[:, ts].unsqueeze(1).to_broadcast([P, NK, BT]), ALU.is_equal)
                            dve.wait_ge(S["hot_chain"], n + 1)
                            for c in range(3):
                                ins = nc.vector.tensor_tensor(
                                    hotg[:, b, c], hot1[:, b], gt[:, c, ts].unsqueeze(1).to_broadcast([P, HALF_J, BT]),
                                    ALU.mult)
                            ins.then_inc(S["onehot_rows"], 1)

                        def gate(i, b):
                            dve.wait_ge(S["gates_made"], half * BATCHES + i * 2 + b + 2 + 1)
                            w3 = w_view[:, :, bass.ds((i * 2 + b) * BT, BT)]
                            nc.vector.tensor_tensor(w3, bank(2 * b, 2).rearrange("p (t j) -> p j t", t=BT), w3,
                                                    ALU.mult).then_inc(S["w_gated"], 1)

                        with dve.Fori(0, BATCHES // 2) as i:
                            for b in range(2):
                                hot_rows(i, b)
                            for b in range(2):
                                gate(i, b)
                        with dve.Fori(0, GROUPS) as g:
                            for b in range(4):
                                j = g * 4 + b
                                dve.wait_ge(S["wj_hi_ready"], half * HALF_J + j + 1)
                                nc.vector.tensor_tensor(wj_lo[:, b % 2], arena[:, bass.ds(j * T, T)],
                                                        wj_hi[:, b % 2].bitcast(F32), ALU.subtract
                                                        ).then_inc(S["wj_lo_ready"], 1)
                                for k in range(4):
                                    unit_low(dve, U_A + half * U_HALF + U_AHALF + j * 4 + k, k, unit_src(b, k), SL)
                        dve.wait_ge(S["unit_used"], U_A + (half + 1) * U_HALF)
                        for tt in range(TT):
                            ins = nc.vector.tensor_tensor(x[:, tt], bank(4 * tt, 4), x[:, tt], ALU.add)
                        ins.then_inc(S["psum_clear"], 1)

                @block.tensor
                def _(pe):
                    pe.sem_inc(S["gelu_turned"], 2)
                    pe.sem_inc(S["gates_made"], 2)
                    turn_chunks(pe, 1, 0, [lambda tt, c=c: yn[:, tt, c * P:(c + 1) * P] for c in range(DC)])
                    pe.wait_ge(S["chunk_lo"], DC)
                    with pe.Fori(0, 4) as s:
                        outs = [ps[:, bass.ds(s * (2 * SL) + tt * SL, SL)] for tt in range(TT)]
                        slice_product(pe, s * DC, 0, outs, SL)
                    pe.wait_ge(S["q_out"], 4)
                    for i in range(8):
                        for k in range(4):
                            blk, tt = 2 * i + k // 2, k % 2
                            ins = nc.tensor.transpose(bank(i)[:, k * P:(k + 1) * P],
                                                      q_peer[:, tt, blk * NK:(blk + 1) * NK], ident)
                        ins.then_inc(S["qt_full"], 1)
                    pe.wait_ge(S["keys_in"], 16)
                    pe.wait_ge(S["qt_read"], 1)
                    for s in range(2):
                        ins = nc.tensor.transpose(bank(0)[:, s * NK:(s + 1) * NK],
                                                  keys_rows[:, 0, s], ident)
                    ins.then_inc(S["qt_full"], 1)
                    pe.wait_ge(S["qt_read"], 9)
                    for i in range(8):
                        tt = i // 4
                        for k in range(4):
                            blk = 4 * (i % 4) + k
                            ins = nc.tensor.matmul(bank(i)[:, k * NK:(k + 1) * NK],
                                                   q_peer_t[:, blk, tt * P:(tt + 1) * P],
                                                   keys_t[:, (blk % 2) * NK:(blk % 2 + 1) * NK],
                                                   start=True, stop=True)
                        ins.then_inc(S["score_full"], 1)
                    def turn_unit(half, i, k):
                        a = i * (2 * DC) + k
                        slot = (k // PU) % NP
                        if k % PU == 0:
                            piece_here(pe, slot, N_A + half * N_HALF + i * 8 + k // PU)
                        pe.wait_ge(S["lo_ready"], U_A + half * U_HALF + a - 1)
                        for jj in range(GJ):
                            ins = nc.tensor.transpose(bank(4 + k % 2)[:, jj * P:(jj + 1) * P],
                                                      u_block(slot, jj, k % PU), ident)
                        ins.then_inc(S["u_turned"], 1)

                    def u_block(slot, jj, c):
                        return piece[:, slot, jj * SL + c * P:jj * SL + (c + 1) * P]

                    def turn_gelu(g, par):
                        pe.wait_ge(S["gelu_done"], g_count(g) + 2 + 1)
                        pe.wait_ge(S["w_stored"], g_count(g) + 1)
                        for jj in range(GJ):
                            for tt in range(TT):
                                ins = nc.tensor.transpose(bank(6, 2)[:, jj * T + tt * P:jj * T + (tt + 1) * P],
                                                          ga[:, par, tt, jj * P:(jj + 1) * P], ident)
                        ins.then_inc(S["gelu_turned"], 1)

                    def step(half, i, k, tails, ahead=True):
                        g = (half, i * 2 + k // DC)
                        if ahead:
                            turn_unit(half, i + (k + 2) // (2 * DC), (k + 2) % (2 * DC))
                        par = k // DC
                        if k % DC == 0:
                            pe.wait_ge(S["gelu_done"], g_count(g) + 1)
                        unit_product(pe, U_A + half * U_HALF + i * (2 * DC) + k, k, ht_hi[:, k % DC],
                                     ht_lo[:, k % DC], [bank(2 * par + tt) for tt in range(TT)], SL,
                                     k % DC == 0, k % DC == DC - 1)
                        if tails and k % DC == 4:
                            turn_gelu((half, g[1] - 1), (par + 1) % 2)

                    def gates_step(half, i, b):
                        n = half * BATCHES + i * 2 + b
                        pe.wait_ge(S["onehot_rows"], n + 1)
                        pe.wait_ge(S["w_gated"], n - 1 + GATE0)
                        for t in range(BT):
                            for c in range(3):
                                ins = nc.tensor.matmul(bank(2 * b, 2)[:, t * HALF_J:(t + 1) * HALF_J],
                                                       hot2[:, b, :, t], hotg[:, b, c, :, t],
                                                       start=(c == 0), stop=(c == 2))
                        ins.then_inc(S["gates_made"], 1)

                    def v_steps(half, g, first, last):
                        for b in range(4):
                            j = g * 4 + b
                            pe.wait_ge(S["wj_lo_ready"], half * HALF_J + j + 1)
                            for k in range(4):
                                outs = [bank(4 * tt + k) for tt in range(TT)]
                                unit_product(pe, U_A + half * U_HALF + U_AHALF + j * 4 + k, k, wj_hi[:, b % 2],
                                             wj_lo[:, b % 2], outs, SL, first and b == 0, last and b == 3)

                    with pe.Fori(0, 2) as half:
                        pe.wait_ge(S["psum_clear"], half + 1)
                        turn_unit(half, 0, 0)
                        turn_unit(half, 0, 1)
                        for k in range(SHIFT):
                            step(half, 0, k, False)
                        with pe.Fori(0, PAIRS - 1) as i:
                            for k in range(SHIFT, 2 * DC + SHIFT):
                                step(half, i + k // (2 * DC), k % (2 * DC), True)
                        for k in range(SHIFT, 2 * DC):
                            step(half, PAIRS - 1, k, True, ahead=k < 2 * DC - 2)
                        turn_gelu((half, GROUPS - 1), 1)
                        pe.wait_ge(S["rows_ready"], half + 2)
                        for i, rows in enumerate((key_rows[0], key_rows[1], gates)):
                            for tt in range(TT):
                                ins = nc.tensor.transpose(bank(i)[:, tt * P:(tt + 1) * P],
                                                          rows[:, tt * HK:(tt + 1) * HK], ident)
                        ins.then_inc(S["small_full"], 1)
                        with pe.Fori(0, BATCHES // 2) as i:
                            pe.wait_ge(S["w_stored"], (half + 1) * GROUPS + 1)
                            for b in range(2):
                                gates_step(half, i, b)
                        pe.wait_ge(S["w_gated"], (half + 1) * BATCHES + GATE0)
                        v_steps(half, 0, True, False)
                        with pe.Fori(1, GROUPS - 1) as g:
                            v_steps(half, g, False, False)
                        v_steps(half, GROUPS - 1, False, True)

            nc.all_engine_barrier(sems_to_clear=cleared)

        with nc.Block() as block:
            gain = arena[:, 0:D]
            rows = arena[:, YN:YN + TT * D].rearrange("p (a d) -> p a d", a=TT)

            @block.sync
            def _(sp):
                sp.dma_start(gain, final_norm.rearrange("(o d) -> o d", o=1).to_broadcast([P, D])
                             ).then_inc(S["keys_in"], 16)
                o = out.rearrange("(a p) d -> p a d", p=P)
                for tt in range(TT):
                    sp.wait_ge(S["ranked"], tt + 1)
                    sp.dma_start(o[:, tt], rows[:, tt]).then_inc(S["stored"], 16)
                sp.wait_ge(S["stored"], 16 * TT)

            @block.scalar
            def _(act):
                squares(act, [(tt, x[:, tt], rows[:, tt]) for tt in range(TT)])
                roots(act, 1, 2)

            @block.vector
            def _(dve):
                chain = chainer(dve, S["chain_v"])
                means(dve, 1, [(0, 2, D)])
                dve.wait_ge(S["root_ready"], 1)
                dve.wait_ge(S["keys_in"], 16)
                chain(nc.vector.reciprocal(rstd[:, 0:2], ssq[:, 0:2]))
                for tt in range(TT):
                    nc.vector.scalar_tensor_tensor(rows[:, tt], x[:, tt], rstd[:, tt:tt + 1], gain,
                                                   ALU.mult, ALU.mult).then_inc(S["ranked"], 1)


def kernel(**inputs):
    import numpy as np
    import concourse.bacc as bacc
    from concourse.bass_utils import run_bass_kernel_spmd

    inv = (np.float32(10000.0) ** (-np.arange(0, ROPE, 2, dtype=np.float32) / np.float32(ROPE))).astype(np.float32)
    ang = np.arange(T, dtype=np.float32)[:, None] * inv[None, :]
    tables = [np.ascontiguousarray(f(ang).astype(np.float32).reshape(TT, P, ROPE // 2).transpose(1, 0, 2)).reshape(
        P, -1) for f in (np.cos, np.sin)]
    c = np.arange(P) % GRID_W
    c0 = np.clip(c - WIN_C // 2, 0, GRID_W - WIN_C)[:, None]
    kc = np.arange(GRID_W)[None, :]
    outside = np.where((kc >= c0) & (kc < c0 + WIN_C), 0.0, -1.0e30).astype(np.float32)
    consts = np.concatenate([np.eye(P, dtype=np.float32), *tables, outside,
                             np.broadcast_to(np.arange(TOPK, dtype=np.float32), (P, TOPK))], axis=1)

    order = ["x", "attn_norm", "ffn_norm", "mla_q_norm", "mla_kv_norm", "mla_out_norm", "nat_out_norm", "w_in",
             "mla_w_uq", "mla_w_ukv", "nat_rpb", "w_out", "peer_w_q", "peer_sub_keys", "peer_u", "peer_v",
             "final_norm"]
    nc = bacc.Bacc("TRN2", target_bir_lowering=False, num_devices=1)
    arrays, ap = {}, {}
    for name in order:
        a = np.ascontiguousarray(inputs[name])
        if name == "x":
            a = a.reshape(T, D)
        arrays["in_" + name] = a
        ap[name] = nc.dram_tensor("in_" + name, a.shape, mybir.dt.from_np(a.dtype), kind="ExternalInput").ap()
    arrays["in_consts"] = np.ascontiguousarray(consts)
    consts_ap = nc.dram_tensor("in_consts", consts.shape, F32, kind="ExternalInput").ap()
    out = nc.dram_tensor("out_0", (T, D), F32, kind="ExternalOutput").ap()
    gains = dict(attn=ap["attn_norm"], ffn=ap["ffn_norm"], q=ap["mla_q_norm"], kv=ap["mla_kv_norm"],
                 mla=ap["mla_out_norm"], nat=ap["nat_out_norm"])
    build(nc, ap["x"], gains, ap["w_in"], ap["mla_w_uq"], ap["mla_w_ukv"], ap["nat_rpb"], ap["w_out"],
          ap["peer_w_q"], ap["peer_sub_keys"], ap["peer_u"], ap["peer_v"], ap["final_norm"], consts_ap, out)
    r = run_bass_kernel_spmd(nc, [arrays], core_ids=[0])
    return r.results[0]["out_0"].reshape(1, T, D)
```

```python
from contextlib import ExitStack, contextmanager

import concourse.bass as bass
from concourse import mybir

F32 = mybir.dt.float32
F32R = mybir.dt.float32r
BF16 = mybir.dt.bfloat16
U32 = mybir.dt.uint32
ACT = mybir.ActivationFunctionType
ALU = mybir.AluOpType
AX = mybir.AxisListType

P = 128
L, D, T = 2, 2048, 256
TT = T // P
DC = D // P
SL = 512
Q_LORA, KV_LORA, ROPE = 512, 256, 64
MH, NOPE, MV = 8, 128, 128
NH, ND = 16, 64
W_MIX = 1024
D_IN = 3904
NAT0 = Q_LORA + KV_LORA + ROPE
GRID_W, WIN_R, WIN_C, ROWS = 64, 8, 16, 4
NDR = 6
DR_ALL = 2 * WIN_R - 1
DC_ALL = 2 * WIN_C - 1
PH, NK, TOPK = 8, 128, 16
HK = PH * TOPK
HALF_J = NK // 2
EPS = 1e-6
NEG = -3.0e38
NP = 4
PU = 4
R = 4
GC = dict(attn=0, ffn=16, q=32, kv=36, mla=38, nat=46)
NG = 54

ARENA = HALF_J * T
GJ, BT, SHIFT = 4, 16, 8
GROUPS, PAIRS, BATCHES = HALF_J // GJ, HALF_J // GJ // 2, T // BT
N_A, N_HALF = 16, 2 * HALF_J
U_A, U_HALF, U_AHALF = 4 * DC, 2 * GROUPS * DC, GROUPS * DC
GATE0 = 2
VL = 4
U_POOL = U_AHALF // VL * (VL - 1)
YN = 8192
REST = 12288
STAGE = 7168


def build(nc, x_in, gains, w_in, w_uq, w_ukv, rpb, w_out, w_q, keys, u_tab, v_tab, final_norm, consts, out):
    ctx = ExitStack()
    with ctx:
        def sb(name, shape, dt=F32):
            return ctx.enter_context(nc.sbuf_tensor(name, shape, dt))

        x = sb("x", [P, TT, D])
        arena = sb("arena", [P, ARENA])
        stage = sb("stage", [P, STAGE])
        ht_hi = sb("ht_hi", [P, DC, T], F32R)
        ht_lo = sb("ht_lo", [P, DC, T], F32R)
        unit_hi = sb("unit_hi", [P, R, SL], F32R)
        unit_lo = sb("unit_lo", [P, R, SL], F32R)
        piece = sb("piece", [P, NP, PU * SL])
        wj_hi = sb("wj_hi", [P, 2, T], F32R)
        wj_lo = sb("wj_lo", [P, 2, T], F32R)
        ga = sb("ga", [P, 2, TT, SL])
        con = sb("con", [P, 128 + 128 + 64 + 16])
        iota = sb("iota", [P, NK], BF16)
        grow = stage[:, 0:P]
        gall = sb("gall", [P, L * NG])
        gcol = sb("gcol", [P, NG])
        i1t = sb("i1t", [P, T], BF16)
        i2t = sb("i2t", [P, T], BF16)
        gt = sb("gt", [P, 3, T], BF16)
        ssq = sb("ssq", [P, 4])
        rms = sb("rms", [P, 4])
        rstd = sb("rstd", [P, 4])
        mx = sb("mx", [P, 2, 4])
        den = sb("den", [P, 2, 4])
        rden = sb("rden", [P, 2, 4])
        smax = sb("smax", [P, 2, 4])
        per_round = sb("per_round", [P, 2 * TT * PH])
        ident = con[:, 0:128]
        cos = con[:, 128:192].rearrange("p (a f) -> p a f", a=TT)
        sin = con[:, 192:256].rearrange("p (a f) -> p a f", a=TT)
        mask = con[:, 256:320]
        iota16 = con[:, 320:336]
        ps = ctx.enter_context(nc.psum_tensor("ps", [P, 8 * SL], F32))

        rpb_pad = nc.dram_tensor("rpb_pad", (L * NH * DR_ALL, P), F32).ap()
        skewed = nc.dram_tensor("skewed", (NH, NDR + 1, GRID_W, P - 1), F32).ap()

        names = [f"arrived{s}" for s in range(NP)] + """hi_ready lo_ready unit_used squared mean_ready root_ready
            rows_ready chunk_turned chunk_hi chunk_lo chain_v chain_a bank_full bank_read scored maxed expd probs_turned
            probs_read mixed attended layer_in bias_in keys_in ranked gates_exp slice_out nat_turned rope_ready heads_turned
            u_turned gelu_done gelu_turned w_stored onehot_rows gates_made w_gated wj_hi_ready wj_lo_ready
            hot_chain rank_chain psum_clear bias_skewed stored q_out qt_full qt_read score_full score_read small_full small_read x_added bias_masked pool_lo_ready inverse_ready rows_ready_2""".split()
        S = {n: ctx.enter_context(nc.semaphore(n)) for n in names}
        setup_in = ctx.enter_context(nc.semaphore("setup_in"))
        setup_c = ctx.enter_context(nc.semaphore("setup_c"))
        pad_ready = ctx.enter_context(nc.semaphore("pad_ready"))
        bias_made = ctx.enter_context(nc.semaphore("bias_made"))
        nums = sorted(s.num for s in S.values())
        assert nums[-1] - nums[0] == len(nums) - 1
        cleared = range(nums[0], nums[-1] + 1)

        def bank(b, n=1):
            return ps[:, b * SL:(b + n) * SL]

        def rounds(slot, n):
            return (n - slot) * (16 // NP) + 16

        def piece_here(eng, slot, n, parts=1):
            eng.wait_ge(S[f"arrived{slot}"], parts * rounds(slot, n))

        def unit_high(act, u, k, src, w, wait=True):
            if wait:
                act.wait_ge(S["unit_used"], u - R + 1)
            nc.scalar.activation(unit_hi[:, k % R, 0:w], src, ACT.Copy).then_inc(S["hi_ready"], 1)

        def unit_low(dve, u, k, src, w):
            dve.wait_ge(S["hi_ready"], u + 1)
            nc.vector.tensor_tensor(unit_lo[:, k % R, 0:w], src, unit_hi[:, k % R, 0:w].bitcast(F32),
                                    ALU.subtract).then_inc(S["lo_ready"], 1)

        def unit_product(pe, u, k, hi, lo, outs, w, start, stop):
            pe.wait_ge(S["lo_ready"], u + 1)
            last = None
            for tt in range(TT):
                a, b = hi[:, tt * P:(tt + 1) * P], lo[:, tt * P:(tt + 1) * P]
                nc.tensor.matmul(outs[tt], a, unit_hi[:, k % R, 0:w], start=start, stop=False)
                nc.tensor.matmul(outs[tt], a, unit_lo[:, k % R, 0:w], start=False, stop=False)
                last = nc.tensor.matmul(outs[tt], b, unit_hi[:, k % R, 0:w], start=False, stop=stop)
            last.then_inc(S["unit_used"], 1)

        def unit_src(n, k, w=SL):
            return piece[:, n % NP, k * w:(k + 1) * w]

        def slice_high(act, u0, n0, k0, m0, w, wait=True, parts=1):
            for k in range(DC):
                if k % PU == 0:
                    piece_here(act, (m0 + k // PU) % NP, n0 + k // PU, parts)
                unit_high(act, u0 + k, k0 + k, unit_src(m0 + k // PU, k % PU, w), w, wait or k >= R)

        def slice_low(dve, u0, k0, m0, w):
            for k in range(DC):
                unit_low(dve, u0 + k, k0 + k, unit_src(m0 + k // PU, k % PU, w), w)

        def slice_product(pe, u0, k0, outs, w):
            for k in range(DC):
                unit_product(pe, u0 + k, k0 + k, ht_hi[:, k], ht_lo[:, k], outs, w, k == 0, k == DC - 1)

        def squares(act, parts, wait=None):
            if wait:
                act.wait_ge(*wait)
            for i, (c, rows, junk) in enumerate(parts):
                ins = nc.scalar.activation(junk, rows, ACT.Square, accum_out=ssq[:, c:c + 1])
            ins.then_inc(S["squared"], 1)

        def means(dve, n, parts):
            dve.wait_ge(S["squared"], n)
            for c0, c1, width in parts:
                ins = nc.vector.tensor_scalar(rms[:, c0:c1], ssq[:, c0:c1], 1.0 / width, EPS, ALU.mult, ALU.add)
            ins.then_inc(S["mean_ready"], 1)

        def roots(act, n, cols):
            act.wait_ge(S["mean_ready"], n)
            nc.scalar.activation(ssq[:, 0:cols], rms[:, 0:cols], ACT.Sqrt).then_inc(S["root_ready"], 1)

        def scale_first(dve, n, cols, groups, chain):
            dve.wait_ge(S["root_ready"], n)
            chain(nc.vector.reciprocal(rstd[:, 0:cols], ssq[:, 0:cols]))
            dve.sem_inc(S["inverse_ready"], 1)
            for c, dst, src in groups:
                nc.vector.tensor_scalar(dst(0), src(0), rstd[:, c:c + 1], None, ALU.mult).then_inc(S["rows_ready"], 1)

        def scale_second(act, n, groups):
            act.wait_ge(S["inverse_ready"], n)
            for c, dst, src in groups:
                nc.scalar.activation(dst(1), src(1), ACT.Copy, scale=rstd[:, c + 1:c + 2]
                                     ).then_inc(S["rows_ready_2"], 1)

        def turn_chunks(pe, groups_before, c0, chunks):
            for i, src in enumerate(chunks):
                c = c0 + i
                if i % 4 == 0:
                    pe.wait_ge(S["rows_ready"], groups_before + i // 4 + 1)
                    pe.wait_ge(S["rows_ready_2"], groups_before + i // 4 + 1)
                if c >= 4:
                    pe.wait_ge(S["chunk_lo"], c - 3)
                for tt in range(TT):
                    ins = nc.tensor.transpose(bank(4 + c % 4)[:, tt * P:(tt + 1) * P], src(tt), ident)
                ins.then_inc(S["chunk_turned"], 1)

        def chunks_high(act, c0, count, gain0):
            for i in range(count):
                c = c0 + i
                act.wait_ge(S["chunk_turned"], c + 1)
                nc.scalar.activation(ht_hi[:, i], bank(4 + c % 4)[:, 0:T], ACT.Copy,
                                     scale=gcol[:, gain0(i):gain0(i) + 1]).then_inc(S["chunk_hi"], 1)

        def chunks_low(dve, c0, count, gain0):
            for i in range(count):
                c = c0 + i
                dve.wait_ge(S["chunk_hi"], c + 1)
                nc.vector.scalar_tensor_tensor(ht_lo[:, i], bank(4 + c % 4)[:, 0:T], gcol[:, gain0(i):gain0(i) + 1],
                                               ht_hi[:, i].bitcast(F32), ALU.mult, ALU.subtract
                                               ).then_inc(S["chunk_lo"], 1)

        def quarter(rows, q):
            return lambda tt: rows[:, tt, q * SL:(q + 1) * SL]

        def chainer(eng, sem):
            count = [0]

            def chain(ins):
                count[0] += 1
                ins.then_inc(sem, 1)
                eng.wait_ge(sem, count[0])
            return chain

        with nc.Block() as block:
            @block.sync
            def _(sp):
                sp.dma_start(con[:, :], consts).then_inc(setup_in, 16)
                for l in range(L):
                    for name in GC:
                        r0 = l * NG + GC[name]
                        if name == "ffn":
                            src = gains[name][l].rearrange("(q a b r) -> q b a r", q=4, a=4, b=4)
                            for q in range(4):
                                sp.dma_start(grow[r0 + 4 * q:r0 + 4 * q + 4, :].rearrange("b (a r) -> b a r", a=4),
                                             src[q]).then_inc(setup_in, 16)
                            continue
                        src = gains[name][l].rearrange("(c p) -> c p", p=P)
                        sp.dma_start(grow[r0:r0 + src.shape[0], :], src).then_inc(setup_in, 16)

            @block.gpsimd
            def _(pool):
                nc.gpsimd.iota(iota[:, :], [[1, NK]], base=0, channel_multiplier=0,
                               allow_small_or_imprecise_dtypes=True)
                zeros = arena[0:120, 0:512]
                nc.gpsimd.memset(zeros, 0.0).then_inc(pad_ready, 1)

            @block.scalar
            def _(act):
                act.dma_start(x[:, :, :], x_in.rearrange("(a p) d -> p a d", p=P)).then_inc(setup_in, 16)
                act.wait_ge(pad_ready, 1)
                pad = rpb_pad.rearrange("(p a) m -> p a m", p=120)
                act.dma_start(pad, arena[0:120, 0:512].rearrange("p (a m) -> p a m", m=P)).then_inc(bias_made, 16)
                act.wait_ge(bias_made, 16)
                m0 = GRID_W - WIN_C
                act.dma_start(rpb_pad[:, m0:m0 + DC_ALL], rpb.rearrange("l h r c -> (l h r) c")).then_inc(bias_made, 16)

            @block.tensor
            def _(pe):
                pe.wait_ge(setup_in, 16 * (2 + L * (len(GC) + 3)))
                nc.tensor.transpose(bank(0)[:, 0:L * NG], grow[0:L * NG, :], ident[0:L * NG, 0:L * NG]
                                    ).then_inc(setup_c, 1)

            @block.vector
            def _(dve):
                dve.wait_ge(setup_c, 1)
                nc.vector.tensor_copy(gall[:, :], bank(0)[:, 0:L * NG])

        proj = arena[:, 0:YN].rearrange("p (s a n) -> p s a n", s=8, a=TT)
        ckv = proj[:, 0, :, 0:KV_LORA]
        kpe = proj[:, 0, :, KV_LORA:KV_LORA + ROPE]
        cq = proj[:, 1]
        yn = arena[:, YN:YN + TT * D].rearrange("p (a d) -> p a d", a=TT)
        nqt = arena[:, YN:YN + 2048].rearrange("p (h t) -> p h t", h=8)
        nkt = arena[:, YN + 2048:YN + 4096].rearrange("p (h t) -> p h t", h=8)
        sbuf_s = arena[:, REST:REST + 2048].rearrange("p (b h k) -> p b h k", b=2, h=4)
        sbuf_p = arena[:, REST + 2048:REST + 4096].rearrange("p (b h c q) -> p b h c q", b=2, h=4, c=2)
        nat_o = arena[:, 2048:4096].rearrange("p (a n) -> p a n", a=TT)
        bias = stage[:, 0:NH * NDR * GRID_W].rearrange("p (h m) -> p h m", h=NH)
        bias_rows = stage[:, 0:NH * NDR * GRID_W].rearrange("p (h r k) -> p h r k", h=NH, r=NDR)
        cqn = arena[:, 4096:5120].rearrange("p (a n) -> p a n", a=TT)
        ckvn = arena[:, 5120:5632].rearrange("p (a n) -> p a n", a=TT)
        q_mla = arena[:, YN:YN + 3072].rearrange("p (a n) -> p a n", a=TT)
        kv_mla = arena[:, 4096:8192].rearrange("p (a n) -> p a n", a=TT)
        qpe = arena[:, YN + 3072:YN + 4096].rearrange("p (a h f) -> p a h f", a=TT, h=MH)
        mla_o = arena[:, YN:YN + 2048].rearrange("p (a n) -> p a n", a=TT)
        qnt = stage[:, 0:2048].rearrange("p (h t) -> p h t", h=MH)
        qpt = stage[:, 2048:3072].rearrange("p (h t) -> p h t", h=4)
        knt = stage[:, 3072:5120].rearrange("p (h t) -> p h t", h=MH)
        kpt = stage[:, 5120:5376]
        kpr = stage[:, 5376:5632].rearrange("p (a b f) -> p a b f", a=TT, b=2)
        rt1 = stage[:, 5632:6144].rearrange("p (a h f) -> p a h f", a=TT, h=MH)
        rt2 = stage[:, 6144:6656].rearrange("p (a h f) -> p a h f", a=TT, h=MH)

        SCALE = float(NOPE + ROPE) ** -0.5
        NB = 8
        MB = 4
        U_UQ, U_UKV, U_OUT = 8 * DC, 8 * DC + 12, 8 * DC + 20
        N_UQ, N_UKV, N_OUT = 32, 35, 37

        QH, KVH = NOPE + ROPE, NOPE + MV

        def k_head(h, tt):
            return kv_mla[:, tt, h * KVH:h * KVH + NOPE]

        def v_head(h, tt):
            return kv_mla[:, tt, h * KVH + NOPE:(h + 1) * KVH]

        norm_x = [(0, quarter(yn, q), quarter(x, q)) for q in range(4)]
        norm_latents = [(0, lambda tt: cqn[:, tt], lambda tt: cq[:, tt]),
                        (2, lambda tt: ckvn[:, tt], lambda tt: ckv[:, tt])]
        norm_mixed = [(c, quarter(rows, q), quarter(rows, q)) for c, rows in ((0, mla_o), (2, nat_o))
                      for q in range(2)]
        norm_ffn = [(0, lambda tt, q=q: yn[:, tt, q * SL:(q + 1) * SL].rearrange("p (b a r) -> p b a r", a=4, b=4),
                     lambda tt, q=q: x[:, tt, q * SL:(q + 1) * SL].rearrange("p (a b r) -> p b a r", a=4, b=4))
                    for q in range(4)]

        q_peer = arena[:, 0:TT * D].rearrange("p (a n) -> p a n", a=TT)
        q_peer_t = arena[:, 4096:8192].rearrange("p (b t) -> p b t", t=T)
        w_view = arena[:, :].rearrange("p (j t) -> p j t", t=T)
        score_rows = stage[:, 0:4096]
        scores = score_rows.rearrange("p (a b n) -> p a b n", a=TT, b=2 * PH)
        keys_rows = stage[:, 5888:6144].rearrange("p (l s d) -> p l s d", l=1, s=2)
        keys_t = stage[:, 4096:4352]
        work, cand, pick = (stage[:, c:c + 512].rearrange("p (a n) -> p a n", a=2) for c in (4096, 4608, 5120))
        pick = pick.rearrange("p a (k j) -> p a k j", k=TOPK)
        small = stage[:, 5632:5888]
        key_rows = [stage[:, 6144:6400], stage[:, 6400:6656]]
        gate_rows, gates = stage[:, 6656:6912], stage[:, 6912:7168]
        top_v = small[:, 0:32].rearrange("p (a k) -> p a k", a=2)
        top_i = small[:, 32:64].bitcast(U32).rearrange("p (a k) -> p a k", a=2)
        top_if = small[:, 64:96].rearrange("p (a k) -> p a k", a=2)
        best_v = small[:, 96:112]
        best_p = small[:, 112:128].bitcast(U32)
        pos_i = small[:, 128:160].bitcast(U32).rearrange("p (a k) -> p a k", a=2)
        pos_f = small[:, 160:192].rearrange("p (a k) -> p a k", a=2)
        gmax, gsum = per_round[:, 0:TT * PH], per_round[:, TT * PH:2 * TT * PH]
        hot2 = stage[:, 0:2048].bitcast(BF16).rearrange("p (b k t) -> p b k t", b=2, t=BT)
        hotg = stage[:, 2048:5120].bitcast(BF16).rearrange("p (b c k t) -> p b c k t", b=2, c=3, t=BT)
        iota_t = stage[:, 5120:6144].bitcast(BF16).rearrange("p (k t) -> p k t", t=BT)
        rest = ga[:, 1, 0].rearrange("p (a t) -> p a t", a=2)
        hot1 = stage[:, 6144:7168].bitcast(BF16).rearrange("p (b k t) -> p b k t", b=2, t=BT)

        def u_src(k):
            return piece[:, k // PU].rearrange("p (e b r) -> p b e r", e=GJ * 4, b=4)[:, k % PU]

        def pool_count(half, g, k):
            return half * U_POOL + g * (DC // VL * (VL - 1)) + k // VL * (VL - 1) + k % VL

        def u_view(unit):
            return unit.rearrange("p (e r) -> p e r", r=32)

        def g_count(g):
            return g[0] * GROUPS + g[1]

        def g_units(g):
            return g[0] * U_HALF + g[1] * DC

        def latent_src(s, k):
            if s < 3:
                return unit_src(N_UQ + s, k)
            c = k * 2 * SL + ((s - 3) % 2) * SL
            return piece[:, (N_UKV + (s - 3) // 2) % NP, c:c + SL]

        def heads_dst(i):
            if i < 4:
                return qnt[:, 2 * i:2 * i + 2].rearrange("p h t -> p (h t)"), SL
            if i < 8:
                return knt[:, 2 * (i - 4):2 * (i - 4) + 2].rearrange("p h t -> p (h t)"), SL
            if i < 10:
                return qpt[:, 2 * (i - 8):2 * (i - 8) + 2].rearrange("p h t -> p (h t)"), SL
            return kpt, T

        def score_at(b, h):
            c = 2 * (h % 2) + h // 2
            return bank(2 * (b % 2), 2)[:, c * T:(c + 1) * T]

        def attention_act(act, b0, count, mla):
            def probs(b):
                if b >= b0 + 2:
                    act.wait_ge(S["probs_turned"], b - 1)
                act.wait_ge(S["maxed"], b + 1)
                for h in range(4):
                    src = score_at(b, h) if mla else sbuf_s[:, b % 2, h]
                    ins = nc.scalar.activation(sbuf_s[:, b % 2, h], src, ACT.Exp,
                                               bias=mx[:, b % 2, h:h + 1], scale=SCALE if mla else 1.0,
                                               accum_out=den[:, b % 2, h:h + 1])
                ins.then_inc(S["expd"], 1)

            def turned(b):
                act.wait_ge(S["probs_turned"], b + 1)
                if b >= b0 + 2:
                    act.wait_ge(S["mixed"], b - 1)
                nc.scalar.activation(sbuf_p[:, b % 2].rearrange("p h c q -> p (h c q)"), bank(4, 2),
                                     ACT.Copy).then_inc(S["probs_read"], 1)

            for b in range(b0, b0 + count + 1):
                if b < b0 + count:
                    probs(b)
                if b > b0:
                    turned(b - 1)

        def attention_dve(dve, b0, count, mla, chain):
            def maxima(b):
                dve.wait_ge(S["scored"], b + 1)
                i = b - b0
                sc = bank(2 * (b % 2), 2).rearrange("p (o e k) -> p e o k", o=2, e=2)
                if not mla:
                    if b >= b0 + 2:
                        dve.wait_ge(S["probs_turned"], b - 1)
                    tt, h0 = i // 4, 4 * (i % 4)
                    r0 = (2 - 2 * tt) * GRID_W
                    for o in range(2):
                        ins = nc.vector.scalar_tensor_tensor(
                            sbuf_s[:, b % 2, o::2], bank(2 * (b % 2) + o).rearrange("p (e k) -> p e k", e=2),
                            float(ND) ** -0.5, bias[:, h0 + o:h0 + 4:2, r0:r0 + T], ALU.mult, ALU.add)
                    chain(ins)
                    chain(nc.vector.tensor_reduce(smax[:, b % 2, :], sbuf_s[:, b % 2], AX.X, ALU.max))
                else:
                    chain(nc.vector.tensor_reduce(smax[:, b % 2, :].rearrange("p (e o) -> p e o", o=2), sc, AX.X,
                                                  ALU.max))
                nc.vector.tensor_scalar(mx[:, b % 2, :], smax[:, b % 2, :], -(SCALE if mla else 1.0), None,
                                        ALU.mult).then_inc(S["maxed"], 1)

            def normalise(b):
                dve.wait_ge(S["mixed"], b + 1)
                i = b - b0
                w = MV if mla else ND
                tt, h0 = (i // 2, 4 * (i % 2)) if mla else (i // 4, 4 * (i % 4))
                dst = (mla_o if mla else nat_o)[:, tt, h0 * w:(h0 + 4) * w].rearrange("p (h d) -> p h d", h=4)
                nc.vector.tensor_tensor(dst, bank(6 + b % 2)[:, 0:4 * w].rearrange("p (h d) -> p h d", h=4),
                                        rden[:, b % 2, :].unsqueeze(2).to_broadcast([P, 4, w]),
                                        ALU.mult).then_inc(S["attended"], 1)

            for b in range(b0, b0 + count + 2):
                if b >= b0 + 2:
                    dve.wait_ge(S["expd"], b - 1)
                    chain(nc.vector.reciprocal(rden[:, b % 2, :], den[:, b % 2, :]))
                if b < b0 + count:
                    maxima(b)
                if b >= b0 + 2:
                    normalise(b - 2)

        def attention_pe(pe, b0, count, scores, v_of, w, mla):
            for b in range(b0, b0 + count + 2):
                if b < b0 + count:
                    if b >= b0 + 2:
                        pe.wait_ge(S["expd" if mla else "maxed"], b - 1)
                    outs = [score_at(b, h) for h in range(4)]
                    scores(b - b0, outs).then_inc(S["scored"], 1)
                if b0 + 1 <= b <= b0 + count:
                    a = b - 1
                    pe.wait_ge(S["expd"], a + 1)
                    if a > b0:
                        pe.wait_ge(S["probs_read"], a)
                    for h in range(4):
                        for c in range(2):
                            ins = nc.tensor.transpose(bank(4, 2)[:, (2 * h + c) * P:(2 * h + c + 1) * P],
                                                      sbuf_s[:, a % 2, h, c * P:(c + 1) * P], ident)
                    ins.then_inc(S["probs_turned"], 1)
                if b >= b0 + 2:
                    a = b - 2
                    pe.wait_ge(S["probs_read"], a + 1)
                    if a >= b0 + 2:
                        pe.wait_ge(S["attended"], a - 1)
                    for h in range(4):
                        for c in range(2):
                            ins = nc.tensor.matmul(bank(6 + a % 2)[:, h * w:(h + 1) * w],
                                                   sbuf_p[:, a % 2, h, c], v_of(a - b0, h, c),
                                                   start=(c == 0), stop=(c == 1))
                    ins.then_inc(S["mixed"], 1)

        with nc.Fori(0, L) as layer:
            with nc.Block() as block:
                @block.sync
                def _(sp):
                    wl = w_in.rearrange("l (c p) n -> p l c n", p=P)

                    def w_piece(n, slot, q, col, w, wait=True):
                        dst = piece[:, slot, 0:PU * w].rearrange("p (l c n) -> p l c n", l=1, c=PU)
                        if wait:
                            sp.wait_ge(S["lo_ready"], PU * (n - NP + 1))
                        sp.dma_start(dst, wl[:, bass.ds(layer, 1), q * PU:(q + 1) * PU, col]).then_inc(S[f"arrived{slot}"], 16)

                    for q in range(4):
                        w_piece(q, q, q, slice(Q_LORA, NAT0), NAT0 - Q_LORA, wait=False)
                    for q in range(4):
                        w_piece(4 + q, q, q, slice(0, Q_LORA), SL)
                    pad_rows = rpb_pad.rearrange("(l h r) m -> l h r m", h=NH, r=DR_ALL)
                    sp.wait_ge(bias_made, 16 * 2)

                    def skew(r):
                        src = pad_rows[bass.ds(layer, 1), :, bass.ds(r + WIN_R - ROWS, 1), 0:P - 1].rearrange(
                            "l h r m -> (l h) r m").to_broadcast([NH, GRID_W, P - 1])
                        dst = skewed[:, bass.ds(r, 1)].rearrange("h r c m -> h (r c) m")
                        sp.dma_start(dst, src).then_inc(S["bias_skewed"], 16)

                    def nat_pieces(s):
                        for q in range(4):
                            w_piece(8 + s * 4 + q, q, q, bass.ds(NAT0 + s * SL, SL), SL)

                    row = GRID_W * (P - 1)

                    def bias_part(par):
                        for r in range(NDR):
                            src = bass.AP(skewed.tensor, (r + 1 - par) * row + GRID_W - 1,
                                          [[P - 2, GRID_W], [(NDR + 1) * row, NH], [1, GRID_W]])
                            sp.dma_start(bias_rows[par * GRID_W:(par + 1) * GRID_W, :, r], src
                                         ).then_inc(S["bias_in"], 16)

                    with sp.Fori(0, 3) as s:
                        nat_pieces(s)
                        skew(2 * s)
                        skew(2 * s + 1)
                    skew(NDR)
                    nat_pieces(3)
                    sp.wait_ge(S["bias_skewed"], 16 * (NDR + 1))
                    bias_part(0)
                    nat_pieces(4)
                    bias_part(1)
                    nat_pieces(5)
                    uq = w_uq.rearrange("l (c p) n -> p l c n", p=P)
                    for s in range(3):
                        n = N_UQ + s
                        sp.wait_ge(S["lo_ready"], PU * (n - NP + 1))
                        sp.dma_start(piece[:, n % NP, :].rearrange("p (l c n) -> p l c n", l=1, c=4),
                                     uq[:, bass.ds(layer, 1), :, s * SL:(s + 1) * SL]).then_inc(S[f"arrived{n % NP}"], 16)
                    ukv = w_ukv.rearrange("l (c p) n -> p l c n", p=P)
                    for s in range(2):
                        n = N_UKV + s
                        sp.wait_ge(S["lo_ready"], PU * (n - NP + 1))
                        sp.dma_start(piece[:, n % NP, :].rearrange("p (l c n) -> p l c n", l=1, c=2),
                                     ukv[:, bass.ds(layer, 1), :, s * 1024:(s + 1) * 1024]).then_inc(S[f"arrived{n % NP}"], 16)
                    wo = w_out.rearrange("l (c p) n -> p l c n", p=P)
                    with sp.Fori(0, 4) as s:
                        for q in range(4):
                            slot = (N_OUT + q) % NP
                            sp.wait_ge(S["lo_ready"], PU * (N_OUT + s * 4 + q - NP + 1))
                            sp.dma_start(piece[:, slot, :].rearrange("p (l c n) -> p l c n", l=1, c=PU),
                                         wo[:, bass.ds(layer, 1), q * PU:(q + 1) * PU, bass.ds(s * SL, SL)]
                                         ).then_inc(S[f"arrived{slot}"], 16)

                @block.gpsimd
                def _(pool):
                    pool.wait_ge(S["bias_in"], 16 * 2 * NDR)
                    b3 = stage[:, 0:NH * NDR * GRID_W].rearrange("p (m k) -> p m k", k=GRID_W)
                    nc.gpsimd.tensor_tensor(b3, b3, mask.unsqueeze(1).to_broadcast([P, NH * NDR, GRID_W]), ALU.add
                                            ).then_inc(S["bias_masked"], 1)

                @block.scalar
                def _(act):
                    chain = chainer(act, S["chain_a"])
                    squares(act, [(tt, x[:, tt], yn[:, tt]) for tt in range(TT)])
                    roots(act, 1, 2)
                    scale_second(act, 1, norm_x)
                    chunks_high(act, 0, DC, lambda i: GC["attn"] + i)
                    slice_high(act, 0, 0, 0, 0, NAT0 - Q_LORA, wait=False)
                    slice_high(act, DC, 4, 0, 0, SL)

                    def evacuate(s, first, w=SL):
                        act.wait_ge(S["unit_used"], (s + 1) * DC)
                        dst = proj[:, s] if isinstance(s, int) else arena[:, bass.ds(s * 1024, 1024)].rearrange(
                            "p (a n) -> p a n", a=TT)
                        nc.scalar.activation(dst[:, :, 0:w], bank(2 * first, 2).rearrange(
                            "p (a n) -> p a n", a=TT)[:, :, 0:w], ACT.Copy).then_inc(S["slice_out"], 1)

                    evacuate(0, 0, NAT0 - Q_LORA)
                    with act.Fori(0, 3) as i:
                        for b in range(2):
                            s = 2 + i * 2 + b
                            for k in range(DC):
                                if k % PU == 0:
                                    piece_here(act, k // PU, 4 * s + k // PU)
                                unit_high(act, s * DC + k, k, unit_src(k // PU, k % PU), SL)
                                if k == 2:
                                    evacuate(s - 1, 1 - b)
                    evacuate(7, 1)
                    for i in range(8):
                        act.wait_ge(S["bank_full"], i + 1)
                        dst = (nqt if i < 4 else nkt)[:, 2 * (i % 4):2 * (i % 4) + 2].rearrange("p h t -> p (h t)")
                        nc.scalar.activation(dst, bank(4 + i % 4), ACT.Copy).then_inc(S["bank_read"], 1)
                    attention_act(act, 0, NB, False)
                    squares(act, [(tt, cq[:, tt], cqn[:, tt]) for tt in range(TT)]
                            + [(2 + tt, ckv[:, tt], ckvn[:, tt]) for tt in range(TT)])
                    roots(act, 2, 4)
                    scale_second(act, 2, norm_latents)
                    chunks_high(act, DC, 6, lambda i: GC["q"] + i)
                    def latent_out(s):
                        act.wait_ge(S["unit_used"], U_UQ + 4 * (s + 1) if s < 3 else U_UKV + 2 * (s - 2))
                        dst = q_mla[:, :, s * SL:(s + 1) * SL] if s < 3 else kv_mla[:, :, (s - 3) * SL:(s - 2) * SL]
                        nc.scalar.activation(dst, bank(2 * (s % 4), 2).rearrange("p (a n) -> p a n", a=TT),
                                             ACT.Copy).then_inc(S["slice_out"], 1)

                    for s in range(7):
                        n = N_UQ + s if s < 3 else N_UKV + (s - 3) // 2
                        if s < 3 or s % 2 == 1:
                            piece_here(act, n % NP, n)
                        for k in range(4 if s < 3 else 2):
                            u = U_UQ + 4 * s + k if s < 3 else U_UKV + 2 * (s - 3) + k
                            unit_high(act, u, u, latent_src(s, k), SL)
                        if s >= 1:
                            latent_out(s - 1)
                    latent_out(6)
                    for i in range(11):
                        act.wait_ge(S["bank_full"], 8 + i + 1)
                        dst, w = heads_dst(i)
                        nc.scalar.activation(dst, bank(4 + i % 4)[:, 0:w], ACT.Copy).then_inc(S["bank_read"], 1)
                    attention_act(act, NB, MB, True)
                    act.wait_ge(S["attended"], NB + MB)
                    squares(act, [(tt, mla_o[:, tt], kv_mla[:, 0, tt * W_MIX:(tt + 1) * W_MIX]) for tt in range(TT)]
                            + [(2 + tt, nat_o[:, tt], kv_mla[:, 1, tt * W_MIX:(tt + 1) * W_MIX])
                               for tt in range(TT)])
                    roots(act, 3, 4)
                    scale_second(act, 3, norm_mixed)
                    chunks_high(act, DC + 6, DC, lambda i: GC["mla"] + i)
                    with act.Fori(0, 4) as s:
                        for k in range(DC):
                            if k % PU == 0:
                                piece_here(act, (N_OUT + k // PU) % NP, N_OUT + 4 * s + k // PU)
                            unit_high(act, U_OUT + s * DC + k, U_OUT + k, unit_src(N_OUT + k // PU, k % PU), SL)

                @block.vector
                def _(dve):
                    chain = chainer(dve, S["chain_v"])
                    chain(nc.vector.tensor_copy(gcol[:, :], gall[:, bass.ds(layer * NG, NG)]))
                    means(dve, 1, [(0, 2, D)])
                    scale_first(dve, 1, 2, norm_x, chain)
                    chunks_low(dve, 0, DC, lambda i: GC["attn"] + i)
                    slice_low(dve, 0, 0, 0, NAT0 - Q_LORA)
                    slice_low(dve, DC, 0, 0, SL)
                    with dve.Fori(0, 6) as s:
                        slice_low(dve, 2 * DC + s * DC, 0, 0, SL)
                    dve.wait_ge(S["bias_masked"], 1)
                    attention_dve(dve, 0, NB, False, chain)
                    means(dve, 2, [(0, 2, Q_LORA), (2, 4, KV_LORA)])
                    scale_first(dve, 2, 4, norm_latents, chain)
                    chunks_low(dve, DC, 6, lambda i: GC["q"] + i)
                    for s in range(7):
                        for k in range(4 if s < 3 else 2):
                            u = U_UQ + 4 * s + k if s < 3 else U_UKV + 2 * (s - 3) + k
                            unit_low(dve, u, u, latent_src(s, k), SL)
                    def rotate(parts):
                        for f, s, c, n, of, os_, a, b in parts:
                            nc.vector.tensor_tensor(a, f, c, ALU.mult)
                            ins = nc.vector.tensor_tensor(b, s, n, ALU.mult)
                        chain(ins)
                        for f, s, c, n, of, os_, a, b in parts:
                            ins = nc.vector.tensor_tensor(of, a, b, ALU.subtract)
                        chain(ins)
                        for f, s, c, n, of, os_, a, b in parts:
                            nc.vector.tensor_tensor(a, s, c, ALU.mult)
                            ins = nc.vector.tensor_tensor(b, f, n, ALU.mult)
                        chain(ins)
                        for f, s, c, n, of, os_, a, b in parts:
                            ins = nc.vector.tensor_tensor(os_, a, b, ALU.add)
                        chain(ins)

                    HR = ROPE // 2
                    rotate([(kpe[:, :, 0:HR], kpe[:, :, HR:ROPE], cos, sin, kpr[:, :, 0, 0:HR], kpr[:, :, 0, HR:ROPE],
                             rt1[:, :, 0], rt2[:, :, 0])])
                    chain(nc.vector.tensor_copy(kpr[:, :, 1], kpr[:, :, 0]))
                    dve.wait_ge(S["slice_out"], 8 + 3)
                    parts = []
                    for h in range(MH):
                        c = h * QH + NOPE
                        parts.append((q_mla[:, :, c:c + HR], q_mla[:, :, c + HR:c + ROPE], cos, sin,
                                      qpe[:, :, h, 0:HR], qpe[:, :, h, HR:ROPE], rt1[:, :, h], rt2[:, :, h]))
                    rotate(parts)
                    dve.sem_inc(S["rope_ready"], 1)
                    attention_dve(dve, NB, MB, True, chain)
                    means(dve, 3, [(0, 4, W_MIX)])
                    scale_first(dve, 3, 4, norm_mixed, chain)
                    chunks_low(dve, DC + 6, DC, lambda i: GC["mla"] + i)
                    with dve.Fori(0, 4) as s:
                        for k in range(DC):
                            unit_low(dve, U_OUT + s * DC + k, U_OUT + k, unit_src(N_OUT + k // PU, k % PU), SL)
                    for s in range(4):
                        dve.wait_ge(S["unit_used"], U_OUT + (s + 1) * DC)
                        xs = x[:, :, s * SL:(s + 1) * SL]
                        nc.vector.tensor_tensor(xs, bank(2 * s, 2).rearrange("p (a n) -> p a n", a=TT), xs, ALU.add)

                @block.tensor
                def _(pe):
                    turn_chunks(pe, 0, 0, [lambda tt, c=c: yn[:, tt, c * P:(c + 1) * P] for c in range(DC)])
                    pe.wait_ge(S["chunk_lo"], DC)
                    slice_product(pe, 0, 0, [bank(tt)[:, 0:NAT0 - Q_LORA] for tt in range(TT)], NAT0 - Q_LORA)
                    slice_product(pe, DC, 0, [bank(2 + tt) for tt in range(TT)], SL)
                    with pe.Fori(0, 3) as i:
                        for b in range(2):
                            s = 2 + i * 2 + b
                            pe.wait_ge(S["slice_out"], s - 1)
                            slice_product(pe, s * DC, 0, [bank(2 * b + tt) for tt in range(TT)], SL)
                    pe.wait_ge(S["slice_out"], 8)
                    for i in range(8):
                        if i >= 4:
                            pe.wait_ge(S["bank_read"], i - 3)
                        for k in range(4):
                            pair, tt = 2 * (i % 4) + k // 2, k % 2
                            src = proj[:, (2 if i < 4 else 4) + pair // 4, tt, (pair % 4) * P:(pair % 4 + 1) * P]
                            ins = nc.tensor.transpose(bank(4 + i % 4)[:, k * P:(k + 1) * P], src, ident)
                        ins.then_inc(S["bank_full"], 1)
                    pe.wait_ge(S["bank_read"], 8)

                    def nat_scores(i, outs):
                        tt, h0 = i // 4, 4 * (i % 4)
                        for h in range(4):
                            pair, r0 = (h0 + h) // 2, ((h0 + h) % 2) * ND
                            ins = nc.tensor.matmul(outs[h], nqt[r0:r0 + ND, pair, tt * P:(tt + 1) * P],
                                                   nkt[r0:r0 + ND, pair, :], start=True, stop=True)
                        return ins

                    def nat_v(i, h, c):
                        hh = 4 * (i % 4) + h
                        return proj[:, 6 + hh // 8, c, (hh % 8) * ND:(hh % 8 + 1) * ND]

                    attention_pe(pe, 0, NB, nat_scores, nat_v, ND, False)
                    turn_chunks(pe, 4, DC, [lambda tt, c=c: cqn[:, tt, c * P:(c + 1) * P] for c in range(4)]
                                + [lambda tt, c=c: ckvn[:, tt, c * P:(c + 1) * P] for c in range(2)])
                    pe.wait_ge(S["chunk_lo"], DC + 6)
                    pe.wait_ge(S["attended"], NB)
                    for s in range(3):
                        for k in range(4):
                            u = U_UQ + 4 * s + k
                            unit_product(pe, u, u, ht_hi[:, k], ht_lo[:, k], [bank(2 * s + tt) for tt in range(TT)],
                                         SL, k == 0, k == 3)
                    for s in range(4):
                        if s >= 1:
                            pe.wait_ge(S["slice_out"], 8 + s)
                        for c in range(2):
                            u = U_UKV + 2 * s + c
                            unit_product(pe, u, u, ht_hi[:, 4 + c], ht_lo[:, 4 + c],
                                         [bank(2 * ((3 + s) % 4) + tt) for tt in range(TT)], SL, c == 0, c == 1)
                    pe.wait_ge(S["slice_out"], 8 + 7)
                    for i in range(11):
                        if i == 8:
                            pe.wait_ge(S["rope_ready"], 1)
                        if i >= 4:
                            pe.wait_ge(S["bank_read"], 8 + i - 3)
                        for k in range(4 if i < 10 else 2):
                            tt = k % 2
                            o = bank(4 + i % 4)[:, k * P:(k + 1) * P]
                            if i < 4:
                                h = 2 * i + k // 2
                                ins = nc.tensor.transpose(o, q_mla[:, tt, h * QH:h * QH + NOPE], ident)
                            elif i < 8:
                                ins = nc.tensor.transpose(o, k_head(2 * (i - 4) + k // 2, tt), ident)
                            elif i < 10:
                                hp = 2 * (i - 8) + k // 2
                                ins = nc.tensor.transpose(
                                    o, qpe[:, tt, 2 * hp:2 * hp + 2].rearrange("p h f -> p (h f)"), ident)
                            else:
                                ins = nc.tensor.transpose(o, kpr[:, tt].rearrange("p b f -> p (b f)"), ident)
                        ins.then_inc(S["bank_full"], 1)
                    pe.wait_ge(S["bank_read"], 8 + 11)

                    def mla_scores(i, outs):
                        tt, h0 = i // 2, 4 * (i % 2)
                        for h in range(4):
                            hh = h0 + h
                            r0 = (hh % 2) * ROPE
                            nc.tensor.matmul(outs[h], qnt[:, hh, tt * P:(tt + 1) * P], knt[:, hh, :],
                                             start=True, stop=False)
                            ins = nc.tensor.matmul(outs[h], qpt[r0:r0 + ROPE, hh // 2, tt * P:(tt + 1) * P],
                                                   kpt[r0:r0 + ROPE, :], start=False, stop=True)
                        return ins

                    attention_pe(pe, NB, MB, mla_scores, lambda i, h, c: v_head(4 * (i % 2) + h, c), MV, True)
                    turn_chunks(pe, 6, DC + 6, [lambda tt, c=c: mla_o[:, tt, c * P:(c + 1) * P] for c in range(8)]
                                + [lambda tt, c=c: nat_o[:, tt, c * P:(c + 1) * P] for c in range(8)])
                    pe.wait_ge(S["chunk_lo"], DC + 6 + DC)
                    with pe.Fori(0, 4) as s:
                        outs = [ps[:, bass.ds(s * (2 * SL) + tt * SL, SL)] for tt in range(TT)]
                        for k in range(DC):
                            unit_product(pe, U_OUT + s * DC + k, U_OUT + k, ht_hi[:, k], ht_lo[:, k], outs, SL,
                                         k == 0, k == DC - 1)

            nc.all_engine_barrier(sems_to_clear=cleared)
            with nc.Block() as block:
                @block.sync
                def _(sp):
                    sp.dma_start(keys_rows, keys.rearrange("l s n d -> n l s d")[:, bass.ds(layer, 1)]
                                 ).then_inc(S["keys_in"], 16)
                    wq = w_q.rearrange("l (q a b r) n -> q a r l b n", q=4, a=4, b=4)
                    ut = u_tab.rearrange("l (e i) (q a c) -> q a i l e c", i=32, q=4, a=4)
                    vt = v_tab.rearrange("l (j p) d -> p l j d", p=P)

                    def put(slot, part, c):
                        for a in range(4):
                            rows = piece[a * 32:(a + 1) * 32, slot, :]
                            sp.dma_start(rows.rearrange("p (l c n) -> p l c n", l=1, c=c), part(a)
                                         ).then_inc(S[f"arrived{slot}"], 16)

                    ly = bass.ds(layer, 1)
                    for q in range(4):
                        put(q, lambda a: wq[q, a][:, ly, :, 0:SL], PU)
                    with sp.Fori(1, 4) as s:
                        for q in range(4):
                            sp.wait_ge(S["lo_ready"], s * DC - DC + (q + 1) * PU)
                            put(q, lambda a: wq[q, a][:, ly, :, bass.ds(s * SL, SL)], PU)
                    with sp.Fori(0, 2) as half:
                        def u_part(g, q):
                            return lambda a: ut[q, a][:, ly, bass.ds((half * HALF_J + g * GJ) * 4, GJ * 4)]

                        def v_part(g, q):
                            return lambda a: vt[a * 32:(a + 1) * 32, ly, bass.ds(half * HALF_J + g * 4 + q, 1), :]

                        for q in range(4):
                            sp.wait_ge(S["lo_ready"], U_A + half * U_HALF - (NP - q - 1) * PU)
                            put(q, u_part(0, q), GJ * 4)
                        with sp.Fori(1, GROUPS) as g:
                            for q in range(4):
                                sp.wait_ge(S["pool_lo_ready"], pool_count(half, g - 1, q * PU + PU - 1))
                                put(q, u_part(g, q), GJ * 4)
                        for q in range(4):
                            sp.wait_ge(S["pool_lo_ready"], pool_count(half, GROUPS - 1, q * PU + PU - 1))
                            put(q, v_part(0, q), 1)
                        with sp.Fori(1, GROUPS) as g:
                            for q in range(4):
                                sp.wait_ge(S["lo_ready"], U_A + half * U_HALF + U_AHALF
                                           + (g - 1) * (4 * PU) + (q + 1) * PU)
                                put(q, v_part(g, q), 1)

                @block.gpsimd
                def _(pool):
                    with pool.Fori(0, 2) as half:
                        with pool.Fori(0, GROUPS) as g:
                            for k in range(DC):
                                if k % VL == 0:
                                    continue
                                u = U_A + half * U_HALF + g * DC + k
                                pool.wait_ge(S["hi_ready"], u + 1)
                                if k % PU == PU - 1:
                                    pool.wait_ge(S["lo_ready"], u + 1)
                                nc.gpsimd.tensor_tensor(u_view(unit_lo[:, k % R]), u_src(k),
                                                        u_view(unit_hi[:, k % R].bitcast(F32)), ALU.subtract
                                                        ).then_inc(S["pool_lo_ready"], 1)

                @block.scalar
                def _(act):
                    chain = chainer(act, S["chain_a"])
                    act.sem_inc(S["gelu_done"], 2)
                    act.sem_inc(S["w_stored"], 1)
                    squares(act, [(tt, x[:, tt], yn[:, tt]) for tt in range(TT)])
                    roots(act, 1, 2)
                    scale_second(act, 1, norm_ffn)
                    chunks_high(act, 0, DC, lambda i: GC["ffn"] + i)
                    slice_high(act, 0, 0, 0, 0, SL, wait=False, parts=4)
                    with act.Fori(1, 4) as s:
                        slice_high(act, s * DC, s * 4, 0, 0, SL, parts=4)
                    for s in range(4):
                        act.wait_ge(S["unit_used"], (s + 1) * DC)
                        nc.scalar.activation(q_peer[:, :, s * SL:(s + 1) * SL],
                                             bank(2 * s, 2).rearrange("p (a n) -> p a n", a=TT), ACT.Copy
                                             ).then_inc(S["q_out"], 1)
                    for i in range(9):
                        act.wait_ge(S["qt_full"], i + 1)
                        if i < 8:
                            dst = q_peer_t[:, 2 * i:2 * i + 2].rearrange("p b t -> p (b t)")
                            nc.scalar.activation(dst, bank(i), ACT.Copy).then_inc(S["qt_read"], 1)
                        else:
                            nc.scalar.activation(keys_t, bank(0)[:, 0:2 * NK], ACT.Copy).then_inc(S["qt_read"], 1)
                    for i in range(8):
                        act.wait_ge(S["score_full"], i + 1)
                        nc.scalar.activation(scores[:, i // 4, 4 * (i % 4):4 * (i % 4) + 4].rearrange(
                            "p b n -> p (b n)"), bank(i), ACT.Copy).then_inc(S["score_read"], 1)
                    def gelu(g, par):
                        act.wait_ge(S["unit_used"], U_A + g_units(g) + DC)
                        act.wait_ge(S["gelu_turned"], g_count(g) + 1)
                        for tt in range(TT):
                            ins = nc.scalar.activation(ga[:, par, tt], bank(2 * par + tt), ACT.Gelu)
                        ins.then_inc(S["gelu_done"], 1)

                    def store(g):
                        act.wait_ge(S["gelu_turned"], g_count(g) + 2 + 1)
                        nc.scalar.activation(arena[:, bass.ds(g[1] * (GJ * T), GJ * T)], bank(6, 2), ACT.Copy
                                             ).then_inc(S["w_stored"], 1)

                    def step(half, i, k, tails):
                        g = (half, i * 2 + k // DC)
                        a = i * (2 * DC) + k
                        act.wait_ge(S["unit_used"], U_A + half * U_HALF + a - R + 1)
                        act.wait_ge(S["u_turned"], half * U_AHALF + a + 1)
                        nc.scalar.activation(u_view(unit_hi[:, k % R]), u_src(k % DC), ACT.Copy
                                             ).then_inc(S["hi_ready"], 1)
                        before = (half, g[1] - 1)
                        if tails and k % DC == 2:
                            gelu(before, (k // DC + 1) % 2)
                        if tails and k % DC == 7:
                            store(before)

                    for half in range(2):
                        for k in range(SHIFT):
                            step(half, 0, k, False)
                        with act.Fori(0, PAIRS - 1) as i:
                            for k in range(SHIFT, 2 * DC + SHIFT):
                                step(half, i + k // (2 * DC), k % (2 * DC), True)
                        for k in range(SHIFT, 2 * DC):
                            step(half, PAIRS - 1, k, True)
                        gelu((half, GROUPS - 1), 1)
                        store((half, GROUPS - 1))
                        if half == 0:
                            act.wait_ge(S["ranked"], 1)
                            nc.scalar.activation(gates, gate_rows, ACT.Exp).then_inc(S["gates_exp"], 1)
                            act.wait_ge(S["small_full"], 1)
                            nc.scalar.activation(i1t[:, :], bank(0)[:, 0:T], ACT.Copy)
                            nc.scalar.activation(i2t[:, :], bank(1)[:, 0:T], ACT.Copy).then_inc(S["small_read"], 1)
                        act.wait_ge(S["w_gated"], (half + 1) * BATCHES + GATE0)
                        with act.Fori(0, GROUPS) as g:
                            for b in range(4):
                                j = g * 4 + b
                                act.wait_ge(S["unit_used"], U_A + half * U_HALF + U_AHALF + (j - 1) * 4)
                                nc.scalar.activation(wj_hi[:, b % 2], arena[:, bass.ds(j * T, T)], ACT.Copy
                                                     ).then_inc(S["wj_hi_ready"], 1)
                                n = N_A + half * N_HALF + HALF_J + j
                                piece_here(act, b, n, 4)
                                for k in range(4):
                                    unit_high(act, U_A + half * U_HALF + U_AHALF + j * 4 + k, k, unit_src(b, k), SL)

                @block.vector
                def _(dve):
                    chain = chainer(dve, S["chain_v"])
                    means(dve, 1, [(0, 2, D)])
                    scale_first(dve, 1, 2, norm_ffn, chain)
                    chunks_low(dve, 0, DC, lambda i: GC["ffn"] + i)
                    with dve.Fori(0, 4) as s:
                        slice_low(dve, s * DC, 0, 0, SL)
                    dve.wait_ge(S["score_read"], 8)
                    dve.sem_inc(S["psum_clear"], 1)
                    dve.sem_inc(S["w_gated"], GATE0)

                    def link(n, ins):
                        ins.then_inc(S["rank_chain"], 1)
                        dve.wait_ge(S["rank_chain"], n)

                    def rank(part, r):
                        if part == 0:
                            dve.sem_clear(S["rank_chain"])
                            link(1, nc.vector.tensor_copy(work[:, 0], score_rows[:, bass.ds(r * 2 * NK, 2 * NK)]))
                        elif part == 1:
                            for s in range(2):
                                ins = nc.vector.max(top_v[:, s, 0:8], work[:, 0, s * NK:(s + 1) * NK])
                            link(2, ins)
                        elif part == 2:
                            for s in range(2):
                                nc.vector.max_index(top_i[:, s, 0:8], top_v[:, s, 0:8],
                                                    work[:, 0, s * NK:(s + 1) * NK])
                        elif part == 3:
                            for s in range(2):
                                ins = nc.vector.match_replace(work[:, 1, s * NK:(s + 1) * NK], top_v[:, s, 0:8],
                                                              work[:, 0, s * NK:(s + 1) * NK], NEG)
                            link(3, ins)
                        elif part == 4:
                            for s in range(2):
                                ins = nc.vector.max(top_v[:, s, 8:16], work[:, 1, s * NK:(s + 1) * NK])
                            link(4, ins)
                        elif part == 5:
                            for s in range(2):
                                nc.vector.max_index(top_i[:, s, 8:16], top_v[:, s, 8:16],
                                                    work[:, 1, s * NK:(s + 1) * NK])
                        elif part == 6:
                            link(5, nc.vector.tensor_tensor(
                                cand[:, 0].rearrange("p (a b) -> p a b", a=TOPK),
                                top_v[:, 0].unsqueeze(2).to_broadcast([P, TOPK, TOPK]),
                                top_v[:, 1].unsqueeze(1).to_broadcast([P, TOPK, TOPK]), ALU.add))
                            nc.vector.tensor_copy(top_if, top_i)
                        elif part == 7:
                            link(6, nc.vector.max(best_v[:, 0:8], cand[:, 0]))
                            nc.vector.max_index(best_p[:, 0:8], best_v[:, 0:8], cand[:, 0])
                        elif part == 8:
                            link(7, nc.vector.match_replace(cand[:, 1], best_v[:, 0:8], cand[:, 0], NEG))
                        elif part == 9:
                            link(8, nc.vector.max(best_v[:, 8:16], cand[:, 1]))
                            link(9, nc.vector.max_index(best_p[:, 8:16], best_v[:, 8:16], cand[:, 1]))
                        elif part == 10:
                            nc.vector.tensor_copy(gate_rows[:, bass.ds(r * TOPK, TOPK)], best_v)
                            nc.vector.tensor_scalar(pos_i[:, 0], best_p, 4, None, ALU.logical_shift_right)
                            link(10, nc.vector.tensor_scalar(pos_i[:, 1], best_p, TOPK - 1, None, ALU.bitwise_and))
                        elif part == 11:
                            link(11, nc.vector.tensor_copy(pos_f, pos_i))
                        elif part == 12:
                            for s in range(2):
                                ins = nc.vector.tensor_tensor(
                                    pick[:, s], iota16.unsqueeze(1).to_broadcast([P, TOPK, TOPK]),
                                    pos_f[:, s].unsqueeze(2).to_broadcast([P, TOPK, TOPK]), ALU.is_equal)
                            link(12, ins)
                        elif part == 13:
                            for s in range(2):
                                ins = nc.vector.tensor_tensor(
                                    pick[:, s], pick[:, s],
                                    top_if[:, s].unsqueeze(1).to_broadcast([P, TOPK, TOPK]), ALU.mult)
                            link(13, ins)
                        elif part == 14:
                            for s in range(2):
                                ins = nc.vector.tensor_reduce(key_rows[s][:, bass.ds(r * TOPK, TOPK)], pick[:, s],
                                                              AX.X, ALU.add)
                            link(14, ins)

                    assert TT * PH == GROUPS, "a round for each group of experts"
                    def turn_unit(half, g, k):
                        if k % PU == 0:
                            piece_here(dve, k // PU, N_A + half * N_HALF + g * 4 + k // PU, 4)
                        blocks = u_src(k).bitcast(U32)
                        nc.vector.transpose(blocks, blocks).then_inc(S["u_turned"], 1)

                    def u_group(half, g, ahead=True):
                        for k in range(DC):
                            if k + 2 < DC:
                                turn_unit(half, g, k + 2)
                            elif ahead:
                                turn_unit(half, g + 1, k + 2 - DC)
                            if k % VL == 0:
                                dve.wait_ge(S["hi_ready"], U_A + half * U_HALF + g * DC + k + 1)
                                nc.vector.tensor_tensor(u_view(unit_lo[:, k % R]), u_src(k),
                                                        u_view(unit_hi[:, k % R].bitcast(F32)), ALU.subtract
                                                        ).then_inc(S["lo_ready"], VL)
                            if half == 0:
                                rank(k, g)
                            elif not ahead and k < 10:
                                hot_rows(1, 0, k // 5, k % 5)

                    def selected():
                        r3 = gate_rows.rearrange("p (r k) -> p r k", k=TOPK)
                        chain(nc.vector.tensor_copy(gmax, r3[:, :, 0]))
                        chain(nc.vector.tensor_tensor(
                            r3, r3, gmax.unsqueeze(2).to_broadcast([P, TT * PH, TOPK]), ALU.subtract))
                        dve.sem_inc(S["ranked"], 1)
                        chain(nc.vector.tensor_copy(iota_t, iota[:, :].unsqueeze(2).to_broadcast([P, NK, BT])))
                        g3 = gates.rearrange("p (r k) -> p r k", k=TOPK)
                        dve.wait_ge(S["gates_exp"], 1)
                        chain(nc.vector.tensor_reduce(gsum, g3, AX.X, ALU.add))
                        chain(nc.vector.reciprocal(gmax, gsum))
                        nc.vector.tensor_tensor(g3, g3, gmax.unsqueeze(2).to_broadcast([P, TT * PH, TOPK]), ALU.mult
                                                ).then_inc(S["rows_ready"], 1)
                        dve.wait_ge(S["small_read"], 1)
                        gps = bank(2)[:, 0:T]
                        chain(nc.vector.tensor_copy(gt[:, 0], gps))
                        chain(nc.vector.tensor_tensor(rest[:, 0], gps, gt[:, 0], ALU.subtract))
                        chain(nc.vector.tensor_copy(gt[:, 1], rest[:, 0]))
                        chain(nc.vector.tensor_tensor(rest[:, 1], rest[:, 0], gt[:, 1], ALU.subtract))
                        chain(nc.vector.tensor_copy(gt[:, 2], rest[:, 1]))

                    def hot_rows(half, i, b, part):
                        ts = bass.ds((i * 2 + b) * BT, BT)
                        n = half * BATCHES + i * 2 + b
                        if part == 0:
                            nc.vector.tensor_tensor(
                                hot1[:, b], iota_t[:, half * HALF_J:(half + 1) * HALF_J],
                                i1t[:, ts].unsqueeze(1).to_broadcast([P, HALF_J, BT]), ALU.is_equal
                            ).then_inc(S["hot_chain"], 1)
                        elif part == 1:
                            dve.wait_ge(S["gates_made"], n + 1)
                            nc.vector.tensor_tensor(
                                hot2[:, b], iota_t, i2t[:, ts].unsqueeze(1).to_broadcast([P, NK, BT]), ALU.is_equal)
                            dve.wait_ge(S["hot_chain"], n + 1)
                        else:
                            c = part - 2
                            ins = nc.vector.tensor_tensor(
                                hotg[:, b, c], hot1[:, b], gt[:, c, ts].unsqueeze(1).to_broadcast([P, HALF_J, BT]),
                                ALU.mult)
                            if part == 4:
                                ins.then_inc(S["onehot_rows"], 1)

                    def gate(half, i, b):
                        dve.wait_ge(S["gates_made"], half * BATCHES + i * 2 + b + 2 + 1)
                        w3 = w_view[:, :, bass.ds((i * 2 + b) * BT, BT)]
                        nc.vector.tensor_tensor(w3, bank(2 * b, 2).rearrange("p (t j) -> p j t", t=BT), w3,
                                                ALU.mult).then_inc(S["w_gated"], 1)

                    turn_unit(0, 0, 0)
                    turn_unit(0, 0, 1)
                    for half in range(2):
                        with dve.Fori(0, GROUPS - 1) as g:
                            u_group(half, g)
                        u_group(half, GROUPS - 1, ahead=False)
                        if half == 0:
                            selected()
                            for b in range(2):
                                for part in range(5):
                                    hot_rows(0, 0, b, part)
                        with dve.Fori(0, BATCHES // 2 - 1) as i:
                            for b in range(2):
                                gate(half, i, b)
                                for part in range(5):
                                    hot_rows(half, i + 1, b, part)
                        for b in range(2):
                            gate(half, BATCHES // 2 - 1, b)
                        with dve.Fori(0, GROUPS) as g:
                            for b in range(4):
                                j = g * 4 + b
                                dve.wait_ge(S["wj_hi_ready"], half * HALF_J + j + 1)
                                nc.vector.tensor_tensor(wj_lo[:, b % 2], arena[:, bass.ds(j * T, T)],
                                                        wj_hi[:, b % 2].bitcast(F32), ALU.subtract
                                                        ).then_inc(S["wj_lo_ready"], 1)
                                for k in range(4):
                                    unit_low(dve, U_A + half * U_HALF + U_AHALF + j * 4 + k, k, unit_src(b, k), SL)
                        if half == 0:
                            turn_unit(1, 0, 0)
                            turn_unit(1, 0, 1)
                        dve.wait_ge(S["unit_used"], U_A + (half + 1) * U_HALF)
                        for tt in range(TT):
                            nc.vector.tensor_tensor(x[:, tt], bank(4 * tt, 4), x[:, tt], ALU.add
                                                    ).then_inc(S["psum_clear"], 1)

                @block.tensor
                def _(pe):
                    pe.sem_inc(S["gelu_turned"], 2)
                    pe.sem_inc(S["gates_made"], 2)
                    turn_chunks(pe, 0, 0, [lambda tt, c=c: yn[:, tt, c * P:(c + 1) * P] for c in range(DC)])
                    pe.wait_ge(S["chunk_lo"], DC)
                    with pe.Fori(0, 4) as s:
                        outs = [ps[:, bass.ds(s * (2 * SL) + tt * SL, SL)] for tt in range(TT)]
                        slice_product(pe, s * DC, 0, outs, SL)
                    pe.wait_ge(S["q_out"], 4)
                    for i in range(8):
                        for k in range(4):
                            blk, tt = 2 * i + k // 2, k % 2
                            ins = nc.tensor.transpose(bank(i)[:, k * P:(k + 1) * P],
                                                      q_peer[:, tt, blk * NK:(blk + 1) * NK], ident)
                        ins.then_inc(S["qt_full"], 1)
                    pe.wait_ge(S["keys_in"], 16)
                    pe.wait_ge(S["qt_read"], 1)
                    for s in range(2):
                        ins = nc.tensor.transpose(bank(0)[:, s * NK:(s + 1) * NK],
                                                  keys_rows[:, 0, s], ident)
                    ins.then_inc(S["qt_full"], 1)
                    pe.wait_ge(S["qt_read"], 9)
                    for i in range(8):
                        tt = i // 4
                        for k in range(4):
                            blk = 4 * (i % 4) + k
                            ins = nc.tensor.matmul(bank(i)[:, k * NK:(k + 1) * NK],
                                                   q_peer_t[:, blk, tt * P:(tt + 1) * P],
                                                   keys_t[:, (blk % 2) * NK:(blk % 2 + 1) * NK],
                                                   start=True, stop=True)
                        ins.then_inc(S["score_full"], 1)
                    def turn_gelu(g, par):
                        pe.wait_ge(S["psum_clear"], 2 * g[0] + 1)
                        pe.wait_ge(S["gelu_done"], g_count(g) + 2 + 1)
                        pe.wait_ge(S["w_stored"], g_count(g) + 1)
                        for jj in range(GJ):
                            for tt in range(TT):
                                ins = nc.tensor.transpose(bank(6, 2)[:, jj * T + tt * P:jj * T + (tt + 1) * P],
                                                          ga[:, par, tt, jj * P:(jj + 1) * P], ident)
                        ins.then_inc(S["gelu_turned"], 1)

                    def step(half, i, k, tails):
                        g = (half, i * 2 + k // DC)
                        par = k // DC
                        if k % VL:
                            pe.wait_ge(S["pool_lo_ready"],
                                       pool_count(half, i * 2 + k // DC, k % DC))
                        if k % DC == 0:
                            pe.wait_ge(S["gelu_done"], g_count(g) + 1)
                        unit_product(pe, U_A + half * U_HALF + i * (2 * DC) + k, k, ht_hi[:, k % DC],
                                     ht_lo[:, k % DC], [bank(2 * par + tt) for tt in range(TT)], SL,
                                     k % DC == 0, k % DC == DC - 1)
                        if tails and k % DC == 4:
                            turn_gelu((half, g[1] - 1), (par + 1) % 2)

                    def gates_step(half, i, b):
                        n = half * BATCHES + i * 2 + b
                        pe.wait_ge(S["onehot_rows"], n + 1)
                        pe.wait_ge(S["w_gated"], n - 1 + GATE0)
                        for t in range(BT):
                            for c in range(3):
                                ins = nc.tensor.matmul(bank(2 * b, 2)[:, t * HALF_J:(t + 1) * HALF_J],
                                                       hot2[:, b, :, t], hotg[:, b, c, :, t],
                                                       start=(c == 0), stop=(c == 2))
                        ins.then_inc(S["gates_made"], 1)

                    def v_steps(half, g, first, last):
                        for b in range(4):
                            j = g * 4 + b
                            pe.wait_ge(S["wj_lo_ready"], half * HALF_J + j + 1)
                            for k in range(4):
                                outs = [bank(4 * tt + k) for tt in range(TT)]
                                unit_product(pe, U_A + half * U_HALF + U_AHALF + j * 4 + k, k, wj_hi[:, b % 2],
                                             wj_lo[:, b % 2], outs, SL, first and b == 0, last and b == 3)

                    for half in range(2):
                        pe.wait_ge(S["psum_clear"], half + 1)
                        for k in range(SHIFT):
                            step(half, 0, k, False)
                        with pe.Fori(0, PAIRS - 1) as i:
                            for k in range(SHIFT, 2 * DC + SHIFT):
                                step(half, i + k // (2 * DC), k % (2 * DC), True)
                        for k in range(SHIFT, 2 * DC):
                            step(half, PAIRS - 1, k, True)
                        turn_gelu((half, GROUPS - 1), 1)
                        if half == 0:
                            pe.wait_ge(S["rows_ready"], 4 + 1)
                            for i, rows in enumerate((key_rows[0], key_rows[1], gates)):
                                for tt in range(TT):
                                    ins = nc.tensor.transpose(bank(i)[:, tt * P:(tt + 1) * P],
                                                              rows[:, tt * HK:(tt + 1) * HK], ident)
                            ins.then_inc(S["small_full"], 1)
                        with pe.Fori(0, BATCHES // 2) as i:
                            pe.wait_ge(S["w_stored"], (half + 1) * GROUPS + 1)
                            for b in range(2):
                                gates_step(half, i, b)
                        pe.wait_ge(S["w_gated"], (half + 1) * BATCHES + GATE0)
                        v_steps(half, 0, True, False)
                        with pe.Fori(1, GROUPS - 1) as g:
                            v_steps(half, g, False, False)
                        v_steps(half, GROUPS - 1, False, True)

            nc.all_engine_barrier(sems_to_clear=cleared)

        with nc.Block() as block:
            gain = arena[:, 0:D]
            rows = arena[:, YN:YN + TT * D].rearrange("p (a d) -> p a d", a=TT)

            @block.sync
            def _(sp):
                sp.dma_start(gain, final_norm.rearrange("(o d) -> o d", o=1).to_broadcast([P, D])
                             ).then_inc(S["keys_in"], 16)
                o = out.rearrange("(a p) d -> p a d", p=P)
                for tt in range(TT):
                    sp.wait_ge(S["ranked"], tt + 1)
                    sp.dma_start(o[:, tt], rows[:, tt]).then_inc(S["stored"], 16)
                sp.wait_ge(S["stored"], 16 * TT)

            @block.scalar
            def _(act):
                squares(act, [(tt, x[:, tt], rows[:, tt]) for tt in range(TT)])
                roots(act, 1, 2)

            @block.vector
            def _(dve):
                chain = chainer(dve, S["chain_v"])
                means(dve, 1, [(0, 2, D)])
                dve.wait_ge(S["root_ready"], 1)
                dve.wait_ge(S["keys_in"], 16)
                chain(nc.vector.reciprocal(rstd[:, 0:2], ssq[:, 0:2]))
                for tt in range(TT):
                    nc.vector.scalar_tensor_tensor(rows[:, tt], x[:, tt], rstd[:, tt:tt + 1], gain,
                                                   ALU.mult, ALU.mult).then_inc(S["ranked"], 1)


def kernel(**inputs):
    import numpy as np
    import concourse.bacc as bacc
    from concourse.bass_utils import run_bass_kernel_spmd

    inv = (np.float32(10000.0) ** (-np.arange(0, ROPE, 2, dtype=np.float32) / np.float32(ROPE))).astype(np.float32)
    ang = np.arange(T, dtype=np.float32)[:, None] * inv[None, :]
    tables = [np.ascontiguousarray(f(ang).astype(np.float32).reshape(TT, P, ROPE // 2).transpose(1, 0, 2)).reshape(
        P, -1) for f in (np.cos, np.sin)]
    c = np.arange(P) % GRID_W
    c0 = np.clip(c - WIN_C // 2, 0, GRID_W - WIN_C)[:, None]
    kc = np.arange(GRID_W)[None, :]
    outside = np.where((kc >= c0) & (kc < c0 + WIN_C), 0.0, -1.0e30).astype(np.float32)
    consts = np.concatenate([np.eye(P, dtype=np.float32), *tables, outside,
                             np.broadcast_to(np.arange(TOPK, dtype=np.float32), (P, TOPK))], axis=1)

    order = ["x", "attn_norm", "ffn_norm", "mla_q_norm", "mla_kv_norm", "mla_out_norm", "nat_out_norm", "w_in",
             "mla_w_uq", "mla_w_ukv", "nat_rpb", "w_out", "peer_w_q", "peer_sub_keys", "peer_u", "peer_v",
             "final_norm"]
    nc = bacc.Bacc("TRN2", target_bir_lowering=False, num_devices=1)
    arrays, ap = {}, {}
    for name in order:
        a = np.ascontiguousarray(inputs[name])
        if name == "x":
            a = a.reshape(T, D)
        arrays["in_" + name] = a
        ap[name] = nc.dram_tensor("in_" + name, a.shape, mybir.dt.from_np(a.dtype), kind="ExternalInput").ap()
    arrays["in_consts"] = np.ascontiguousarray(consts)
    consts_ap = nc.dram_tensor("in_consts", consts.shape, F32, kind="ExternalInput").ap()
    out = nc.dram_tensor("out_0", (T, D), F32, kind="ExternalOutput").ap()
    gains = dict(attn=ap["attn_norm"], ffn=ap["ffn_norm"], q=ap["mla_q_norm"], kv=ap["mla_kv_norm"],
                 mla=ap["mla_out_norm"], nat=ap["nat_out_norm"])
    build(nc, ap["x"], gains, ap["w_in"], ap["mla_w_uq"], ap["mla_w_ukv"], ap["nat_rpb"], ap["w_out"],
          ap["peer_w_q"], ap["peer_sub_keys"], ap["peer_u"], ap["peer_v"], ap["final_norm"], consts_ap, out)
    r = run_bass_kernel_spmd(nc, [arrays], core_ids=[0])
    return r.results[0]["out_0"].reshape(1, T, D)
```

```python
from contextlib import ExitStack

import concourse.bass as bass
from concourse import mybir

F32 = mybir.dt.float32
F32R = mybir.dt.float32r
BF16 = mybir.dt.bfloat16
U32 = mybir.dt.uint32
ACT = mybir.ActivationFunctionType
ALU = mybir.AluOpType
AX = mybir.AxisListType

P = 128
L, D, T = 2, 2048, 256
TT = T // P
DC = D // P
SL = 512
Q_LORA, KV_LORA, ROPE = 512, 256, 64
MH, NOPE, MV = 8, 128, 128
NH, ND = 16, 64
W_MIX = 1024
NAT0 = Q_LORA + KV_LORA + ROPE
GRID_W, WIN_R, WIN_C, ROWS = 64, 8, 16, 4
NDR = 6
DR_ALL = 2 * WIN_R - 1
DC_ALL = 2 * WIN_C - 1
PH, NK, TOPK = 8, 128, 16
HK = PH * TOPK
HALF_J = NK // 2
EPS = 1e-6
NEG = -3.0e38
NP = 4
PU = 4
R = 4
GC = dict(attn=0, ffn=16, q=32, kv=36, mla=38, nat=46)
NG = 54

ARENA = HALF_J * T
GJ, BT, SHIFT = 4, 16, 8
GROUPS, PAIRS, BATCHES = HALF_J // GJ, HALF_J // GJ // 2, T // BT
U_A, U_HALF, U_AHALF = 4 * DC, 2 * GROUPS * DC, GROUPS * DC
VL = 4
U_POOL = U_AHALF // VL * (VL - 1)
YN = 8192
REST = 12288
STAGE = 7168


def build(nc, x_in, gains, w_in, w_uq, w_ukv, rpb, w_out, w_q, keys, u_tab, v_tab, final_norm, consts, out):
    ctx = ExitStack()
    with ctx:
        def sb(name, shape, dt=F32):
            return ctx.enter_context(nc.sbuf_tensor(name, shape, dt))

        x = sb("x", [P, TT, D])
        arena = sb("arena", [P, ARENA])
        stage = sb("stage", [P, STAGE])
        ht_hi = sb("ht_hi", [P, DC, T], F32R)
        ht_lo = sb("ht_lo", [P, DC, T], F32R)
        unit_hi = sb("unit_hi", [P, R, SL], F32R)
        unit_lo = sb("unit_lo", [P, R, SL], F32R)
        piece = sb("piece", [P, NP, PU * SL])
        wj_hi = sb("wj_hi", [P, 2, T], F32R)
        wj_lo = sb("wj_lo", [P, 2, T], F32R)
        ga = sb("ga", [P, 2, TT, SL])
        con = sb("con", [P, 128 + 128 + 64 + 16])
        iota = sb("iota", [P, NK], BF16)
        grow = stage[:, 0:P]
        gall = sb("gall", [P, L * NG])
        gcol = sb("gcol", [P, NG])
        i1t = sb("i1t", [P, T], BF16)
        i2t = sb("i2t", [P, T], BF16)
        gt = sb("gt", [P, 3, T], BF16)
        ssq = sb("ssq", [P, 4])
        rms = sb("rms", [P, 4])
        rstd = sb("rstd", [P, 4])
        mx = sb("mx", [P, 2, 4])
        den = sb("den", [P, 2, 4])
        rden = sb("rden", [P, 2, 4])
        smax = sb("smax", [P, 2, 4])
        per_round = sb("per_round", [P, 2 * TT * PH])
        yn = arena[:, YN:YN + TT * D].rearrange("p (a d) -> p a d", a=TT)
        ident = con[:, 0:128]
        cos = con[:, 128:192].rearrange("p (a f) -> p a f", a=TT)
        sin = con[:, 192:256].rearrange("p (a f) -> p a f", a=TT)
        mask = con[:, 256:320]
        iota16 = con[:, 320:336]
        ps = ctx.enter_context(nc.psum_tensor("ps", [P, 8 * SL], F32))

        rpb_pad = nc.dram_tensor("rpb_pad", (L * NH * DR_ALL, P), F32).ap()
        skewed = nc.dram_tensor("skewed", (NH, NDR + 1, GRID_W, P - 1), F32).ap()

        names = [f"arrived{s}" for s in range(NP)] + """
            hi_ready lo_ready unit_used squared mean_ready root_ready rows_ready chunk_turned chunk_hi chunk_lo
            chain_v bank_full bank_read scored maxed expd probs_turned probs_read mixed attended bias_in
            keys_in ranked gates_exp slice_out rope_ready u_turned gelu_done gelu_turned w_stored onehot_rows
            gates_made even_gated odd_gated gates_copied wj_hi_ready wj_lo_ready hot_chain rank_chain psum_clear
            bias_skewed stored q_out qt_full qt_read score_full score_read small_full small_read x_added
            bias_masked pool_lo_ready inverse_ready rows_ready_2""".split()
        S = {n: ctx.enter_context(nc.semaphore(n)) for n in names}
        setup_in = ctx.enter_context(nc.semaphore("setup_in"))
        setup_c = ctx.enter_context(nc.semaphore("setup_c"))
        x_here = ctx.enter_context(nc.semaphore("x_here"))
        pad_ready = ctx.enter_context(nc.semaphore("pad_ready"))
        bias_made = ctx.enter_context(nc.semaphore("bias_made"))
        nums = sorted(s.num for s in S.values())
        assert nums[-1] - nums[0] == len(nums) - 1
        cleared = range(nums[0], nums[-1] + 1)

        def bank(b, n=1):
            return ps[:, b * SL:(b + n) * SL]

        def rounds(slot, n):
            return (n - slot) * (16 // NP) + 16

        def piece_here(eng, slot, n, parts=1):
            eng.wait_ge(S[f"arrived{slot}"], parts * rounds(slot, n))

        def u_here(eng, slot, half, g):
            eng.wait_ge(S[f"arrived{slot}"], (4 + half * GROUPS + g + 1) * (4 * 16) + half * GROUPS * 16)

        def v_here(eng, slot, half, g):
            eng.wait_ge(S[f"arrived{slot}"], (4 + (half + 1) * GROUPS) * (4 * 16) + (half * GROUPS + g + 1) * 16)

        def unit_high(act, u, k, src, w, wait=True):
            if wait:
                act.wait_ge(S["unit_used"], u - R + 1)
            nc.scalar.activation(unit_hi[:, k % R, 0:w], src, ACT.Copy).then_inc(S["hi_ready"], 1)

        def unit_low(dve, u, k, src, w):
            dve.wait_ge(S["hi_ready"], u + 1)
            nc.vector.tensor_tensor(unit_lo[:, k % R, 0:w], src, unit_hi[:, k % R, 0:w].bitcast(F32),
                                    ALU.subtract).then_inc(S["lo_ready"], 1)

        def unit_product(pe, u, k, hi, lo, outs, w, start, stop):
            pe.wait_ge(S["lo_ready"], u + 1)
            last = None
            for tt in range(TT):
                a, b = hi[:, tt * P:(tt + 1) * P], lo[:, tt * P:(tt + 1) * P]
                nc.tensor.matmul(outs[tt], a, unit_hi[:, k % R, 0:w], start=start, stop=False)
                nc.tensor.matmul(outs[tt], a, unit_lo[:, k % R, 0:w], start=False, stop=False)
                last = nc.tensor.matmul(outs[tt], b, unit_hi[:, k % R, 0:w], start=False, stop=stop)
            last.then_inc(S["unit_used"], 1)

        def unit_src(n, k, w=SL):
            return piece[:, n % NP, k * w:(k + 1) * w]

        def slice_high(act, u0, n0, k0, m0, w, wait=True, parts=1):
            for k in range(DC):
                if k % PU == 0:
                    piece_here(act, (m0 + k // PU) % NP, n0 + k // PU, parts)
                unit_high(act, u0 + k, k0 + k, unit_src(m0 + k // PU, k % PU, w), w, wait or k >= R)

        def slice_low(dve, u0, k0, m0, w):
            for k in range(DC):
                unit_low(dve, u0 + k, k0 + k, unit_src(m0 + k // PU, k % PU, w), w)

        def slice_product(pe, u0, k0, outs, w):
            for k in range(DC):
                unit_product(pe, u0 + k, k0 + k, ht_hi[:, k], ht_lo[:, k], outs, w, k == 0, k == DC - 1)

        def squares(parts):
            for c, rows, junk in parts:
                ins = nc.scalar.activation(junk, rows, ACT.Square, accum_out=ssq[:, c:c + 1])
            return ins

        def means(dve, n, parts):
            if n:
                dve.wait_ge(S["squared"], n)
            for c0, c1, width in parts:
                ins = nc.vector.tensor_scalar(rms[:, c0:c1], ssq[:, c0:c1], 1.0 / width, EPS, ALU.mult, ALU.add)
            ins.then_inc(S["mean_ready"], 1)

        def roots(act, n, cols):
            act.wait_ge(S["mean_ready"], n)
            nc.scalar.activation(ssq[:, 0:cols], rms[:, 0:cols], ACT.Sqrt).then_inc(S["root_ready"], 1)

        def scale_first(dve, n, cols, groups, chain):
            dve.wait_ge(S["root_ready"], n)
            chain(nc.vector.reciprocal(rstd[:, 0:cols], ssq[:, 0:cols]))
            dve.sem_inc(S["inverse_ready"], 1)
            for c, dst, src in groups:
                nc.vector.tensor_scalar(dst(0), src(0), rstd[:, c:c + 1], None, ALU.mult).then_inc(S["rows_ready"], 1)

        def scale_second(act, n, groups, c0, gain0):
            def scale(q):
                c, dst, src = groups[q]
                nc.scalar.activation(dst(1), src(1), ACT.Copy, scale=rstd[:, c + 1:c + 2]
                                     ).then_inc(S["rows_ready_2"], 1)

            def chunk(i):
                if i % 4 == 1 and i // 4 + 1 < len(groups):
                    scale(i // 4 + 1)
                chunk_high(act, c0 + i, i, gain0 + i)

            act.wait_ge(S["inverse_ready"], n)
            scale(0)
            return chunk

        def with_chunks(eng, count, units, chunk, unit):
            pe = eng == "tensor"
            ahead = 0 if pe else 2
            for i in range(4):
                chunk(i)
            for k in range(ahead):
                unit(k)
            for k in range(units):
                if not pe and k + ahead < units:
                    unit(k + ahead)
                if k + 4 < count:
                    chunk(k + 4)
                if pe:
                    unit(k)

        def chunk_turner(pe, groups_before, c0, chunks):
            def turn(i):
                c = c0 + i
                if i % 4 == 0:
                    pe.wait_ge(S["rows_ready"], groups_before + i // 4 + 1)
                    pe.wait_ge(S["rows_ready_2"], groups_before + i // 4 + 1)
                if c >= 4:
                    pe.wait_ge(S["chunk_lo"], c - 3)
                for tt in range(TT):
                    ins = nc.tensor.transpose(bank(4 + c % 4)[:, tt * P:(tt + 1) * P], chunks[i](tt), ident)
                ins.then_inc(S["chunk_turned"], 1)
            return turn

        def chunk_high(act, c, i, gain):
            act.wait_ge(S["chunk_turned"], c + 1)
            nc.scalar.activation(ht_hi[:, i], bank(4 + c % 4)[:, 0:T], ACT.Copy,
                                 scale=gcol[:, gain:gain + 1]).then_inc(S["chunk_hi"], 1)

        def chunk_low(dve, c, i, gain):
            dve.wait_ge(S["chunk_hi"], c + 1)
            nc.vector.scalar_tensor_tensor(ht_lo[:, i], bank(4 + c % 4)[:, 0:T], gcol[:, gain:gain + 1],
                                           ht_hi[:, i].bitcast(F32), ALU.mult, ALU.subtract
                                           ).then_inc(S["chunk_lo"], 1)

        def first_products(pe, groups_before, c0, u0, count, units, chunks, w):
            def product(k):
                pe.wait_ge(S["chunk_lo"], c0 + k + 1)
                unit_product(pe, u0 + k, u0 + k, ht_hi[:, k], ht_lo[:, k], [bank(tt)[:, 0:w] for tt in range(TT)], w,
                             k == 0, k == units - 1)

            with_chunks("tensor", count, units, chunk_turner(pe, groups_before, c0, chunks), product)

        def quarter(rows, q):
            return lambda tt: rows[:, tt, q * SL:(q + 1) * SL]

        def chainer(eng, sem):
            count = [0]

            def chain(ins):
                count[0] += 1
                ins.then_inc(sem, 1)
                eng.wait_ge(sem, count[0])
            return chain

        with nc.Block() as block:
            @block.sync
            def _(sp):
                sp.dma_start(con[:, :], consts).then_inc(setup_in, 16)
                for l in range(L):
                    for name in GC:
                        r0 = l * NG + GC[name]
                        if name == "ffn":
                            src = gains[name][l].rearrange("(q a b r) -> q b a r", q=4, a=4, b=4)
                            for q in range(4):
                                sp.dma_start(grow[r0 + 4 * q:r0 + 4 * q + 4, :].rearrange("b (a r) -> b a r", a=4),
                                             src[q]).then_inc(setup_in, 16)
                            continue
                        src = gains[name][l].rearrange("(c p) -> c p", p=P)
                        sp.dma_start(grow[r0:r0 + src.shape[0], :], src).then_inc(setup_in, 16)

            @block.gpsimd
            def _(pool):
                nc.gpsimd.iota(iota[:, :], [[1, NK]], base=0, channel_multiplier=0,
                               allow_small_or_imprecise_dtypes=True)
                zeros = arena[0:120, 0:512]
                nc.gpsimd.memset(zeros, 0.0).then_inc(pad_ready, 1)

            @block.scalar
            def _(act):
                for tt in range(TT):
                    act.dma_start(x[:, tt], x_in[tt * P:(tt + 1) * P, :]).then_inc(x_here, 16)
                act.wait_ge(pad_ready, 1)
                pad = rpb_pad.rearrange("(p a) m -> p a m", p=120)
                act.dma_start(pad, arena[0:120, 0:512].rearrange("p (a m) -> p a m", m=P)).then_inc(bias_made, 16)
                act.wait_ge(bias_made, 16)
                m0 = GRID_W - WIN_C
                act.dma_start(rpb_pad[:, m0:m0 + DC_ALL], rpb.rearrange("l h r c -> (l h r) c")).then_inc(bias_made, 16)
                act.wait_ge(x_here, 16 * TT)
                squares([(tt, x[:, tt], yn[:, tt]) for tt in range(TT)])

            @block.tensor
            def _(pe):
                pe.wait_ge(setup_in, 16 * (1 + L * (len(GC) + 3)))
                nc.tensor.transpose(bank(0)[:, 0:L * NG], grow[0:L * NG, :], ident[0:L * NG, 0:L * NG]
                                    ).then_inc(setup_c, 1)

            @block.vector
            def _(dve):
                dve.wait_ge(setup_c, 1)
                nc.vector.tensor_copy(gall[:, :], bank(0)[:, 0:L * NG])

        proj = arena[:, 0:YN].rearrange("p (s a n) -> p s a n", s=8, a=TT)
        ckv = proj[:, 0, :, 0:KV_LORA]
        kpe = proj[:, 0, :, KV_LORA:KV_LORA + ROPE]
        cq = proj[:, 1]
        nqt = arena[:, YN:YN + 2048].rearrange("p (h t) -> p h t", h=8)
        nkt = arena[:, YN + 2048:YN + 4096].rearrange("p (h t) -> p h t", h=8)
        sbuf_s = arena[:, REST:REST + 2048].rearrange("p (b h k) -> p b h k", b=2, h=4)
        sbuf_p = arena[:, REST + 2048:REST + 4096].rearrange("p (b h c q) -> p b h c q", b=2, h=4, c=2)
        nat_o = arena[:, 2048:4096].rearrange("p (a n) -> p a n", a=TT)
        bias = stage[:, 0:NH * NDR * GRID_W].rearrange("p (h m) -> p h m", h=NH)
        bias_rows = stage[:, 0:NH * NDR * GRID_W].rearrange("p (h r k) -> p h r k", h=NH, r=NDR)
        cqn = arena[:, 4096:5120].rearrange("p (a n) -> p a n", a=TT)
        ckvn = arena[:, 5120:5632].rearrange("p (a n) -> p a n", a=TT)
        q_mla = arena[:, YN:YN + 3072].rearrange("p (a n) -> p a n", a=TT)
        kv_mla = arena[:, 4096:8192].rearrange("p (a n) -> p a n", a=TT)
        qpe = arena[:, YN + 3072:YN + 4096].rearrange("p (a h f) -> p a h f", a=TT, h=MH)
        mla_o = arena[:, YN:YN + 2048].rearrange("p (a n) -> p a n", a=TT)
        qnt = stage[:, 0:2048].rearrange("p (h t) -> p h t", h=MH)
        qpt = stage[:, 2048:3072].rearrange("p (h t) -> p h t", h=4)
        knt = stage[:, 3072:5120].rearrange("p (h t) -> p h t", h=MH)
        kpt = stage[:, 5120:5376]
        kpr = stage[:, 5376:5632].rearrange("p (a b f) -> p a b f", a=TT, b=2)
        rt1 = stage[:, 5632:6144].rearrange("p (a h f) -> p a h f", a=TT, h=MH)
        rt2 = stage[:, 6144:6656].rearrange("p (a h f) -> p a h f", a=TT, h=MH)

        SCALE = float(NOPE + ROPE) ** -0.5
        NB = 8
        MB = 4
        U_UQ, U_UKV, U_OUT = 8 * DC, 8 * DC + 12, 8 * DC + 20
        N_UQ, N_UKV, N_OUT = 32, 35, 37

        QH, KVH = NOPE + ROPE, NOPE + MV

        def k_head(h, tt):
            return kv_mla[:, tt, h * KVH:h * KVH + NOPE]

        def v_head(h, tt):
            return kv_mla[:, tt, h * KVH + NOPE:(h + 1) * KVH]

        norm_x = [(0, quarter(yn, q), quarter(x, q)) for q in range(4)]
        norm_latents = [(0, lambda tt: cqn[:, tt], lambda tt: cq[:, tt]),
                        (2, lambda tt: ckvn[:, tt], lambda tt: ckv[:, tt])]
        norm_mixed = [(c, quarter(rows, q), quarter(rows, q)) for c, rows in ((0, mla_o), (2, nat_o))
                      for q in range(2)]
        norm_ffn = [(0, lambda tt, q=q: yn[:, tt, q * SL:(q + 1) * SL].rearrange("p (b a r) -> p b a r", a=4, b=4),
                     lambda tt, q=q: x[:, tt, q * SL:(q + 1) * SL].rearrange("p (a b r) -> p b a r", a=4, b=4))
                    for q in range(4)]

        q_peer = arena[:, 0:TT * D].rearrange("p (a n) -> p a n", a=TT)
        q_peer_t = arena[:, 4096:8192].rearrange("p (b t) -> p b t", t=T)
        w_view = arena[:, :].rearrange("p (j t) -> p j t", t=T)
        score_rows = stage[:, 0:4096]
        scores = score_rows.rearrange("p (a b n) -> p a b n", a=TT, b=2 * PH)
        keys_rows = stage[:, 5888:6144].rearrange("p (l s d) -> p l s d", l=1, s=2)
        keys_t = stage[:, 4096:4352]
        work, cand, pick = (stage[:, c:c + 512].rearrange("p (a n) -> p a n", a=2) for c in (4096, 4608, 5120))
        pick = pick.rearrange("p a (k j) -> p a k j", k=TOPK)
        small = stage[:, 5632:5888]
        key_rows = [stage[:, 6144:6400], stage[:, 6400:6656]]
        gate_rows, gates = stage[:, 6656:6912], stage[:, 6912:7168]
        top_v = small[:, 0:32].rearrange("p (a k) -> p a k", a=2)
        top_i = small[:, 32:64].bitcast(U32).rearrange("p (a k) -> p a k", a=2)
        top_if = small[:, 64:96].rearrange("p (a k) -> p a k", a=2)
        best_v = small[:, 96:112]
        best_p = small[:, 112:128].bitcast(U32)
        pos_i = small[:, 128:160].bitcast(U32).rearrange("p (a k) -> p a k", a=2)
        pos_f = small[:, 160:192].rearrange("p (a k) -> p a k", a=2)
        gmax, gsum = per_round[:, 0:TT * PH], per_round[:, TT * PH:2 * TT * PH]
        hot2 = stage[:, 0:2048].bitcast(BF16).rearrange("p (b k t) -> p b k t", b=2, t=BT)
        hotg = stage[:, 2048:5120].bitcast(BF16).rearrange("p (b c k t) -> p b c k t", b=2, c=3, t=BT)
        iota_t = stage[:, 5120:6144].bitcast(BF16).rearrange("p (k t) -> p k t", t=BT)
        rest = score_rows[:, 0:2 * T].rearrange("p (a t) -> p a t", a=2)
        hot1 = stage[:, 6144:7168].bitcast(BF16).rearrange("p (b k t) -> p b k t", b=2, t=BT)

        def u_src(k):
            return piece[:, k // PU].rearrange("p (e b r) -> p b e r", e=GJ * 4, b=4)[:, k % PU]

        def pool_count(half, g, k):
            return half * U_POOL + g * (DC // VL * (VL - 1)) + k // VL * (VL - 1) + k % VL

        def u_view(unit):
            return unit.rearrange("p (e r) -> p e r", r=32)

        def gated(i, b):
            return (w_view[:, :, bass.ds((i * 2 + b) * BT, BT)],
                    bank(2 * b, 2).rearrange("p (t j) -> p j t", t=BT))

        gates_out = ga[:, 0].rearrange("p a n -> p (a n)").rearrange("p (j t) -> p j t", t=BT)

        def g_count(g):
            return g[0] * GROUPS + g[1]

        def g_units(g):
            return g[0] * U_HALF + g[1] * DC

        def latent_src(s, k):
            if s < 3:
                return unit_src(N_UQ + s, k)
            c = k * 2 * SL + ((s - 3) % 2) * SL
            return piece[:, (N_UKV + (s - 3) // 2) % NP, c:c + SL]

        def heads_dst(i):
            if i < 4:
                return qnt[:, 2 * i:2 * i + 2].rearrange("p h t -> p (h t)"), SL
            if i < 8:
                return knt[:, 2 * (i - 4):2 * (i - 4) + 2].rearrange("p h t -> p (h t)"), SL
            if i < 10:
                return qpt[:, 2 * (i - 8):2 * (i - 8) + 2].rearrange("p h t -> p (h t)"), SL
            return kpt, T

        def score_at(b, h):
            c = 2 * (h % 2) + h // 2
            return bank(2 * (b % 2), 2)[:, c * T:(c + 1) * T]

        def attention_act(act, b0, count, mla):
            def probs(b):
                if b >= b0 + 2:
                    act.wait_ge(S["probs_turned"], b - 1)
                act.wait_ge(S["maxed"], b + 1)
                for h in range(4):
                    src = score_at(b, h) if mla else sbuf_s[:, b % 2, h]
                    ins = nc.scalar.activation(sbuf_s[:, b % 2, h], src, ACT.Exp,
                                               bias=mx[:, b % 2, h:h + 1], scale=SCALE if mla else 1.0,
                                               accum_out=den[:, b % 2, h:h + 1])
                ins.then_inc(S["expd"], 1)

            def turned(b):
                act.wait_ge(S["probs_turned"], b + 1)
                if b >= b0 + 2:
                    act.wait_ge(S["mixed"], b - 1)
                nc.scalar.activation(sbuf_p[:, b % 2].rearrange("p h c q -> p (h c q)"), bank(4, 2),
                                     ACT.Copy).then_inc(S["probs_read"], 1)

            for b in range(b0, b0 + count + 1):
                if b < b0 + count:
                    probs(b)
                if b > b0:
                    turned(b - 1)

        def attention_dve(dve, b0, count, mla, chain):
            def maxima(b):
                dve.wait_ge(S["scored"], b + 1)
                i = b - b0
                sc = bank(2 * (b % 2), 2).rearrange("p (o e k) -> p e o k", o=2, e=2)
                if not mla:
                    if b >= b0 + 2:
                        dve.wait_ge(S["probs_turned"], b - 1)
                    tt, h0 = i // 4, 4 * (i % 4)
                    r0 = (2 - 2 * tt) * GRID_W
                    for o in range(2):
                        ins = nc.vector.scalar_tensor_tensor(
                            sbuf_s[:, b % 2, o::2], bank(2 * (b % 2) + o).rearrange("p (e k) -> p e k", e=2),
                            float(ND) ** -0.5, bias[:, h0 + o:h0 + 4:2, r0:r0 + T], ALU.mult, ALU.add)
                    chain(ins)
                    chain(nc.vector.tensor_reduce(smax[:, b % 2, :], sbuf_s[:, b % 2], AX.X, ALU.max))
                else:
                    chain(nc.vector.tensor_reduce(smax[:, b % 2, :].rearrange("p (e o) -> p e o", o=2), sc, AX.X,
                                                  ALU.max))
                nc.vector.tensor_scalar(mx[:, b % 2, :], smax[:, b % 2, :], -(SCALE if mla else 1.0), None,
                                        ALU.mult).then_inc(S["maxed"], 1)

            def normalise(b):
                dve.wait_ge(S["mixed"], b + 1)
                i = b - b0
                w = MV if mla else ND
                tt, h0 = (i // 2, 4 * (i % 2)) if mla else (i // 4, 4 * (i % 4))
                dst = (mla_o if mla else nat_o)[:, tt, h0 * w:(h0 + 4) * w].rearrange("p (h d) -> p h d", h=4)
                nc.vector.tensor_tensor(dst, bank(6 + b % 2)[:, 0:4 * w].rearrange("p (h d) -> p h d", h=4),
                                        rden[:, b % 2, :].unsqueeze(2).to_broadcast([P, 4, w]),
                                        ALU.mult).then_inc(S["attended"], 1)

            for b in range(b0, b0 + count + 2):
                if b >= b0 + 2:
                    dve.wait_ge(S["expd"], b - 1)
                    chain(nc.vector.reciprocal(rden[:, b % 2, :], den[:, b % 2, :]))
                if b < b0 + count:
                    maxima(b)
                if b >= b0 + 2:
                    normalise(b - 2)

        def attention_pe(pe, b0, count, scores, v_of, w, mla):
            for b in range(b0, b0 + count + 2):
                if b < b0 + count:
                    if b >= b0 + 2:
                        pe.wait_ge(S["expd" if mla else "maxed"], b - 1)
                    outs = [score_at(b, h) for h in range(4)]
                    scores(b - b0, outs).then_inc(S["scored"], 1)
                if b0 + 1 <= b <= b0 + count:
                    a = b - 1
                    pe.wait_ge(S["expd"], a + 1)
                    if a > b0:
                        pe.wait_ge(S["probs_read"], a)
                    for h in range(4):
                        for c in range(2):
                            ins = nc.tensor.transpose(bank(4, 2)[:, (2 * h + c) * P:(2 * h + c + 1) * P],
                                                      sbuf_s[:, a % 2, h, c * P:(c + 1) * P], ident)
                    ins.then_inc(S["probs_turned"], 1)
                if b >= b0 + 2:
                    a = b - 2
                    pe.wait_ge(S["probs_read"], a + 1)
                    if a >= b0 + 2:
                        pe.wait_ge(S["attended"], a - 1)
                    for h in range(4):
                        for c in range(2):
                            ins = nc.tensor.matmul(bank(6 + a % 2)[:, h * w:(h + 1) * w],
                                                   sbuf_p[:, a % 2, h, c], v_of(a - b0, h, c),
                                                   start=(c == 0), stop=(c == 1))
                    ins.then_inc(S["mixed"], 1)

        with nc.Fori(0, L) as layer:
            with nc.Block() as block:
                @block.sync
                def _(sp):
                    wl = w_in.rearrange("l (c p) n -> p l c n", p=P)

                    def w_piece(n, slot, q, col, w, wait=True):
                        dst = piece[:, slot, 0:PU * w].rearrange("p (l c n) -> p l c n", l=1, c=PU)
                        if wait:
                            sp.wait_ge(S["lo_ready"], PU * (n - NP + 1))
                        sp.dma_start(dst, wl[:, bass.ds(layer, 1), q * PU:(q + 1) * PU, col]
                                     ).then_inc(S[f"arrived{slot}"], 16)

                    for q in range(4):
                        w_piece(q, q, q, slice(Q_LORA, NAT0), NAT0 - Q_LORA, wait=False)
                    for q in range(4):
                        w_piece(4 + q, q, q, slice(0, Q_LORA), SL)
                    pad_rows = rpb_pad.rearrange("(l h r) m -> l h r m", h=NH, r=DR_ALL)
                    sp.wait_ge(bias_made, 16 * 2)

                    def skew(r):
                        src = pad_rows[bass.ds(layer, 1), :, bass.ds(r + WIN_R - ROWS, 1), 0:P - 1].rearrange(
                            "l h r m -> (l h) r m").to_broadcast([NH, GRID_W, P - 1])
                        dst = skewed[:, bass.ds(r, 1)].rearrange("h r c m -> h (r c) m")
                        sp.dma_start(dst, src).then_inc(S["bias_skewed"], 16)

                    def nat_pieces(s):
                        for q in range(4):
                            w_piece(8 + s * 4 + q, q, q, bass.ds(NAT0 + s * SL, SL), SL)

                    row = GRID_W * (P - 1)

                    def bias_part(par):
                        for r in range(NDR):
                            src = bass.AP(skewed.tensor, (r + 1 - par) * row + GRID_W - 1,
                                          [[P - 2, GRID_W], [(NDR + 1) * row, NH], [1, GRID_W]])
                            sp.dma_start(bias_rows[par * GRID_W:(par + 1) * GRID_W, :, r], src
                                         ).then_inc(S["bias_in"], 16)

                    with sp.Fori(0, 3) as s:
                        nat_pieces(s)
                        skew(2 * s)
                        skew(2 * s + 1)
                    skew(NDR)
                    nat_pieces(3)
                    sp.wait_ge(S["bias_skewed"], 16 * (NDR + 1))
                    bias_part(0)
                    nat_pieces(4)
                    bias_part(1)
                    nat_pieces(5)
                    uq = w_uq.rearrange("l (c p) n -> p l c n", p=P)
                    for s in range(3):
                        n = N_UQ + s
                        sp.wait_ge(S["lo_ready"], PU * (n - NP + 1))
                        sp.dma_start(piece[:, n % NP, :].rearrange("p (l c n) -> p l c n", l=1, c=4),
                                     uq[:, bass.ds(layer, 1), :, s * SL:(s + 1) * SL]
                                     ).then_inc(S[f"arrived{n % NP}"], 16)
                    ukv = w_ukv.rearrange("l (c p) n -> p l c n", p=P)
                    for s in range(2):
                        n = N_UKV + s
                        sp.wait_ge(S["lo_ready"], PU * (n - NP + 1))
                        sp.dma_start(piece[:, n % NP, :].rearrange("p (l c n) -> p l c n", l=1, c=2),
                                     ukv[:, bass.ds(layer, 1), :, s * 1024:(s + 1) * 1024]
                                     ).then_inc(S[f"arrived{n % NP}"], 16)
                    wo = w_out.rearrange("l (c p) n -> p l c n", p=P)
                    with sp.Fori(0, 4) as s:
                        for q in range(4):
                            slot = (N_OUT + q) % NP
                            sp.wait_ge(S["lo_ready"], PU * (N_OUT + s * 4 + q - NP + 1))
                            sp.dma_start(piece[:, slot, :].rearrange("p (l c n) -> p l c n", l=1, c=PU),
                                         wo[:, bass.ds(layer, 1), q * PU:(q + 1) * PU, bass.ds(s * SL, SL)]
                                         ).then_inc(S[f"arrived{slot}"], 16)

                @block.gpsimd
                def _(pool):
                    pool.wait_ge(S["bias_in"], 16 * 2 * NDR)
                    b3 = stage[:, 0:NH * NDR * GRID_W].rearrange("p (m k) -> p m k", k=GRID_W)
                    nc.gpsimd.tensor_tensor(b3, b3, mask.unsqueeze(1).to_broadcast([P, NH * NDR, GRID_W]), ALU.add
                                            ).then_inc(S["bias_masked"], 1)

                @block.scalar
                def _(act):
                    roots(act, 1, 2)
                    chunk = scale_second(act, 1, norm_x, 0, GC["attn"])

                    def first_unit(k):
                        if k % PU == 0:
                            piece_here(act, k // PU, k // PU)
                        unit_high(act, k, k, unit_src(k // PU, k % PU, NAT0 - Q_LORA), NAT0 - Q_LORA, k >= R)

                    with_chunks("scalar", DC, DC, chunk, first_unit)
                    slice_high(act, DC, 4, 0, 0, SL)

                    def evacuate(s, first, w=SL):
                        act.wait_ge(S["unit_used"], (s + 1) * DC)
                        dst = proj[:, s] if isinstance(s, int) else arena[:, bass.ds(s * 1024, 1024)].rearrange(
                            "p (a n) -> p a n", a=TT)
                        nc.scalar.activation(dst[:, :, 0:w], bank(2 * first, 2).rearrange(
                            "p (a n) -> p a n", a=TT)[:, :, 0:w], ACT.Copy).then_inc(S["slice_out"], 1)

                    evacuate(0, 0, NAT0 - Q_LORA)
                    with act.Fori(0, 3) as i:
                        for b in range(2):
                            s = 2 + i * 2 + b
                            for k in range(DC):
                                if k % PU == 0:
                                    piece_here(act, k // PU, 4 * s + k // PU)
                                unit_high(act, s * DC + k, k, unit_src(k // PU, k % PU), SL)
                                if k == 2:
                                    evacuate(s - 1, 1 - b)
                    evacuate(7, 1)
                    for i in range(8):
                        act.wait_ge(S["bank_full"], i + 1)
                        dst = (nqt if i < 4 else nkt)[:, 2 * (i % 4):2 * (i % 4) + 2].rearrange("p h t -> p (h t)")
                        nc.scalar.activation(dst, bank(4 + i % 4), ACT.Copy).then_inc(S["bank_read"], 1)
                    attention_act(act, 0, NB, False)
                    squares([(tt, cq[:, tt], cqn[:, tt]) for tt in range(TT)]
                            + [(2 + tt, ckv[:, tt], ckvn[:, tt]) for tt in range(TT)]).then_inc(S["squared"], 1)
                    roots(act, 2, 4)
                    chunk = scale_second(act, 2, norm_latents, DC, GC["q"])

                    def latent_out(s):
                        act.wait_ge(S["unit_used"], U_UQ + 4 * (s + 1) if s < 3 else U_UKV + 2 * (s - 2))
                        dst = q_mla[:, :, s * SL:(s + 1) * SL] if s < 3 else kv_mla[:, :, (s - 3) * SL:(s - 2) * SL]
                        nc.scalar.activation(dst, bank(2 * (s % 4), 2).rearrange("p (a n) -> p a n", a=TT),
                                             ACT.Copy).then_inc(S["slice_out"], 1)

                    for s in range(7):
                        n = N_UQ + s if s < 3 else N_UKV + (s - 3) // 2
                        if s < 3 or s % 2 == 1:
                            piece_here(act, n % NP, n)
                        if s == 0:
                            with_chunks("scalar", 6, 4, chunk,
                                        lambda k: unit_high(act, U_UQ + k, U_UQ + k, latent_src(0, k), SL))
                            continue
                        for k in range(4 if s < 3 else 2):
                            u = U_UQ + 4 * s + k if s < 3 else U_UKV + 2 * (s - 3) + k
                            unit_high(act, u, u, latent_src(s, k), SL)
                        if s >= 1:
                            latent_out(s - 1)
                    latent_out(6)
                    for i in range(11):
                        act.wait_ge(S["bank_full"], 8 + i + 1)
                        dst, w = heads_dst(i)
                        nc.scalar.activation(dst, bank(4 + i % 4)[:, 0:w], ACT.Copy).then_inc(S["bank_read"], 1)
                    squares([(2 + tt, nat_o[:, tt], arena[:, tt * W_MIX:(tt + 1) * W_MIX]) for tt in range(TT)])
                    attention_act(act, NB, MB, True)
                    act.wait_ge(S["attended"], NB + MB)
                    squares([(tt, mla_o[:, tt], kv_mla[:, 0, tt * W_MIX:(tt + 1) * W_MIX]) for tt in range(TT)]
                            ).then_inc(S["squared"], 1)
                    roots(act, 3, 4)
                    chunk = scale_second(act, 3, norm_mixed, DC + 6, GC["mla"])

                    def out_unit(s, k):
                        if k % PU == 0:
                            piece_here(act, (N_OUT + k // PU) % NP, N_OUT + 4 * s + k // PU)
                        unit_high(act, U_OUT + s * DC + k, U_OUT + k, unit_src(N_OUT + k // PU, k % PU), SL)

                    with_chunks("scalar", DC, DC, chunk,
                                lambda k: out_unit(0, k))
                    with act.Fori(1, 4) as s:
                        for k in range(DC):
                            out_unit(s, k)
                    for tt in range(TT):
                        act.wait_ge(S["x_added"], 3 + tt + 1)
                        squares([(tt, x[:, tt], yn[:, tt])])

                @block.vector
                def _(dve):
                    chain = chainer(dve, S["chain_v"])
                    chain(nc.vector.tensor_copy(gcol[:, :], gall[:, bass.ds(layer * NG, NG)]))
                    means(dve, 0, [(0, 2, D)])
                    scale_first(dve, 1, 2, norm_x, chain)
                    with_chunks("vector", DC, DC, lambda i: chunk_low(dve, i, i, GC["attn"] + i),
                                lambda k: unit_low(dve, k, k, unit_src(k // PU, k % PU, NAT0 - Q_LORA), NAT0 - Q_LORA))
                    slice_low(dve, DC, 0, 0, SL)
                    with dve.Fori(0, 6) as s:
                        slice_low(dve, 2 * DC + s * DC, 0, 0, SL)
                    dve.wait_ge(S["bias_masked"], 1)
                    attention_dve(dve, 0, NB, False, chain)
                    means(dve, 1, [(0, 2, Q_LORA), (2, 4, KV_LORA)])
                    scale_first(dve, 2, 4, norm_latents, chain)
                    with_chunks("vector", 6, 4, lambda i: chunk_low(dve, DC + i, i, GC["q"] + i),
                                lambda k: unit_low(dve, U_UQ + k, U_UQ + k, latent_src(0, k), SL))
                    for s in range(1, 7):
                        for k in range(4 if s < 3 else 2):
                            u = U_UQ + 4 * s + k if s < 3 else U_UKV + 2 * (s - 3) + k
                            unit_low(dve, u, u, latent_src(s, k), SL)
                    def rotate(parts):
                        for f, s, c, n, of, os_, a, b in parts:
                            nc.vector.tensor_tensor(a, f, c, ALU.mult)
                            ins = nc.vector.tensor_tensor(b, s, n, ALU.mult)
                        chain(ins)
                        for f, s, c, n, of, os_, a, b in parts:
                            ins = nc.vector.tensor_tensor(of, a, b, ALU.subtract)
                        chain(ins)
                        for f, s, c, n, of, os_, a, b in parts:
                            nc.vector.tensor_tensor(a, s, c, ALU.mult)
                            ins = nc.vector.tensor_tensor(b, f, n, ALU.mult)
                        chain(ins)
                        for f, s, c, n, of, os_, a, b in parts:
                            ins = nc.vector.tensor_tensor(os_, a, b, ALU.add)
                        chain(ins)

                    HR = ROPE // 2
                    rotate([(kpe[:, :, 0:HR], kpe[:, :, HR:ROPE], cos, sin, kpr[:, :, 0, 0:HR], kpr[:, :, 0, HR:ROPE],
                             rt1[:, :, 0], rt2[:, :, 0])])
                    chain(nc.vector.tensor_copy(kpr[:, :, 1], kpr[:, :, 0]))
                    dve.wait_ge(S["slice_out"], 8 + 3)
                    parts = []
                    for h in range(MH):
                        c = h * QH + NOPE
                        parts.append((q_mla[:, :, c:c + HR], q_mla[:, :, c + HR:c + ROPE], cos, sin,
                                      qpe[:, :, h, 0:HR], qpe[:, :, h, HR:ROPE], rt1[:, :, h], rt2[:, :, h]))
                    rotate(parts)
                    dve.sem_inc(S["rope_ready"], 1)
                    attention_dve(dve, NB, MB, True, chain)
                    means(dve, 2, [(0, 4, W_MIX)])
                    scale_first(dve, 3, 4, norm_mixed, chain)
                    def add_slice(s, tt0, tt1):
                        xs = x[:, tt0:tt1, bass.ds(s * SL, SL)]
                        src = ps[:, bass.ds(s * (2 * SL), 2 * SL)].rearrange("p (a n) -> p a n", a=TT)[:, tt0:tt1]
                        nc.vector.tensor_tensor(xs, src, xs, ALU.add).then_inc(S["x_added"], 1)

                    def out_unit(s, k):
                        unit_low(dve, U_OUT + s * DC + k, U_OUT + k, unit_src(N_OUT + k // PU, k % PU), SL)

                    with_chunks("vector", DC, DC, lambda i: chunk_low(dve, DC + 6 + i, i, GC["mla"] + i),
                                lambda k: out_unit(0, k))
                    with dve.Fori(1, 4) as s:
                        for k in range(DC):
                            out_unit(s, k)
                            if k == 4:
                                dve.wait_ge(S["unit_used"], U_OUT + s * DC)
                                add_slice(s - 1, 0, TT)
                    dve.wait_ge(S["unit_used"], U_OUT + 4 * DC)
                    for tt in range(TT):
                        add_slice(3, tt, tt + 1)

                @block.tensor
                def _(pe):
                    first_products(pe, 0, 0, 0, DC, DC,
                                   [lambda tt, c=c: yn[:, tt, c * P:(c + 1) * P] for c in range(DC)],
                                   NAT0 - Q_LORA)
                    slice_product(pe, DC, 0, [bank(2 + tt) for tt in range(TT)], SL)
                    with pe.Fori(0, 3) as i:
                        for b in range(2):
                            s = 2 + i * 2 + b
                            pe.wait_ge(S["slice_out"], s - 1)
                            slice_product(pe, s * DC, 0, [bank(2 * b + tt) for tt in range(TT)], SL)
                    pe.wait_ge(S["slice_out"], 8)
                    for i in range(8):
                        if i >= 4:
                            pe.wait_ge(S["bank_read"], i - 3)
                        for k in range(4):
                            pair, tt = 2 * (i % 4) + k // 2, k % 2
                            src = proj[:, (2 if i < 4 else 4) + pair // 4, tt, (pair % 4) * P:(pair % 4 + 1) * P]
                            ins = nc.tensor.transpose(bank(4 + i % 4)[:, k * P:(k + 1) * P], src, ident)
                        ins.then_inc(S["bank_full"], 1)
                    pe.wait_ge(S["bank_read"], 8)

                    def nat_scores(i, outs):
                        tt, h0 = i // 4, 4 * (i % 4)
                        for h in range(4):
                            pair, r0 = (h0 + h) // 2, ((h0 + h) % 2) * ND
                            ins = nc.tensor.matmul(outs[h], nqt[r0:r0 + ND, pair, tt * P:(tt + 1) * P],
                                                   nkt[r0:r0 + ND, pair, :], start=True, stop=True)
                        return ins

                    def nat_v(i, h, c):
                        hh = 4 * (i % 4) + h
                        return proj[:, 6 + hh // 8, c, (hh % 8) * ND:(hh % 8 + 1) * ND]

                    attention_pe(pe, 0, NB, nat_scores, nat_v, ND, False)
                    first_products(pe, 4, DC, U_UQ, 6, 4,
                                   [lambda tt, c=c: cqn[:, tt, c * P:(c + 1) * P] for c in range(4)]
                                   + [lambda tt, c=c: ckvn[:, tt, c * P:(c + 1) * P] for c in range(2)], SL)
                    pe.wait_ge(S["chunk_lo"], DC + 6)
                    for s in range(1, 3):
                        for k in range(4):
                            u = U_UQ + 4 * s + k
                            unit_product(pe, u, u, ht_hi[:, k], ht_lo[:, k], [bank(2 * s + tt) for tt in range(TT)],
                                         SL, k == 0, k == 3)
                    for s in range(4):
                        if s >= 1:
                            pe.wait_ge(S["slice_out"], 8 + s)
                        for c in range(2):
                            u = U_UKV + 2 * s + c
                            unit_product(pe, u, u, ht_hi[:, 4 + c], ht_lo[:, 4 + c],
                                         [bank(2 * ((3 + s) % 4) + tt) for tt in range(TT)], SL, c == 0, c == 1)
                    pe.wait_ge(S["slice_out"], 8 + 7)
                    for i in range(11):
                        if i == 8:
                            pe.wait_ge(S["rope_ready"], 1)
                        if i >= 4:
                            pe.wait_ge(S["bank_read"], 8 + i - 3)
                        for k in range(4 if i < 10 else 2):
                            tt = k % 2
                            o = bank(4 + i % 4)[:, k * P:(k + 1) * P]
                            if i < 4:
                                h = 2 * i + k // 2
                                ins = nc.tensor.transpose(o, q_mla[:, tt, h * QH:h * QH + NOPE], ident)
                            elif i < 8:
                                ins = nc.tensor.transpose(o, k_head(2 * (i - 4) + k // 2, tt), ident)
                            elif i < 10:
                                hp = 2 * (i - 8) + k // 2
                                ins = nc.tensor.transpose(
                                    o, qpe[:, tt, 2 * hp:2 * hp + 2].rearrange("p h f -> p (h f)"), ident)
                            else:
                                ins = nc.tensor.transpose(o, kpr[:, tt].rearrange("p b f -> p (b f)"), ident)
                        ins.then_inc(S["bank_full"], 1)
                    pe.wait_ge(S["bank_read"], 8 + 11)

                    def mla_scores(i, outs):
                        tt, h0 = i // 2, 4 * (i % 2)
                        for h in range(4):
                            hh = h0 + h
                            r0 = (hh % 2) * ROPE
                            nc.tensor.matmul(outs[h], qnt[:, hh, tt * P:(tt + 1) * P], knt[:, hh, :],
                                             start=True, stop=False)
                            ins = nc.tensor.matmul(outs[h], qpt[r0:r0 + ROPE, hh // 2, tt * P:(tt + 1) * P],
                                                   kpt[r0:r0 + ROPE, :], start=False, stop=True)
                        return ins

                    attention_pe(pe, NB, MB, mla_scores, lambda i, h, c: v_head(4 * (i % 2) + h, c), MV, True)
                    first_products(pe, 6, DC + 6, U_OUT, DC, DC,
                                   [lambda tt, c=c: mla_o[:, tt, c * P:(c + 1) * P] for c in range(8)]
                                   + [lambda tt, c=c: nat_o[:, tt, c * P:(c + 1) * P] for c in range(8)], SL)
                    with pe.Fori(1, 4) as s:
                        outs = [ps[:, bass.ds(s * (2 * SL) + tt * SL, SL)] for tt in range(TT)]
                        for k in range(DC):
                            unit_product(pe, U_OUT + s * DC + k, U_OUT + k, ht_hi[:, k], ht_lo[:, k], outs, SL,
                                         k == 0, k == DC - 1)

            nc.all_engine_barrier(sems_to_clear=cleared)
            with nc.Block() as block:
                @block.sync
                def _(sp):
                    sp.dma_start(keys_rows, keys.rearrange("l s n d -> n l s d")[:, bass.ds(layer, 1)]
                                 ).then_inc(S["keys_in"], 16)
                    wq = w_q.rearrange("l (q a b r) n -> q a r l b n", q=4, a=4, b=4)
                    ut = u_tab.rearrange("l (e i) (q a c) -> q a i l e c", i=32, q=4, a=4)
                    vt = v_tab.rearrange("l (j p) d -> p l j d", p=P)

                    def put(slot, part, c):
                        for a in range(4):
                            rows = piece[a * 32:(a + 1) * 32, slot, :]
                            sp.dma_start(rows.rearrange("p (l c n) -> p l c n", l=1, c=c), part(a)
                                         ).then_inc(S[f"arrived{slot}"], 16)

                    ly = bass.ds(layer, 1)
                    for q in range(4):
                        put(q, lambda a: wq[q, a][:, ly, :, 0:SL], PU)
                    with sp.Fori(1, 4) as s:
                        for q in range(4):
                            sp.wait_ge(S["lo_ready"], (s - 1) * DC + (q + 1) * PU)
                            put(q, lambda a: wq[q, a][:, ly, :, bass.ds(s * SL, SL)], PU)
                    with sp.Fori(0, 2) as half:
                        def u_part(g, q):
                            return lambda a: ut[q, a][:, ly, bass.ds((half * HALF_J + g * GJ) * 4, GJ * 4)]

                        def put_v(g, q):
                            sp.dma_start(piece[:, q, :].rearrange("p (l c n) -> p l c n", l=1, c=1),
                                         vt[:, ly, bass.ds(half * HALF_J + g * 4 + q, 1), :]
                                         ).then_inc(S[f"arrived{q}"], 16)

                        for q in range(4):
                            sp.wait_ge(S["lo_ready"], U_A + half * U_HALF - (NP - q - 1) * PU)
                            put(q, u_part(0, q), GJ * 4)
                        with sp.Fori(1, GROUPS) as g:
                            for q in range(4):
                                sp.wait_ge(S["pool_lo_ready"], pool_count(half, g - 1, q * PU + PU - 1))
                                put(q, u_part(g, q), GJ * 4)
                        for q in range(4):
                            sp.wait_ge(S["pool_lo_ready"], pool_count(half, GROUPS - 1, q * PU + PU - 1))
                            put_v(0, q)
                        with sp.Fori(1, GROUPS) as g:
                            for q in range(4):
                                sp.wait_ge(S["lo_ready"], U_A + half * U_HALF + U_AHALF
                                           + (g - 1) * (4 * PU) + (q + 1) * PU)
                                put_v(g, q)

                @block.gpsimd
                def _(pool):
                    with pool.Fori(0, 2) as half:
                        with pool.Fori(0, GROUPS) as g:
                            for k in range(DC):
                                if k % VL == 0:
                                    continue
                                u = U_A + half * U_HALF + g * DC + k
                                pool.wait_ge(S["hi_ready"], u + 1)
                                if k % PU == PU - 1:
                                    pool.wait_ge(S["lo_ready"], u + 1)
                                nc.gpsimd.tensor_tensor(u_view(unit_lo[:, k % R]), u_src(k),
                                                        u_view(unit_hi[:, k % R].bitcast(F32)), ALU.subtract
                                                        ).then_inc(S["pool_lo_ready"], 1)
                        with pool.Fori(0, BATCHES // 2) as i:
                            pool.wait_ge(S["gates_copied"], half * (BATCHES // 2) + i + 1 + 1)
                            w3 = gated(i, 1)[0]
                            nc.gpsimd.tensor_tensor(w3, gates_out, w3, ALU.mult).then_inc(S["odd_gated"], 1)

                @block.scalar
                def _(act):
                    act.sem_inc(S["gelu_done"], 2)
                    act.sem_inc(S["w_stored"], 1)
                    roots(act, 1, 2)
                    chunk = scale_second(act, 1, norm_ffn, 0, GC["ffn"])

                    def first_unit(k):
                        if k % PU == 0:
                            piece_here(act, k // PU, k // PU, 4)
                        unit_high(act, k, k, unit_src(k // PU, k % PU), SL, k >= R)

                    with_chunks("scalar", DC, DC, chunk, first_unit)
                    with act.Fori(1, 4) as s:
                        slice_high(act, s * DC, s * 4, 0, 0, SL, parts=4)
                    for s in range(4):
                        act.wait_ge(S["unit_used"], (s + 1) * DC)
                        nc.scalar.activation(q_peer[:, :, s * SL:(s + 1) * SL],
                                             bank(2 * s, 2).rearrange("p (a n) -> p a n", a=TT), ACT.Copy
                                             ).then_inc(S["q_out"], 1)
                    for i in range(9):
                        act.wait_ge(S["qt_full"], i + 1)
                        if i < 8:
                            dst = q_peer_t[:, 2 * i:2 * i + 2].rearrange("p b t -> p (b t)")
                            nc.scalar.activation(dst, bank(i), ACT.Copy).then_inc(S["qt_read"], 1)
                        else:
                            nc.scalar.activation(keys_t, bank(0)[:, 0:2 * NK], ACT.Copy).then_inc(S["qt_read"], 1)
                    for i in range(8):
                        act.wait_ge(S["score_full"], i + 1)
                        nc.scalar.activation(scores[:, i // 4, 4 * (i % 4):4 * (i % 4) + 4].rearrange(
                            "p b n -> p (b n)"), bank(i), ACT.Copy).then_inc(S["score_read"], 1)

                    def gelu(g, par):
                        act.wait_ge(S["unit_used"], U_A + g_units(g) + DC)
                        act.wait_ge(S["gelu_turned"], g_count(g) + 1)
                        for tt in range(TT):
                            ins = nc.scalar.activation(ga[:, par, tt], bank(2 * par + tt), ACT.Gelu)
                        ins.then_inc(S["gelu_done"], 1)

                    def store(g):
                        act.wait_ge(S["gelu_turned"], g_count(g) + 2 + 1)
                        nc.scalar.activation(arena[:, bass.ds(g[1] * (GJ * T), GJ * T)], bank(6, 2), ACT.Copy
                                             ).then_inc(S["w_stored"], 1)

                    def step(half, i, k, tails):
                        g = (half, i * 2 + k // DC)
                        a = i * (2 * DC) + k
                        act.wait_ge(S["unit_used"], U_A + half * U_HALF + a - R + 1)
                        act.wait_ge(S["u_turned"], half * U_AHALF + a + 1)
                        nc.scalar.activation(u_view(unit_hi[:, k % R]), u_src(k % DC), ACT.Copy
                                             ).then_inc(S["hi_ready"], 1)
                        before = (half, g[1] - 1)
                        if tails and k % DC == 2:
                            gelu(before, (k // DC + 1) % 2)
                        if tails and k % DC == 7:
                            store(before)

                    for half in range(2):
                        for k in range(SHIFT):
                            step(half, 0, k, False)
                        with act.Fori(0, PAIRS - 1) as i:
                            for k in range(SHIFT, 2 * DC + SHIFT):
                                step(half, i + k // (2 * DC), k % (2 * DC), True)
                        for k in range(SHIFT, 2 * DC):
                            step(half, PAIRS - 1, k, True)
                        if half == 0:
                            act.wait_ge(S["ranked"], 1)
                            nc.scalar.activation(gates, gate_rows, ACT.Exp).then_inc(S["gates_exp"], 1)
                        gelu((half, GROUPS - 1), 1)
                        if half == 0:
                            act.wait_ge(S["small_full"], 1)
                            nc.scalar.activation(i1t[:, :], bank(4)[:, 0:T], ACT.Copy)
                            nc.scalar.activation(i2t[:, :], bank(4)[:, T:2 * T], ACT.Copy).then_inc(S["small_read"], 1)
                        store((half, GROUPS - 1))
                        with act.Fori(0, BATCHES // 2) as i:
                            act.wait_ge(S["gates_made"], half * BATCHES + i * 2 + 1 + 2 + 1)
                            act.wait_ge(S["odd_gated"], half * (BATCHES // 2) + i + 1)
                            nc.scalar.activation(gates_out, gated(i, 1)[1], ACT.Copy).then_inc(S["gates_copied"], 1)
                        act.wait_ge(S["even_gated"], (half + 1) * (BATCHES // 2) + 1)
                        act.wait_ge(S["odd_gated"], (half + 1) * (BATCHES // 2) + 1)
                        with act.Fori(0, GROUPS) as g:
                            for b in range(4):
                                j = g * 4 + b
                                act.wait_ge(S["unit_used"], U_A + half * U_HALF + U_AHALF + (j - 1) * 4)
                                nc.scalar.activation(wj_hi[:, b % 2], arena[:, bass.ds(j * T, T)], ACT.Copy
                                                     ).then_inc(S["wj_hi_ready"], 1)
                                v_here(act, b, half, g)
                                for k in range(4):
                                    unit_high(act, U_A + half * U_HALF + U_AHALF + j * 4 + k, k, unit_src(b, k), SL)
                    for tt in range(TT):
                        act.wait_ge(S["psum_clear"], 1 + 3 + 2 + tt)
                        squares([(tt, x[:, tt], yn[:, tt])])

                @block.vector
                def _(dve):
                    chain = chainer(dve, S["chain_v"])
                    means(dve, 0, [(0, 2, D)])
                    scale_first(dve, 1, 2, norm_ffn, chain)
                    with_chunks("vector", DC, DC, lambda i: chunk_low(dve, i, i, GC["ffn"] + i),
                                lambda k: unit_low(dve, k, k, unit_src(k // PU, k % PU), SL))
                    with dve.Fori(1, 4) as s:
                        slice_low(dve, s * DC, 0, 0, SL)
                    dve.sem_inc(S["even_gated"], 1)
                    dve.sem_inc(S["odd_gated"], 1)
                    dve.sem_inc(S["gates_copied"], 1)

                    def link(n, ins):
                        ins.then_inc(S["rank_chain"], 1)
                        dve.wait_ge(S["rank_chain"], n)

                    def rank(part, r):
                        if part == 0:
                            dve.sem_clear(S["rank_chain"])
                            link(1, nc.vector.tensor_copy(work[:, 0], score_rows[:, bass.ds(r * 2 * NK, 2 * NK)]))
                        elif part == 1:
                            for s in range(2):
                                ins = nc.vector.max(top_v[:, s, 0:8], work[:, 0, s * NK:(s + 1) * NK])
                            link(2, ins)
                        elif part == 2:
                            for s in range(2):
                                nc.vector.max_index(top_i[:, s, 0:8], top_v[:, s, 0:8],
                                                    work[:, 0, s * NK:(s + 1) * NK])
                        elif part == 3:
                            for s in range(2):
                                ins = nc.vector.match_replace(work[:, 1, s * NK:(s + 1) * NK], top_v[:, s, 0:8],
                                                              work[:, 0, s * NK:(s + 1) * NK], NEG)
                            link(3, ins)
                        elif part == 4:
                            for s in range(2):
                                ins = nc.vector.max(top_v[:, s, 8:16], work[:, 1, s * NK:(s + 1) * NK])
                            link(4, ins)
                        elif part == 5:
                            for s in range(2):
                                nc.vector.max_index(top_i[:, s, 8:16], top_v[:, s, 8:16],
                                                    work[:, 1, s * NK:(s + 1) * NK])
                        elif part == 6:
                            link(5, nc.vector.tensor_tensor(
                                cand[:, 0].rearrange("p (a b) -> p a b", a=TOPK),
                                top_v[:, 0].unsqueeze(2).to_broadcast([P, TOPK, TOPK]),
                                top_v[:, 1].unsqueeze(1).to_broadcast([P, TOPK, TOPK]), ALU.add))
                            nc.vector.tensor_copy(top_if, top_i)
                        elif part == 7:
                            link(6, nc.vector.max(best_v[:, 0:8], cand[:, 0]))
                            nc.vector.max_index(best_p[:, 0:8], best_v[:, 0:8], cand[:, 0])
                        elif part == 8:
                            link(7, nc.vector.match_replace(cand[:, 1], best_v[:, 0:8], cand[:, 0], NEG))
                        elif part == 9:
                            link(8, nc.vector.max(best_v[:, 8:16], cand[:, 1]))
                            link(9, nc.vector.max_index(best_p[:, 8:16], best_v[:, 8:16], cand[:, 1]))
                        elif part == 10:
                            nc.vector.tensor_copy(gate_rows[:, bass.ds(r * TOPK, TOPK)], best_v)
                            nc.vector.tensor_scalar(pos_i[:, 0], best_p, 4, None, ALU.logical_shift_right)
                            link(10, nc.vector.tensor_scalar(pos_i[:, 1], best_p, TOPK - 1, None, ALU.bitwise_and))
                        elif part == 11:
                            link(11, nc.vector.tensor_copy(pos_f, pos_i))
                        elif part == 12:
                            for s in range(2):
                                ins = nc.vector.tensor_tensor(
                                    pick[:, s], iota16.unsqueeze(1).to_broadcast([P, TOPK, TOPK]),
                                    pos_f[:, s].unsqueeze(2).to_broadcast([P, TOPK, TOPK]), ALU.is_equal)
                            link(12, ins)
                        elif part == 13:
                            for s in range(2):
                                ins = nc.vector.tensor_tensor(
                                    pick[:, s], pick[:, s],
                                    top_if[:, s].unsqueeze(1).to_broadcast([P, TOPK, TOPK]), ALU.mult)
                            link(13, ins)
                        elif part == 14:
                            for s in range(2):
                                ins = nc.vector.tensor_reduce(key_rows[s][:, bass.ds(r * TOPK, TOPK)], pick[:, s],
                                                              AX.X, ALU.add)
                            link(14, ins)

                    assert TT * PH == GROUPS, "a round for each group of experts"
                    def turn_unit(half, g, k):
                        if k % PU == 0:
                            u_here(dve, k // PU, half, g)
                        blocks = u_src(k).bitcast(U32)
                        nc.vector.transpose(blocks, blocks).then_inc(S["u_turned"], 1)

                    def u_low(half, g, k):
                        dve.wait_ge(S["hi_ready"], U_A + half * U_HALF + g * DC + k + 1)
                        nc.vector.tensor_tensor(u_view(unit_lo[:, k % R]), u_src(k),
                                                u_view(unit_hi[:, k % R].bitcast(F32)), ALU.subtract
                                                ).then_inc(S["lo_ready"], VL)

                    def u_group(half, g, first=False, ahead=True):
                        for k in range(DC):
                            if k + 2 < DC:
                                if not (first and k + 2 < PU):
                                    turn_unit(half, g, k + 2)
                            elif ahead:
                                turn_unit(half, g + 1, k + 2 - DC)
                            if k % VL == 0 and not (k == 0 and first):
                                u_low(half, g, k)
                            if half == 0:
                                rank(k, g)
                            elif not ahead and k < 6:
                                hot_rows(1, 0, k // 3, k % 3)

                    def selected():
                        r3 = gate_rows.rearrange("p (r k) -> p r k", k=TOPK)
                        chain(nc.vector.tensor_copy(gmax, r3[:, :, 0]))
                        chain(nc.vector.tensor_tensor(
                            r3, r3, gmax.unsqueeze(2).to_broadcast([P, TT * PH, TOPK]), ALU.subtract))
                        dve.sem_inc(S["ranked"], 1)
                        chain(nc.vector.tensor_copy(iota_t, iota[:, :].unsqueeze(2).to_broadcast([P, NK, BT])))
                        g3 = gates.rearrange("p (r k) -> p r k", k=TOPK)
                        dve.wait_ge(S["gates_exp"], 1)
                        chain(nc.vector.tensor_reduce(gsum, g3, AX.X, ALU.add))
                        chain(nc.vector.reciprocal(gmax, gsum))
                        nc.vector.tensor_tensor(g3, g3, gmax.unsqueeze(2).to_broadcast([P, TT * PH, TOPK]), ALU.mult
                                                ).then_inc(S["rows_ready"], 1)
                        dve.wait_ge(S["small_read"], 1)
                        gps = bank(5)[:, 0:T]
                        chain(nc.vector.tensor_copy(gt[:, 0], gps))
                        chain(nc.vector.tensor_tensor(rest[:, 0], gps, gt[:, 0], ALU.subtract))
                        chain(nc.vector.tensor_copy(gt[:, 1], rest[:, 0]))
                        chain(nc.vector.tensor_tensor(rest[:, 1], rest[:, 0], gt[:, 1], ALU.subtract))
                        chain(nc.vector.tensor_copy(gt[:, 2], rest[:, 1]))

                    def hot_rows(half, i, b, part):
                        ts = bass.ds((i * 2 + b) * BT, BT)
                        n = half * BATCHES + i * 2 + b
                        if part == 0:
                            nc.vector.tensor_tensor(
                                hot1[:, b], iota_t[:, half * HALF_J:(half + 1) * HALF_J],
                                i1t[:, ts].unsqueeze(1).to_broadcast([P, HALF_J, BT]), ALU.is_equal
                            ).then_inc(S["hot_chain"], 1)
                        elif part == 1:
                            dve.wait_ge(S["gates_made"], n + 1)
                            nc.vector.tensor_tensor(
                                hot2[:, b], iota_t, i2t[:, ts].unsqueeze(1).to_broadcast([P, NK, BT]), ALU.is_equal)
                            dve.wait_ge(S["hot_chain"], n + 1)
                        else:
                            nc.vector.tensor_tensor(
                                hotg[:, b], hot1[:, b].unsqueeze(1).to_broadcast([P, 3, HALF_J, BT]),
                                gt[:, :, ts].unsqueeze(2).to_broadcast([P, 3, HALF_J, BT]), ALU.mult
                            ).then_inc(S["onehot_rows"], 1)

                    def gate(half, i):
                        dve.wait_ge(S["gates_made"], half * BATCHES + i * 2 + 2 + 1)
                        w3, g3 = gated(i, 0)
                        nc.vector.tensor_tensor(w3, g3, w3, ALU.mult).then_inc(S["even_gated"], 1)

                    turn_unit(0, 0, 0)
                    turn_unit(0, 0, 1)
                    dve.wait_ge(S["score_read"], 8)
                    dve.sem_inc(S["psum_clear"], 1)
                    for half in range(2):
                        if half:
                            u_group(half, 0, first=True)
                        with dve.Fori(half, GROUPS - 1) as g:
                            u_group(half, g)
                        u_group(half, GROUPS - 1, ahead=False)
                        if half == 0:
                            selected()
                            for b in range(2):
                                for part in range(3):
                                    hot_rows(0, 0, b, part)
                        with dve.Fori(0, BATCHES // 2 - 1) as i:
                            for b in range(2):
                                if b == 0:
                                    gate(half, i)
                                for part in range(3):
                                    hot_rows(half, i + 1, b, part)
                        gate(half, BATCHES // 2 - 1)
                        with dve.Fori(0, GROUPS) as g:
                            for b in range(4):
                                j = g * 4 + b
                                dve.wait_ge(S["wj_hi_ready"], half * HALF_J + j + 1)
                                nc.vector.tensor_tensor(wj_lo[:, b % 2], arena[:, bass.ds(j * T, T)],
                                                        wj_hi[:, b % 2].bitcast(F32), ALU.subtract
                                                        ).then_inc(S["wj_lo_ready"], 1)
                                for k in range(4):
                                    unit_low(dve, U_A + half * U_HALF + U_AHALF + j * 4 + k, k, unit_src(b, k), SL)
                        if half == 0:
                            for k in range(PU):
                                turn_unit(1, 0, k)
                            u_low(1, 0, 0)
                        dve.wait_ge(S["unit_used"], U_A + (half + 1) * U_HALF)
                        for b0, n in ((0, 2), (2, 2), (4, 4)):
                            xs = x[:, b0 // 4, b0 % 4 * SL:(b0 % 4 + n) * SL]
                            nc.vector.tensor_tensor(xs, bank(b0, n), xs, ALU.add).then_inc(S["psum_clear"], 1)

                @block.tensor
                def _(pe):
                    pe.sem_inc(S["gelu_turned"], 2)
                    pe.sem_inc(S["gates_made"], 2)
                    first_products(pe, 0, 0, 0, DC, DC,
                                   [lambda tt, c=c: yn[:, tt, c * P:(c + 1) * P] for c in range(DC)],
                                   SL)
                    with pe.Fori(1, 4) as s:
                        outs = [ps[:, bass.ds(s * (2 * SL) + tt * SL, SL)] for tt in range(TT)]
                        slice_product(pe, s * DC, 0, outs, SL)
                    pe.wait_ge(S["q_out"], 4)
                    for i in range(8):
                        for k in range(4):
                            blk, tt = 2 * i + k // 2, k % 2
                            ins = nc.tensor.transpose(bank(i)[:, k * P:(k + 1) * P],
                                                      q_peer[:, tt, blk * NK:(blk + 1) * NK], ident)
                        ins.then_inc(S["qt_full"], 1)
                    pe.wait_ge(S["keys_in"], 16)
                    pe.wait_ge(S["qt_read"], 1)
                    for s in range(2):
                        ins = nc.tensor.transpose(bank(0)[:, s * NK:(s + 1) * NK],
                                                  keys_rows[:, 0, s], ident)
                    ins.then_inc(S["qt_full"], 1)
                    pe.wait_ge(S["qt_read"], 9)
                    for i in range(8):
                        tt = i // 4
                        for k in range(4):
                            blk = 4 * (i % 4) + k
                            ins = nc.tensor.matmul(bank(i)[:, k * NK:(k + 1) * NK],
                                                   q_peer_t[:, blk, tt * P:(tt + 1) * P],
                                                   keys_t[:, (blk % 2) * NK:(blk % 2 + 1) * NK],
                                                   start=True, stop=True)
                        ins.then_inc(S["score_full"], 1)

                    def turn_gelu(g, par):
                        pe.wait_ge(S["gelu_done"], g_count(g) + 2 + 1)
                        pe.wait_ge(S["w_stored"], g_count(g) + 1)
                        for jj in range(GJ):
                            for tt in range(TT):
                                ins = nc.tensor.transpose(bank(6, 2)[:, jj * T + tt * P:jj * T + (tt + 1) * P],
                                                          ga[:, par, tt, jj * P:(jj + 1) * P], ident)
                        ins.then_inc(S["gelu_turned"], 1)

                    def step(half, i, k, tails):
                        g = (half, i * 2 + k // DC)
                        par = k // DC
                        if k % VL:
                            pe.wait_ge(S["pool_lo_ready"],
                                       pool_count(half, i * 2 + k // DC, k % DC))
                        if k % DC == 0:
                            pe.wait_ge(S["gelu_done"], g_count(g) + 1)
                        unit_product(pe, U_A + half * U_HALF + i * (2 * DC) + k, k, ht_hi[:, k % DC],
                                     ht_lo[:, k % DC], [bank(2 * par + tt) for tt in range(TT)], SL,
                                     k % DC == 0, k % DC == DC - 1)
                        if tails and k % DC == 4:
                            turn_gelu((half, g[1] - 1), (par + 1) % 2)

                    def gates_step(half, i, b):
                        n = half * BATCHES + i * 2 + b
                        pe.wait_ge(S["onehot_rows"], n + 1)
                        pe.wait_ge(S["gates_copied" if b else "even_gated"], half * (BATCHES // 2) + i + 1)
                        for t in range(BT):
                            for c in range(3):
                                ins = nc.tensor.matmul(bank(2 * b, 2)[:, t * HALF_J:(t + 1) * HALF_J],
                                                       hot2[:, b, :, t], hotg[:, b, c, :, t],
                                                       start=(c == 0), stop=(c == 2))
                        ins.then_inc(S["gates_made"], 1)

                    def v_steps(half, g, first, last):
                        for b in range(4):
                            j = g * 4 + b
                            pe.wait_ge(S["wj_lo_ready"], half * HALF_J + j + 1)
                            for k in range(4):
                                outs = [bank(4 * tt + k) for tt in range(TT)]
                                unit_product(pe, U_A + half * U_HALF + U_AHALF + j * 4 + k, k, wj_hi[:, b % 2],
                                             wj_lo[:, b % 2], outs, SL, first and b == 0, last and b == 3)

                    for half in range(2):
                        pe.wait_ge(S["psum_clear"], half + 1)
                        for k in range(SHIFT):
                            step(half, 0, k, False)
                        pe.wait_ge(S["psum_clear"], 3 * half + 1)
                        with pe.Fori(0, PAIRS - 1) as i:
                            for k in range(SHIFT, 2 * DC + SHIFT):
                                step(half, i + k // (2 * DC), k % (2 * DC), True)
                        for k in range(SHIFT, 2 * DC):
                            step(half, PAIRS - 1, k, True)
                        if half == 0:
                            pe.wait_ge(S["rows_ready"], 4 + 1)
                            for i, rows in enumerate((key_rows[0], key_rows[1], gates)):
                                for tt in range(TT):
                                    ins = nc.tensor.transpose(bank(4, 2)[:, i * T + tt * P:i * T + (tt + 1) * P],
                                                              rows[:, tt * HK:(tt + 1) * HK], ident)
                            ins.then_inc(S["small_full"], 1)
                        turn_gelu((half, GROUPS - 1), 1)
                        with pe.Fori(0, BATCHES // 2) as i:
                            pe.wait_ge(S["w_stored"], (half + 1) * GROUPS + 1)
                            for b in range(2):
                                gates_step(half, i, b)
                        pe.wait_ge(S["even_gated"], (half + 1) * (BATCHES // 2) + 1)
                        pe.wait_ge(S["odd_gated"], (half + 1) * (BATCHES // 2) + 1)
                        v_steps(half, 0, True, False)
                        with pe.Fori(1, GROUPS - 1) as g:
                            v_steps(half, g, False, False)
                        v_steps(half, GROUPS - 1, False, True)

            nc.all_engine_barrier(sems_to_clear=cleared)

        with nc.Block() as block:
            gain = arena[:, 0:D]
            rows = arena[:, YN:YN + TT * D].rearrange("p (a d) -> p a d", a=TT)

            @block.sync
            def _(sp):
                sp.dma_start(gain, final_norm.rearrange("(o d) -> o d", o=1).to_broadcast([P, D])
                             ).then_inc(S["keys_in"], 16)
                o = out.rearrange("(a p) d -> p a d", p=P)
                for tt in range(TT):
                    sp.wait_ge(S["ranked"], tt + 1)
                    sp.dma_start(o[:, tt], rows[:, tt]).then_inc(S["stored"], 16)
                sp.wait_ge(S["stored"], 16 * TT)

            @block.scalar
            def _(act):
                roots(act, 1, 2)

            @block.vector
            def _(dve):
                chain = chainer(dve, S["chain_v"])
                means(dve, 0, [(0, 2, D)])
                dve.wait_ge(S["root_ready"], 1)
                dve.wait_ge(S["keys_in"], 16)
                chain(nc.vector.reciprocal(rstd[:, 0:2], ssq[:, 0:2]))
                for tt in range(TT):
                    nc.vector.scalar_tensor_tensor(rows[:, tt], x[:, tt], rstd[:, tt:tt + 1], gain,
                                                   ALU.mult, ALU.mult).then_inc(S["ranked"], 1)


def kernel(**inputs):
    import numpy as np
    import concourse.bacc as bacc
    from concourse.bass_utils import run_bass_kernel_spmd

    inv = (np.float32(10000.0) ** (-np.arange(0, ROPE, 2, dtype=np.float32) / np.float32(ROPE))).astype(np.float32)
    ang = np.arange(T, dtype=np.float32)[:, None] * inv[None, :]
    tables = [np.ascontiguousarray(f(ang).astype(np.float32).reshape(TT, P, ROPE // 2).transpose(1, 0, 2)).reshape(
        P, -1) for f in (np.cos, np.sin)]
    c = np.arange(P) % GRID_W
    c0 = np.clip(c - WIN_C // 2, 0, GRID_W - WIN_C)[:, None]
    kc = np.arange(GRID_W)[None, :]
    outside = np.where((kc >= c0) & (kc < c0 + WIN_C), 0.0, -1.0e30).astype(np.float32)
    consts = np.concatenate([np.eye(P, dtype=np.float32), *tables, outside,
                             np.broadcast_to(np.arange(TOPK, dtype=np.float32), (P, TOPK))], axis=1)

    order = ["x", "attn_norm", "ffn_norm", "mla_q_norm", "mla_kv_norm", "mla_out_norm", "nat_out_norm", "w_in",
             "mla_w_uq", "mla_w_ukv", "nat_rpb", "w_out", "peer_w_q", "peer_sub_keys", "peer_u", "peer_v",
             "final_norm"]
    nc = bacc.Bacc("TRN2", target_bir_lowering=False, num_devices=1)
    arrays, ap = {}, {}
    for name in order:
        a = np.ascontiguousarray(inputs[name])
        if name == "x":
            a = a.reshape(T, D)
        arrays["in_" + name] = a
        ap[name] = nc.dram_tensor("in_" + name, a.shape, mybir.dt.from_np(a.dtype), kind="ExternalInput").ap()
    arrays["in_consts"] = np.ascontiguousarray(consts)
    consts_ap = nc.dram_tensor("in_consts", consts.shape, F32, kind="ExternalInput").ap()
    out = nc.dram_tensor("out_0", (T, D), F32, kind="ExternalOutput").ap()
    gains = dict(attn=ap["attn_norm"], ffn=ap["ffn_norm"], q=ap["mla_q_norm"], kv=ap["mla_kv_norm"],
                 mla=ap["mla_out_norm"], nat=ap["nat_out_norm"])
    build(nc, ap["x"], gains, ap["w_in"], ap["mla_w_uq"], ap["mla_w_ukv"], ap["nat_rpb"], ap["w_out"],
          ap["peer_w_q"], ap["peer_sub_keys"], ap["peer_u"], ap["peer_v"], ap["final_norm"], consts_ap, out)
    r = run_bass_kernel_spmd(nc, [arrays], core_ids=[0])
    return r.results[0]["out_0"].reshape(1, T, D)
```
